# Optimizing a Trainium2 kernel written in Bass

```python
import jax, jax.numpy as jnp
from jax import lax
import numpy as np

D_MODEL = 1024
BATCH = 1
SEQ = 256
DEPTH = 2

N_MIXERS = 2
N_A = (DEPTH + 1) // 2
N_B = DEPTH // 2
EPS = 1e-6

MLA_HEADS = 16
MLA_Q_LORA = 384
MLA_KV_LORA = 256
MLA_NOPE = 64
MLA_ROPE = 32
MLA_V = 64
MLA_IN = MLA_Q_LORA + MLA_KV_LORA + MLA_ROPE
ROPE_THETA = 10000.0
Q_BLOCK = 128

HG_HEADS = 8
HG_DK = 128
HG_DV = D_MODEL // HG_HEADS
HG_WIDTH = HG_HEADS * HG_DK
HG_VWIDTH = HG_HEADS * HG_DV
HG_IN = 2 * HG_WIDTH + 2 * HG_VWIDTH
HG_CHUNK = 64

D_FF = 3584
N_EXPERTS = 8
TOP_K = 2
D_FF_EXPERT = 3584

kernel_name = 'hybrid_mla_hgrn2_moe'

def rms_norm(x, g):
    xf = x.astype(jnp.float32)
    y = xf * lax.rsqrt(jnp.mean(xf * xf, axis=-1, keepdims=True) + EPS)
    return (y * g.astype(jnp.float32)).astype(x.dtype)

def rope_tables(positions):
    inv_freq = ROPE_THETA ** (-jnp.arange(0, MLA_ROPE, 2, dtype=jnp.float32) / MLA_ROPE)
    ang = positions.astype(jnp.float32)[..., None] * inv_freq
    return jnp.cos(ang), jnp.sin(ang)

def apply_rope(x, cos, sin):
    xf = x.astype(jnp.float32)
    half = MLA_ROPE // 2
    x1, x2 = xf[..., :half], xf[..., half:]
    return jnp.concatenate([x1 * cos - x2 * sin, x2 * cos + x1 * sin], axis=-1).astype(x.dtype)

def causal_latent_attention(qn, qr, kn, kr, v):
    B, S, H, _ = qn.shape
    nb = S // Q_BLOCK
    scale = (MLA_NOPE + MLA_ROPE) ** -0.5
    qn_b = qn.reshape(B, nb, Q_BLOCK, H, MLA_NOPE).transpose(1, 0, 2, 3, 4)
    qr_b = qr.reshape(B, nb, Q_BLOCK, H, MLA_ROPE).transpose(1, 0, 2, 3, 4)
    key_idx = jnp.arange(S)

    def block(args):
        qn_i, qr_i, blk = args
        s = (jnp.einsum('bqhd,bkhd->bhqk', qn_i, kn)
             + jnp.einsum('bqhr,bkr->bhqk', qr_i, kr)).astype(jnp.float32) * scale
        q_idx = blk * Q_BLOCK + jnp.arange(Q_BLOCK)
        mask = key_idx[None, :] <= q_idx[:, None]
        s = jnp.where(mask, s, -jnp.inf)
        p = jax.nn.softmax(s, axis=-1).astype(v.dtype)
        return jnp.einsum('bhqk,bkhd->bqhd', p, v)

    out = lax.map(block, (qn_b, qr_b, jnp.arange(nb)))
    return out.transpose(1, 0, 2, 3, 4).reshape(B, S, H * MLA_V)

def mla_mixer(hn, cos, sin, w_in, q_norm_g, w_q_up, kv_norm_g, w_kv_up, w_o):
    B, S, _ = hn.shape
    proj = hn @ w_in
    c_q = proj[..., :MLA_Q_LORA]
    c_kv = proj[..., MLA_Q_LORA:MLA_Q_LORA + MLA_KV_LORA]
    k_r = proj[..., MLA_Q_LORA + MLA_KV_LORA:]
    q = (rms_norm(c_q, q_norm_g) @ w_q_up).reshape(B, S, MLA_HEADS, MLA_NOPE + MLA_ROPE)
    qn, qr = q[..., :MLA_NOPE], q[..., MLA_NOPE:]
    qr = apply_rope(qr, cos[:, :, None, :], sin[:, :, None, :])
    kr = apply_rope(k_r, cos, sin)
    kv = (rms_norm(c_kv, kv_norm_g) @ w_kv_up).reshape(B, S, MLA_HEADS, MLA_NOPE + MLA_V)
    kn, v = kv[..., :MLA_NOPE], kv[..., MLA_NOPE:]
    o = causal_latent_attention(qn, qr, kn, kr, v)
    return o @ w_o

def hgrn2_chunked(q, k, v, log_f):
    B, S, H, dk = q.shape
    dv = v.shape[-1]
    C = HG_CHUNK
    N = S // C
    to_chunks = lambda a: a.reshape(B, N, C, H, a.shape[-1]).transpose(0, 3, 1, 2, 4)
    q, k, v, log_f = to_chunks(q), to_chunks(k), to_chunks(v), to_chunks(log_f)
    b = jnp.cumsum(log_f, axis=3)
    b_last = b[:, :, :, -1:, :]
    qd = q * jnp.exp(b)
    kd = k * jnp.exp(-b)
    A = jnp.einsum('bhnck,bhnsk->bhncs', qd, kd)
    tril = jnp.tril(jnp.ones((C, C), dtype=bool))
    A = jnp.where(tril, A, 0.0)
    o_intra = jnp.einsum('bhncs,bhnsv->bhncv', A, v)
    kv = jnp.einsum('bhnsk,bhnsv->bhnkv', k * jnp.exp(b_last - b), v)
    decay = jnp.exp(b_last[:, :, :, 0, :])

    def step(state, inp):
        d, kv_n = inp
        return d[..., None] * state + kv_n, state

    _, s_prev = lax.scan(step, jnp.zeros((B, H, dk, dv), jnp.float32),
                         (jnp.moveaxis(decay, 2, 0), jnp.moveaxis(kv, 2, 0)))
    s_prev = jnp.moveaxis(s_prev, 0, 2)
    o = o_intra + jnp.einsum('bhnck,bhnkv->bhncv', qd, s_prev)
    return o.transpose(0, 2, 3, 1, 4).reshape(B, S, H, dv)

def hgrn2_mixer(hn, lb, w_in, out_norm_g, w_o):
    B, S, _ = hn.shape
    proj = hn @ w_in
    q = proj[..., :HG_WIDTH]
    f_pre = proj[..., HG_WIDTH:2 * HG_WIDTH]
    i_in = proj[..., 2 * HG_WIDTH:2 * HG_WIDTH + HG_VWIDTH]
    g = proj[..., 2 * HG_WIDTH + HG_VWIDTH:]
    heads_k = lambda a: a.astype(jnp.float32).reshape(B, S, HG_HEADS, HG_DK)
    heads_v = lambda a: a.astype(jnp.float32).reshape(B, S, HG_HEADS, HG_DV)
    lb = lb.astype(jnp.float32).reshape(HG_HEADS, HG_DK)
    f = lb + (1.0 - lb) * jax.nn.sigmoid(heads_k(f_pre))
    log_f = jnp.log(f)
    k = 1.0 - f
    o = hgrn2_chunked(heads_k(q) * HG_DK ** -0.5, k, heads_v(i_in), log_f)
    o = rms_norm(o, out_norm_g) * jax.nn.silu(heads_v(g))
    return o.reshape(B, S, HG_VWIDTH).astype(hn.dtype) @ w_o

def swiglu(t, w_gate, w_up, w_down):
    return (jax.nn.silu(t @ w_gate) * (t @ w_up)) @ w_down

def moe_ffn(hn, router, w_gate, w_up, w_down):
    B, S, D = hn.shape
    t = hn.reshape(B * S, D)
    logits = (t @ router).astype(jnp.float32)
    vals, idx = lax.top_k(logits, TOP_K)
    w = jax.nn.softmax(vals, axis=-1)
    gate = jnp.sum(jax.nn.one_hot(idx, N_EXPERTS, dtype=jnp.float32) * w[..., None], axis=1)
    gate = gate.astype(t.dtype)
    y = jnp.zeros_like(t)
    for e in range(N_EXPERTS):
        y = y + gate[:, e:e + 1] * swiglu(t, w_gate[e], w_up[e], w_down[e])
    return y.reshape(B, S, D)

def _w(key, shape, fan_in):
    return jax.random.normal(key, shape, jnp.float32) * (fan_in ** -0.5)

def _gain(key, shape):
    return 1.0 + 0.02 * jax.random.normal(key, shape, jnp.float32)

def setup_inputs(seed: int = 0) -> dict:
    key = jax.random.key(seed)
    ks = jax.random.split(key, 26)
    x = jax.random.normal(ks[0], (BATCH, SEQ, D_MODEL), jnp.float32)
    offset = jax.random.randint(ks[1], (BATCH, 1), 0, 1024, dtype=jnp.int32)
    positions = jnp.arange(SEQ, dtype=jnp.int32)[None, :] + offset
    return {
        'x': x,
        'positions': positions,
        'mix_norm': _gain(ks[2], (DEPTH, D_MODEL)),
        'ffn_norm': _gain(ks[3], (DEPTH, D_MODEL)),
        'final_norm': _gain(ks[4], (D_MODEL,)),
        'mla_w_in': _w(ks[5], (N_A, D_MODEL, MLA_IN), D_MODEL),
        'mla_q_norm': _gain(ks[6], (N_A, MLA_Q_LORA)),
        'mla_w_q_up': _w(ks[7], (N_A, MLA_Q_LORA, MLA_HEADS * (MLA_NOPE + MLA_ROPE)), MLA_Q_LORA),
        'mla_kv_norm': _gain(ks[8], (N_A, MLA_KV_LORA)),
        'mla_w_kv_up': _w(ks[9], (N_A, MLA_KV_LORA, MLA_HEADS * (MLA_NOPE + MLA_V)), MLA_KV_LORA),
        'mla_w_o': _w(ks[10], (N_A, MLA_HEADS * MLA_V, D_MODEL), MLA_HEADS * MLA_V),
        'hgrn_w_in': _w(ks[11], (N_B, D_MODEL, HG_IN), D_MODEL),
        'hgrn_lower_bounds': 0.5 * jax.random.normal(ks[12], (DEPTH, HG_WIDTH), jnp.float32),
        'hgrn_out_norm': _gain(ks[13], (N_B, HG_DV)),
        'hgrn_w_o': _w(ks[14], (N_B, HG_VWIDTH, D_MODEL), HG_VWIDTH),
        'ffn_w_gate': _w(ks[15], (N_A, D_MODEL, D_FF), D_MODEL),
        'ffn_w_up': _w(ks[16], (N_A, D_MODEL, D_FF), D_MODEL),
        'ffn_w_down': _w(ks[17], (N_A, D_FF, D_MODEL), D_FF),
        'moe_router': _w(ks[18], (N_B, D_MODEL, N_EXPERTS), D_MODEL),
        'moe_w_gate': _w(ks[19], (N_B, N_EXPERTS, D_MODEL, D_FF_EXPERT), D_MODEL),
        'moe_w_up': _w(ks[20], (N_B, N_EXPERTS, D_MODEL, D_FF_EXPERT), D_MODEL),
        'moe_w_down': _w(ks[21], (N_B, N_EXPERTS, D_FF_EXPERT, D_MODEL), D_FF_EXPERT),
    }

def reference(x, positions, mix_norm, ffn_norm, final_norm,
              mla_w_in, mla_q_norm, mla_w_q_up, mla_kv_norm, mla_w_kv_up, mla_w_o,
              hgrn_w_in, hgrn_lower_bounds, hgrn_out_norm, hgrn_w_o,
              ffn_w_gate, ffn_w_up, ffn_w_down,
              moe_router, moe_w_gate, moe_w_up, moe_w_down):
    cos, sin = rope_tables(positions)
    lb_all = jnp.cumsum(jax.nn.softmax(hgrn_lower_bounds.astype(jnp.float32), axis=0), axis=0)
    lb_all = lb_all - lb_all[0:1]
    h = x
    for i in range(DEPTH):
        j = i // N_MIXERS
        hn = rms_norm(h, mix_norm[i])
        if i % N_MIXERS == 0:
            h = h + mla_mixer(hn, cos, sin, mla_w_in[j], mla_q_norm[j], mla_w_q_up[j],
                              mla_kv_norm[j], mla_w_kv_up[j], mla_w_o[j])
        else:
            h = h + hgrn2_mixer(hn, lb_all[i], hgrn_w_in[j], hgrn_out_norm[j], hgrn_w_o[j])
        hn = rms_norm(h, ffn_norm[i])
        if i % 2 == 0:
            h = h + swiglu(hn, ffn_w_gate[j], ffn_w_up[j], ffn_w_down[j])
        else:
            h = h + moe_ffn(hn, moe_router[j], moe_w_gate[j], moe_w_up[j], moe_w_down[j])
    return rms_norm(h, final_norm)


_drawn_inputs = setup_inputs


def setup_inputs(seed=0):
    import zlib

    import numpy as np

    out = dict(_drawn_inputs(seed))
    spreads = {}
    factors = {}
    for name, (base, spread) in spreads.items():
        noise = np.random.default_rng([zlib.crc32(name.encode()), seed]).standard_normal(out[name].shape)
        drawn = base * np.exp(spread * noise) if base else spread * noise
        out[name] = __import__('jax').numpy.asarray(drawn.astype(out[name].dtype))
    for name, factor in factors.items():
        out[name] = (out[name] * factor).astype(out[name].dtype)
    return out
```

```python
from contextlib import ExitStack

import numpy as np
import concourse.bass as bass
from concourse import mybir

F32 = mybir.dt.float32
F32R = mybir.dt.float32r
I32 = mybir.dt.int32
U32 = mybir.dt.uint32
ALU = mybir.AluOpType
ACT = mybir.ActivationFunctionType
AX = mybir.AxisListType

P = 128
D = 1024
SEQ = 256
TT = SEQ // P
KD = D // P
HALF = 512
EPS = 1e-6
HEADS, NOPE, ROPE, VD = 16, 64, 32, 64
QL, KVL = 384, 256
MLA_IN = QL + KVL + ROPE
QD = NOPE + ROPE
ROPE_THETA = 10000.0
HG, DK, CH = 8, 128, 64
NCH = SEQ // CH
FF = 3584
FB = FF // HALF
E = 8
RAW, SPLIT, CW = 6, 3, 2048
AHEAD = 2
NEG = -1e30

N_IN, N_QUP, N_KVUP, N_O = 3, 3, 2, 4
C_IN = 0
C_QUP = C_IN + N_IN
C_KVUP = C_QUP + N_QUP
C_O = C_KVUP + N_KVUP
C_FFN = C_O + N_O
C_DOWN = C_FFN + 4 * FB
C_HG = C_DOWN + 2 * FB
C_HGO = C_HG + 16
C_MOE = C_HGO + 4
PER_ITEM = 6 * FB
MAX_EXTRA = 3
MAX_ITEMS = E + MAX_EXTRA


def dense_chunks(w):
    def rows(m, k0, k1, n0=0, n1=None):
        v = m[k0 * P:k1 * P, :].rearrange("(k p) n -> p k n", p=P)
        return v[:, :, n0:(n1 if n1 is not None else m.shape[1])]
    out = [rows(w["mla_w_in"][0], 0, 3), rows(w["mla_w_in"][0], 3, 6), rows(w["mla_w_in"][0], 6, 8)]
    out += [rows(w["mla_w_q_up"][0], k, k + 1) for k in range(3)]
    out += [rows(w["mla_w_kv_up"][0], k, k + 1) for k in range(2)]
    out += [rows(w["mla_w_o"][0], 2 * k, 2 * k + 2) for k in range(4)]
    for b in range(FB):
        for m in ("ffn_w_gate", "ffn_w_up"):
            out += [rows(w[m][0], 4 * q, 4 * q + 4, b * HALF, (b + 1) * HALF) for q in range(2)]
    out += [rows(w["ffn_w_down"][0], 2 * k, 2 * k + 2) for k in range(2 * FB)]
    for b in (2, 3, 0, 1, 4, 5, 6, 7):
        out += [rows(w["hgrn_w_in"][0], 4 * q, 4 * q + 4, b * HALF, (b + 1) * HALF) for q in range(2)]
    out += [rows(w["hgrn_w_o"][0], 2 * k, 2 * k + 2) for k in range(4)]
    assert len(out) == C_MOE
    return out


def item_chunks():
    out = []
    for b in range(FB):
        out += [("gate", b, 0), ("gate", b, 1), ("up", b, 0), ("up", b, 1)]
        if b:
            out += [("down", b - 1, 0), ("down", b - 1, 1)]
    out += [("down", FB - 1, 0), ("down", FB - 1, 1)]
    assert len(out) == PER_ITEM
    return out


def at_most(x, low=0):
    return x if x > low else low


def trunk(nc, w, out):
    ctx = ExitStack()

    def sb(name, shape, dt=F32, where=None):
        return (where or ctx).enter_context(nc.sbuf_tensor(name, shape, dt))

    def sem(name):
        return ctx.enter_context(nc.semaphore(name))

    with ctx:
        w_raw = sb("w_raw", [P, RAW, CW])
        w_hi = sb("w_hi", [P, SPLIT, CW], F32R)
        w_lo = sb("w_lo", [P, SPLIT, CW], F32R)
        h = sb("h", [P, TT, D])
        hn = sb("hn", [P, TT, D])
        hnT_hi = sb("hnT_hi", [P, KD, SEQ], F32R)
        hnT_lo = sb("hnT_lo", [P, KD, SEQ], F32R)
        gain = sb("gain", [P, 2, D])
        ident = sb("ident", [P, P])
        ss = sb("ss", [P, 2 * TT])
        rms = sb("rms", [P, 2 * TT])
        rstd = sb("rstd", [P, 2 * TT])
        bank = [ctx.enter_context(nc.psum_tensor(f"bank{i}", [P, HALF], F32)) for i in range(8)]

        raw_loaded = [sem(f"raw_loaded{i}") for i in range(RAW)]
        hi_ready, lo_ready, chunk_used = sem("hi_ready"), sem("lo_ready"), sem("chunk_used")
        x_loaded = sem("x_loaded")
        gain_loaded = [sem("gain_loaded0"), sem("gain_loaded1")]
        sq_done = sem("sq_done")
        ms_ready = sem("ms_ready")
        rms_ready = sem("rms_ready")
        hn_ready = sem("hn_ready")
        nT_done = sem("nT_done")
        nT_hi_ready = sem("nT_hi_ready")
        nT_lo_ready = sem("nT_lo_ready")
        h_added = sem("h_added")
        const_ready = sem("const_ready")
        pe_out = sem("pe_out")
        dve_step = sem("dve_step")
        act_step = sem("act_step")
        pool_step = sem("pool_step")
        steps = {"dve": 0, "act": 0, "pool": 0}

        def dve_link(ins):
            steps["dve"] += 1
            ins.then_inc(dve_step, 1)
            nc.vector.wait_ge(dve_step, steps["dve"])

        def act_link(ins):
            steps["act"] += 1
            ins.then_inc(act_step, 1)
            nc.scalar.wait_ge(act_step, steps["act"])

        def pool_link(ins):
            steps["pool"] += 1
            ins.then_inc(pool_step, 1)
            nc.gpsimd.wait_ge(pool_step, steps["pool"])

        chunks = dense_chunks(w)
        item = item_chunks()
        C_END = C_MOE + AHEAD + 1

        def load_chunk(c, dram=None):
            src = chunks[c] if dram is None else dram
            if c >= RAW:
                nc.sync.wait_ge(lo_ready, c - RAW + 1)
            k, n = src.shape[1], src.shape[2]
            dst = w_raw[:, c % RAW, 0:k * n].rearrange("p (k n) -> p k n", k=k)
            nc.sync.dma_start(dst, src).then_inc(raw_loaded[c % RAW], 16)

        def width(c):
            return chunks[c].shape[1] * chunks[c].shape[2] if c < C_MOE else CW

        def split_hi(c, base=0, turn=0):
            n = width(c)
            nc.scalar.wait_ge(raw_loaded[c % RAW], turn + 16 * (c // RAW + 1))
            if c >= SPLIT:
                nc.scalar.wait_ge(chunk_used, base + (c - SPLIT + 1))
            nc.scalar.activation(w_hi[:, c % SPLIT, 0:n], w_raw[:, c % RAW, 0:n],
                                 ACT.Copy).then_inc(hi_ready, 1)

        def split_lo(c, base=0):
            n = width(c)
            nc.vector.wait_ge(hi_ready, base + (c + 1))
            nc.vector.tensor_tensor(w_lo[:, c % SPLIT, 0:n], w_raw[:, c % RAW, 0:n],
                                    w_hi[:, c % SPLIT, 0:n].bitcast(F32),
                                    ALU.subtract).then_inc(lo_ready, 1)

        def chunk_here(c, base=0):
            nc.tensor.wait_ge(lo_ready, base + (c + 1))

        def weights(c, k, n0, n1, n):
            return w_hi[:, c % SPLIT, k * n + n0:k * n + n1], w_lo[:, c % SPLIT, k * n + n0:k * n + n1]

        def mm3(o, a, b, start, stop):
            nc.tensor.matmul(o, a[0], b[0], start=start, stop=False)
            nc.tensor.matmul(o, a[0], b[1], start=False, stop=False)
            return nc.tensor.matmul(o, a[1], b[0], start=False, stop=stop)

        def tok(a, k, t):
            return a[0][:, k, t * P:(t + 1) * P], a[1][:, k, t * P:(t + 1) * P]

        hnT = (hnT_hi, hnT_lo)

        def item_dram(k, e):
            kind, b, q = item[k]
            m = w["moe_w_" + kind]
            m = m[0, bass.ds(e, 1)].rearrange("e a n -> (e a) n")
            if kind == "down":
                r = (4 * b + 2 * q) * P
                return m[r:r + 2 * P, :].rearrange("(k p) n -> p k n", p=P)
            return m[4 * q * P:(4 * q + 4) * P, b * HALF:(b + 1) * HALF].rearrange("(k p) n -> p k n", p=P)

        def rng(lo, hi):
            return range(lo, hi)

        def norm_act(k):
            for t in range(TT):
                if k == 0:
                    nc.scalar.wait_ge(x_loaded, 16)
                nc.scalar.activation(hn[:, t, :], h[:, t, :], ACT.Square,
                                     accum_out=ss[:, t:t + 1]).then_inc(sq_done, 1)
            nc.scalar.wait_ge(ms_ready, k + 1)
            nc.scalar.activation(rms[:, 0:TT], ss[:, 0:TT], ACT.Sqrt).then_inc(rms_ready, 1)

        def norm_dve(k):
            nc.vector.wait_ge(sq_done, TT * (k + 1))
            nc.vector.tensor_scalar(ss[:, 0:TT], ss[:, 0:TT], 1.0 / D, EPS, ALU.mult,
                                    ALU.add).then_inc(ms_ready, 1)
            nc.vector.wait_ge(rms_ready, k + 1)
            dve_link(nc.vector.reciprocal(rstd[:, 0:TT], rms[:, 0:TT]))
            nc.vector.wait_ge(gain_loaded[k % 2], 16 * (k // 2 + 1))
            for t in range(TT):
                nc.vector.scalar_tensor_tensor(hn[:, t, :], h[:, t, :], rstd[:, t:t + 1],
                                               gain[:, k % 2, :], ALU.mult, ALU.mult).then_inc(hn_ready, 1)

        def transpose_pe(src, ready, ready_at, done):
            for t in range(TT):
                nc.tensor.wait_ge(ready, ready_at(t))
                for g in range(2):
                    for j in range(4):
                        col = (4 * g + j) * P
                        last = nc.tensor.transpose(bank[2 * t + g][:, j * P:(j + 1) * P],
                                                   src[:, t, col:col + P], ident[:])
                    last.then_inc(done, 1)

        def bank4(b):
            return bank[b][:, :].rearrange("p (j s) -> p j s", j=4)

        def transpose_act(done, base, hi_sem):
            for t in range(TT):
                for g in range(2):
                    nc.scalar.wait_ge(done, base + 2 * t + g + 1)
                    nc.scalar.activation(hnT_hi[:, 4 * g:4 * g + 4, t * P:(t + 1) * P], bank4(2 * t + g),
                                         ACT.Copy).then_inc(hi_sem, 1)

        def transpose_dve(base, hi_sem, lo_sem):
            for t in range(TT):
                for g in range(2):
                    nc.vector.wait_ge(hi_sem, base + 2 * t + g + 1)
                    dst = hnT_lo[:, 4 * g:4 * g + 4, t * P:(t + 1) * P]
                    nc.vector.tensor_tensor(dst, bank4(2 * t + g),
                                            hnT_hi[:, 4 * g:4 * g + 4, t * P:(t + 1) * P].bitcast(F32),
                                            ALU.subtract).then_inc(lo_sem, 1)

        def out_proj_pe(c0, n_chunks, src, b0=4, between=(), before=None):
            for q in range(n_chunks):
                chunk_here(c0 + q)
                if before:
                    before(q)
                for k in range(2):
                    for t in range(TT):
                        for n in range(2):
                            kt = 2 * q + k
                            last = mm3(bank[b0 + 2 * t + n][:, :], tok(src, kt, t),
                                       weights(c0 + q, k, n * HALF, (n + 1) * HALF, D),
                                       kt == 0, kt == 2 * n_chunks - 1)
                last.then_inc(chunk_used, 1)
                if q in between:
                    between[q]()

        def residual_dve(c_last, b0=4):
            nc.vector.wait_ge(chunk_used, c_last + 1)
            for t in range(TT):
                for n in range(2):
                    part = h[:, t, n * HALF:(n + 1) * HALF]
                    nc.vector.tensor_tensor(part, part, bank[b0 + 2 * t + n][:, :],
                                            ALU.add).then_inc(h_added, 1)

        def load_gain(k, name, row):
            src = w[name]
            src = src[row:row + 1, :] if row is not None else src.rearrange("(a n) -> a n", a=1)
            if k >= 2:
                nc.scalar.wait_ge(hn_ready, TT * (k - 1))
            nc.scalar.dma_start(gain[:, k % 2, :], src.broadcast_to([P, D])).then_inc(gain_loaded[k % 2], 16)

        ph = ExitStack()
        with ph:
            qg = sb("qg", [P, QL], where=ph)
            kvg = sb("kvg", [P, KVL], where=ph)
            pos_i = sb("pos_i", [P, TT], I32, where=ph)
            posf = sb("posf", [P, TT], where=ph)
            freq = sb("freq", [P, ROPE // 2], where=ph)
            ang = sb("ang", [P, TT, ROPE // 2], where=ph)
            turns = sb("turns", [P, TT, ROPE // 2], where=ph)
            absr = sb("absr", [P, TT, ROPE // 2], where=ph)
            cos = sb("cos", [P, TT, ROPE // 2], where=ph)
            sin = sb("sin", [P, TT, ROPE // 2], where=ph)
            halfpi = sb("halfpi", [P, 1], where=ph)
            mask = sb("mask", [P, 3 * P], where=ph)
            cqv = sb("cqv", [P, TT, MLA_IN], where=ph)
            krp = sb("krp", [P, TT, QD], where=ph)
            krT = sb("krT", [P, SEQ], where=ph)
            cT_hi = sb("cT_hi", [P, 5, SEQ], F32R, where=ph)
            cT_lo = sb("cT_lo", [P, 5, SEQ], F32R, where=ph)
            q_sb = sb("q_sb", [P, TT, HEADS * QD], where=ph)
            qT = sb("qT", [QD, HEADS, SEQ], where=ph)
            kT = sb("kT", [QD, HEADS, SEQ], where=ph)
            rt = sb("rt", [P, 4, HEADS * ROPE // 2], where=ph)
            nmax = sb("nmax", [P, 2, TT], where=ph)
            psum_ = sb("prob_sum", [P, 2, TT], where=ph)
            prcp = sb("prcp", [P, 2, TT], where=ph)
            v_sb = hn
            prob = q_sb[:, 0, 0:2 * 3 * P].rearrange("p (a n) -> p a n", a=2)
            probT = q_sb[:, 1, 0:2 * 3 * P].rearrange("p (a n) -> p a n", a=2)

            small_loaded = sem("small_loaded")
            rope_ready = sem("rope_ready")
            trig_ready = sem("trig_ready")
            red_ready = sem("red_ready")
            cqv_ready = sem("cqv_ready")
            cq_ms = sem("cq_ms")
            cq_rms = sem("cq_rms")
            cn_ready = sem("cn_ready")
            cT_done = sem("cT_done")
            cT_hi_ready = sem("cT_hi_ready")
            cT_lo_ready = sem("cT_lo_ready")
            krT_ready = sem("krT_ready")
            kr_spread = sem("kr_spread")
            q_copied = sem("q_copied")
            q_roped = sem("q_roped")
            kn_done = sem("kn_done")
            kn_copied = sem("kn_copied")
            v_done = sem("v_done")
            v_copied = sem("v_copied")
            qT_done = sem("qT_done")
            qT_copied = sem("qT_copied")
            score_done = sem("score_done")
            masked = sem("masked")
            max_ready = sem("max_ready")
            exp_done = sem("exp_done")
            prob_ready = sem("prob_ready")
            probT_done = sem("probT_done")
            probT_copied = sem("probT_copied")
            pv_done = sem("pv_done")
            oT_hi_ready = sem("oT_hi_ready")
            oT_lo_ready = sem("oT_lo_ready")

            with nc.Block() as block:
                @block.sync
                def _(sp):
                    nc.sync.dma_start(h[:, :, :], w["x"][0].rearrange("(t p) d -> p t d", p=P)
                                      ).then_inc(x_loaded, 16)
                    for c in range(0, C_FFN + RAW + AHEAD + 1):
                        load_chunk(c)

                @block.gpsimd
                def _(pool):
                    pool_link(nc.gpsimd.memset(ident[:], 0.0))
                    nc.gpsimd.affine_select(out=ident[:], in_=ident[:], compare_op=ALU.not_equal, fill=1.0,
                                            base=0, pattern=[[-1, P]], channel_multiplier=1
                                            ).then_inc(const_ready, 1)
                    inv = ROPE_THETA ** (-np.arange(0, ROPE, 2, dtype=np.float32) / np.float32(ROPE))
                    for j in range(ROPE // 2):
                        nc.gpsimd.memset(freq[:, j:j + 1], float(np.float32(inv[j])))
                    nc.gpsimd.memset(halfpi[:], float(np.pi / 2))
                    nc.gpsimd.memset(krp[:], 0.0).then_inc(const_ready, 1)
                    pool_link(nc.gpsimd.memset(mask[:], 0.0))
                    for b in (0, 2):
                        nc.gpsimd.affine_select(out=mask[:, b * P:(b + 1) * P], in_=mask[:, b * P:(b + 1) * P],
                                                compare_op=ALU.is_ge, fill=NEG, base=0, pattern=[[-1, P]],
                                                channel_multiplier=1).then_inc(const_ready, 1)
                    nc.gpsimd.wait_ge(const_ready, 4)
                    nc.gpsimd.wait_ge(krT_ready, 1)
                    nc.gpsimd.tensor_copy(kT[NOPE:QD, :, :],
                                          krT[NOPE:QD, :].unsqueeze(1).broadcast_to([ROPE, HEADS, SEQ])
                                          ).then_inc(kr_spread, 1)

                @block.scalar
                def _(act):
                    load_gain(0, "mix_norm", 0)
                    nc.scalar.dma_start(pos_i[:], w["positions"].rearrange("b (t p) -> p (b t)", p=P),
                                        allow_slow_non_contiguous=True).then_inc(small_loaded, 16)
                    nc.scalar.dma_start(qg[:], w["mla_q_norm"].broadcast_to([P, QL])).then_inc(small_loaded, 16)
                    nc.scalar.dma_start(kvg[:], w["mla_kv_norm"].broadcast_to([P, KVL])
                                        ).then_inc(small_loaded, 16)
                    load_gain(1, "ffn_norm", 0)
                    norm_act(0)
                    transpose_act(nT_done, 0, nT_hi_ready)
                    for c in rng(0, 3):
                        split_hi(c)
                    act.wait_ge(red_ready, 1)
                    nc.scalar.activation(sin[:], turns[:], ACT.Sin).then_inc(trig_ready, 1)
                    act_link(nc.scalar.activation(absr[:], turns[:], ACT.Abs))
                    act.wait_ge(const_ready, 2)
                    nc.scalar.activation(cos[:], absr[:], ACT.Sin, bias=halfpi[:], scale=-1.0
                                         ).then_inc(trig_ready, 1)
                    act.wait_ge(chunk_used, C_IN + N_IN)
                    for t in range(TT):
                        nc.scalar.activation(cqv[:, t, 0:QL], bank[4 + 2 * t][:, 0:QL], ACT.Copy
                                             ).then_inc(cqv_ready, 1)
                        nc.scalar.activation(cqv[:, t, QL:MLA_IN], bank[5 + 2 * t][:, 0:KVL + ROPE], ACT.Copy
                                             ).then_inc(cqv_ready, 1)
                        nc.scalar.activation(q_sb[:, t, 0:QL], bank[4 + 2 * t][:, 0:QL], ACT.Square,
                                             accum_out=ss[:, 2 * t:2 * t + 1]).then_inc(cqv_ready, 1)
                        nc.scalar.activation(q_sb[:, t, QL:QL + KVL], bank[5 + 2 * t][:, 0:KVL], ACT.Square,
                                             accum_out=ss[:, 2 * t + 1:2 * t + 2]).then_inc(cqv_ready, 1)
                    act.wait_ge(cq_ms, 1)
                    nc.scalar.activation(rms[:], ss[:], ACT.Sqrt).then_inc(cq_rms, 1)
                    for c in rng(3, 6):
                        split_hi(c)
                    for b in range(3):
                        act.wait_ge(cT_done, b + 1)
                        n = 2 if b < 2 else 1
                        nc.scalar.activation(cT_hi[:, 2 * b:2 * b + n, :],
                                             bank[b][:, 0:n * SEQ].rearrange("p (j s) -> p j s", j=n),
                                             ACT.Copy).then_inc(cT_hi_ready, 1)
                    act.wait_ge(cT_done, 4)
                    nc.scalar.activation(krT[NOPE:QD, :], bank[3][NOPE:QD, 0:SEQ], ACT.Copy
                                         ).then_inc(krT_ready, 1)
                    for c in rng(6, 8):
                        split_hi(c)
                    act.wait_ge(chunk_used, C_QUP + N_QUP)
                    for n in range(3):
                        for t in range(TT):
                            nc.scalar.activation(q_sb[:, t, n * HALF:(n + 1) * HALF], bank[2 * n + t][:, :],
                                                 ACT.Copy).then_inc(q_copied, 1)
                    for u in range(HEADS // 2):
                        act.wait_ge(kn_done, u + 1)
                        nc.scalar.activation(kT[0:NOPE, 2 * u:2 * u + 2, :],
                                             bank[6 + u % 2][0:NOPE, :].rearrange("p (a s) -> p a s", a=2),
                                             ACT.Copy).then_inc(kn_copied, 1)
                    split_hi(8)
                    for g in range(4):
                        if g < 3:
                            act.wait_ge(v_done, g + 1)
                        else:
                            act.wait_ge(chunk_used, C_KVUP + N_KVUP)
                        nc.scalar.activation(v_sb[:, g // 2, (g % 2) * HALF:(g % 2 + 1) * HALF], bank[g][:, :],
                                             ACT.Copy).then_inc(v_copied, 1)
                    for c in rng(9, 11):
                        split_hi(c)
                    for u in range(HEADS // 2):
                        act.wait_ge(qT_done, u + 1)
                        nc.scalar.activation(qT[:, 2 * u:2 * u + 2, :],
                                             bank[4 + u % 2][0:QD, :].rearrange("p (a s) -> p a s", a=2),
                                             ACT.Copy).then_inc(qT_copied, 1)

                    def evacuate_T(i):
                        act.wait_ge(probT_done, i + 1)
                        if i >= 2:
                            act.wait_ge(pv_done, i - 1)
                        nc.scalar.activation(probT[:, i % 2, :], bank[2 + i % 2][:, 0:3 * P], ACT.Copy
                                             ).then_inc(probT_copied, 1)
                        if i % 2 and i > 1:
                            evacuate_o(i // 2 - 1)

                    def evacuate_o(u):
                        act.wait_ge(pv_done, 2 * u + 2)
                        nc.scalar.activation(hnT_hi[:, u, :], bank[4 + u % 2][:, 0:SEQ], ACT.Copy
                                             ).then_inc(oT_hi_ready, 1)

                    for i in range(HEADS):
                        act.wait_ge(max_ready, i + 1)
                        for t in range(TT):
                            s = prob[:, i % 2, 0:P] if t == 0 else prob[:, i % 2, P:3 * P]
                            nc.scalar.activation(s, s, ACT.Exp, bias=nmax[:, i % 2, t:t + 1],
                                                 accum_out=psum_[:, i % 2, t:t + 1]).then_inc(exp_done, 1)
                        if i >= 1:
                            evacuate_T(i - 1)
                    evacuate_T(HEADS - 1)
                    evacuate_o(HEADS // 2 - 1)
                    for c in rng(11, C_FFN + AHEAD + 1):
                        split_hi(c)

                @block.vector
                def _(dve):
                    norm_dve(0)
                    transpose_dve(0, nT_hi_ready, nT_lo_ready)
                    dve.wait_ge(small_loaded, 48)
                    dve_link(nc.vector.tensor_copy(posf[:], pos_i[:]))
                    dve.wait_ge(const_ready, 2)
                    for t in range(TT):
                        last = nc.vector.tensor_scalar(ang[:, t, :], freq[:], posf[:, t:t + 1], None, ALU.mult)
                    dve_link(last)
                    magic = 1.5 * 2.0 ** 23
                    two_pi = 2 * np.pi
                    p1 = 6.28125
                    p2 = float(np.float32(np.round((two_pi - p1) * 2 ** 20) / 2 ** 20))
                    p3 = float(np.float32(two_pi - p1 - p2))
                    dve_link(nc.vector.tensor_scalar(absr[:], ang[:], float(1 / two_pi), magic, ALU.mult, ALU.add))
                    dve_link(nc.vector.tensor_scalar(absr[:], absr[:], -magic, None, ALU.add))
                    dve_link(nc.vector.scalar_tensor_tensor(turns[:], absr[:], -p1, ang[:], ALU.mult, ALU.add))
                    dve_link(nc.vector.scalar_tensor_tensor(ang[:], absr[:], -p2, turns[:], ALU.mult, ALU.add))
                    dve_link(nc.vector.scalar_tensor_tensor(turns[:], absr[:], -p3, ang[:], ALU.mult, ALU.add))
                    nc.vector.tensor_scalar(turns[:], turns[:], float(np.float32(np.pi)), -float(np.float32(np.pi)),
                                            ALU.min, ALU.max).then_inc(red_ready, 1)
                    for c in rng(0, 3):
                        split_lo(c)
                    dve.wait_ge(cqv_ready, 4 * TT)
                    sv = ss[:, :].rearrange("p (t a) -> p a t", a=2)
                    nc.vector.tensor_scalar(sv[:, 0, :], sv[:, 0, :], 1.0 / QL, EPS, ALU.mult, ALU.add)
                    nc.vector.tensor_scalar(sv[:, 1, :], sv[:, 1, :], 1.0 / KVL, EPS, ALU.mult, ALU.add
                                            ).then_inc(cq_ms, 1)
                    dve.wait_ge(trig_ready, 2)

                    def rotate(dst, src, t, n, first):
                        hf = ROPE // 2
                        c = cos[:, t, :].unsqueeze(1).broadcast_to([P, n, hf])
                        s = sin[:, t, :].unsqueeze(1).broadcast_to([P, n, hf])
                        x1, x2 = src[:, :, 0:hf], src[:, :, hf:ROPE]
                        tmp = [rt[:, j, 0:n * hf].rearrange("p (a b) -> p a b", a=n) for j in range(4)]
                        nc.vector.tensor_tensor(tmp[0], x1, c, ALU.mult)
                        nc.vector.tensor_tensor(tmp[1], x2, s, ALU.mult)
                        nc.vector.tensor_tensor(tmp[2], x2, c, ALU.mult)
                        dve_link(nc.vector.tensor_tensor(tmp[3], x1, s, ALU.mult))
                        nc.vector.tensor_tensor(dst[:, :, 0:hf], tmp[0], tmp[1], ALU.subtract)
                        return nc.vector.tensor_tensor(dst[:, :, hf:ROPE], tmp[2], tmp[3], ALU.add)

                    for t in range(TT):
                        dve_link(rotate(krp[:, t:t + 1, NOPE:QD], cqv[:, t:t + 1, QL + KVL:MLA_IN], t, 1, t == 0))
                    dve.wait_ge(cq_rms, 1)
                    dve_link(nc.vector.reciprocal(rstd[:], rms[:]))
                    for t in range(TT):
                        nc.vector.scalar_tensor_tensor(cqv[:, t, 0:QL], cqv[:, t, 0:QL], rstd[:, 2 * t:2 * t + 1],
                                                       qg[:], ALU.mult, ALU.mult).then_inc(cn_ready, 1)
                        nc.vector.scalar_tensor_tensor(cqv[:, t, QL:QL + KVL], cqv[:, t, QL:QL + KVL],
                                                       rstd[:, 2 * t + 1:2 * t + 2], kvg[:], ALU.mult, ALU.mult
                                                       ).then_inc(cn_ready, 1)
                    for c in rng(3, 6):
                        split_lo(c)
                    for b in range(3):
                        dve.wait_ge(cT_hi_ready, b + 1)
                        n = 2 if b < 2 else 1
                        nc.vector.tensor_tensor(cT_lo[:, 2 * b:2 * b + n, :],
                                                bank[b][:, 0:n * SEQ].rearrange("p (j s) -> p j s", j=n),
                                                cT_hi[:, 2 * b:2 * b + n, :].bitcast(F32), ALU.subtract
                                                ).then_inc(cT_lo_ready, 1)
                    for c in rng(6, 8):
                        split_lo(c)
                    dve.wait_ge(q_copied, 6)
                    for t in range(TT):
                        part = q_sb[:, t, :].rearrange("p (a b) -> p a b", a=HEADS)[:, :, NOPE:QD]
                        last = rotate(part, part, t, HEADS, False)
                        if t + 1 < TT:
                            dve_link(last)
                    last.then_inc(q_roped, 1)
                    for c in rng(8, 11):
                        split_lo(c)

                    def scores_dve(i):
                        dve.wait_ge(score_done, i + 1)
                        if i == 0:
                            dve.wait_ge(qT_done, HEADS // 2)
                            dve.wait_ge(const_ready, 4)
                        if i >= 2:
                            dve.wait_ge(probT_done, i - 1)
                        dve_link(nc.vector.scalar_tensor_tensor(prob[:, i % 2, :], bank[i % 2][:, 0:3 * P],
                                                                float(np.float32(QD ** -0.5)), mask[:],
                                                                ALU.mult, ALU.add))
                        nc.vector.tensor_reduce(nmax[:, i % 2, 0:1], prob[:, i % 2, 0:P], AX.X, ALU.max, negate=True)
                        nc.vector.tensor_reduce(nmax[:, i % 2, 1:2], prob[:, i % 2, P:3 * P], AX.X, ALU.max,
                                                negate=True).then_inc(max_ready, 1)

                    def probs_dve(i):
                        dve.wait_ge(exp_done, TT * (i + 1))
                        dve_link(nc.vector.reciprocal(prcp[:, i % 2, :], psum_[:, i % 2, :]))
                        for t in range(TT):
                            s = prob[:, i % 2, 0:P] if t == 0 else prob[:, i % 2, P:3 * P]
                            last = nc.vector.tensor_scalar(s, s, prcp[:, i % 2, t:t + 1], None, ALU.mult)
                        last.then_inc(prob_ready, 1)

                    def o_dve(u):
                        dve.wait_ge(oT_hi_ready, u + 1)
                        nc.vector.tensor_tensor(hnT_lo[:, u, :], bank[4 + u % 2][:, 0:SEQ],
                                                hnT_hi[:, u, :].bitcast(F32), ALU.subtract
                                                ).then_inc(oT_lo_ready, 1)

                    scores_dve(0)
                    for i in range(HEADS):
                        if i + 1 < HEADS:
                            scores_dve(i + 1)
                        probs_dve(i)
                        if i % 2 == 0 and i >= 4:
                            o_dve(i // 2 - 2)
                    for u in (HEADS // 2 - 2, HEADS // 2 - 1):
                        o_dve(u)
                    for c in rng(11, C_O + 4):
                        split_lo(c)
                    residual_dve(C_O + 3)
                    for c in rng(C_FFN, C_FFN + AHEAD + 1):
                        split_lo(c)

                @block.tensor
                def _(pe):
                    pe.wait_ge(const_ready, 1)
                    transpose_pe(hn, hn_ready, lambda t: t + 1, nT_done)
                    pe.wait_ge(nT_lo_ready, 4)
                    kt = 0
                    for c in range(N_IN):
                        chunk_here(C_IN + c)
                        for k in range(3 if c < 2 else 2):
                            for t in range(TT):
                                for part, (n0, n1) in enumerate(((0, QL), (QL, MLA_IN))):
                                    last = mm3(bank[4 + 2 * t + part][:, 0:n1 - n0], tok(hnT, kt, t),
                                               weights(c, k, n0, n1, MLA_IN), kt == 0, kt == KD - 1)
                            kt += 1
                        last.then_inc(chunk_used, 1)
                    pe.wait_ge(cn_ready, 2 * TT)
                    for b in range(3):
                        for j in range(2 if b < 2 else 1):
                            for t in range(TT):
                                col = (2 * b + j) * P
                                last = nc.tensor.transpose(bank[b][:, j * SEQ + t * P:j * SEQ + (t + 1) * P],
                                                           cqv[:, t, col:col + P], ident[:])
                        last.then_inc(cT_done, 1)
                    for t in range(TT):
                        last = nc.tensor.transpose(bank[3][0:QD, t * P:(t + 1) * P], krp[:, t, :], ident[:])
                    last.then_inc(cT_done, 1)
                    cT = (cT_hi, cT_lo)
                    pe.wait_ge(cT_lo_ready, 3)
                    pe.wait_ge(krT_ready, 1)
                    for c in range(N_QUP):
                        chunk_here(C_QUP + c)
                        for t in range(TT):
                            for n in range(3):
                                last = mm3(bank[2 * n + t][:, :], tok(cT, c, t),
                                           weights(C_QUP + c, 0, n * HALF, (n + 1) * HALF, HEADS * QD),
                                           c == 0, c == N_QUP - 1)
                        last.then_inc(chunk_used, 1)
                    chunk_here(C_KVUP + 1)
                    for u in range(HEADS // 2):
                        if u >= 2:
                            pe.wait_ge(kn_copied, u - 1)
                        for a in range(2):
                            for k in range(N_KVUP):
                                wk = weights(C_KVUP + k, 0, (2 * u + a) * P, (2 * u + a + 1) * P, 0)
                                last = mm3(bank[6 + u % 2][:, a * SEQ:(a + 1) * SEQ], wk,
                                           (cT_hi[:, 3 + k, :], cT_lo[:, 3 + k, :]), k == 0, k == N_KVUP - 1)
                        last.then_inc(kn_done, 1)
                    pe.wait_ge(q_copied, 6)
                    for t in range(TT):
                        for n in range(2):
                            for k in range(N_KVUP):
                                wv = [x[:, (C_KVUP + k) % SPLIT, n * 1024:(n + 1) * 1024].rearrange(
                                    "p (a b) -> p a b", a=8)[:, :, NOPE:NOPE + VD] for x in (w_hi, w_lo)]
                                last = mm3(bank[2 * t + n][:, :].rearrange("p (a b) -> p a b", a=8),
                                           tok(cT, 3 + k, t), wv, k == 0, k == N_KVUP - 1)
                            if (t, n) != (1, 1):
                                last.then_inc(v_done, 1)
                    last.then_inc(chunk_used, 2)
                    pe.wait_ge(q_roped, 1)
                    for u in range(HEADS // 2):
                        if u >= 2:
                            pe.wait_ge(qT_copied, u - 1)
                        for a in range(2):
                            for t in range(TT):
                                col = (2 * u + a) * QD
                                last = nc.tensor.transpose(
                                    bank[4 + u % 2][0:QD, a * SEQ + t * P:a * SEQ + (t + 1) * P],
                                    q_sb[:, t, col:col + QD], ident[:])
                        last.then_inc(qT_done, 1)
                    pe.wait_ge(kr_spread, 1)
                    pe.wait_ge(kn_copied, HEADS // 2)
                    pe.wait_ge(qT_copied, HEADS // 2)
                    pe.wait_ge(v_copied, 4)

                    def scores(i):
                        if i >= 2:
                            pe.wait_ge(max_ready, i - 1)
                        nc.tensor.matmul(bank[i % 2][:, 0:P], qT[:, i, 0:P], kT[:, i, 0:P], start=True, stop=True)
                        nc.tensor.matmul(bank[i % 2][:, P:3 * P], qT[:, i, P:SEQ], kT[:, i, :],
                                         start=True, stop=True).then_inc(score_done, 1)

                    scores(0)
                    for i in range(HEADS):
                        if i + 1 < HEADS:
                            scores(i + 1)
                        pe.wait_ge(prob_ready, i + 1)
                        if i >= 2:
                            pe.wait_ge(probT_copied, i - 1)
                        for j in range(3):
                            last = nc.tensor.transpose(bank[2 + i % 2][:, j * P:(j + 1) * P],
                                                       prob[:, i % 2, j * P:(j + 1) * P], ident[:])
                        last.then_inc(probT_done, 1)
                        pe.wait_ge(probT_copied, i + 1)
                        u, r = i // 2, (i % 2) * VD
                        if i % 2 == 0 and u >= 2:
                            pe.wait_ge(oT_lo_ready, u - 1)
                        ob = bank[4 + u % 2]
                        nc.tensor.matmul(ob[r:r + VD, 0:SEQ], v_sb[:, 0, i * VD:(i + 1) * VD],
                                         probT[:, i % 2, 0:SEQ], start=True, stop=False)
                        nc.tensor.matmul(ob[r:r + VD, P:SEQ], v_sb[:, 1, i * VD:(i + 1) * VD],
                                         probT[:, i % 2, SEQ:3 * P], start=False, stop=True).then_inc(pv_done, 1)
                    pe.wait_ge(oT_lo_ready, HEADS // 2)
                    out_proj_pe(C_O, N_O, hnT)

        ph = ExitStack()
        with ph:
            hidT_hi = sb("hidT_hi", [P, 4 * FB, SEQ], F32R, where=ph)
            hidT_lo = sb("hidT_lo", [P, 4 * FB, SEQ], F32R, where=ph)
            silu = sb("silu", [P, TT, HALF], where=ph)
            hid = sb("hid", [P, TT, HALF], where=ph)
            silu_ready = sem("silu_ready")
            hid_ready = sem("hid_ready")
            hidT_done = sem("hidT_done")
            hidT_hi_ready = sem("hidT_hi_ready")
            hidT_lo_ready = sem("hidT_lo_ready")

            with nc.Block() as block:
                @block.sync
                def _(sp):
                    for c in range(C_FFN + RAW + AHEAD + 1, C_HG + RAW + AHEAD + 1):
                        load_chunk(c)

                @block.scalar
                def _(act):
                    load_gain(2, "mix_norm", 1)
                    act.wait_ge(h_added, 4)
                    norm_act(1)
                    transpose_act(nT_done, 4, nT_hi_ready)

                    def silu_act(b):
                        act.wait_ge(chunk_used, C_FFN + 4 * b + 2)
                        if b:
                            act.wait_ge(hid_ready, TT * b)
                        for t in range(TT):
                            nc.scalar.activation(silu[:, t, :], bank[t][:, :], ACT.Silu).then_inc(silu_ready, 1)

                    def hid_act(b):
                        for t in range(TT):
                            act.wait_ge(hidT_done, TT * b + t + 1)
                            nc.scalar.activation(hidT_hi[:, 4 * b:4 * b + 4, t * P:(t + 1) * P], bank4(4 + t),
                                                 ACT.Copy).then_inc(hidT_hi_ready, 1)

                    for b in range(FB):
                        split_hi(C_FFN + 4 * b + 3)
                        silu_act(b)
                        if 1 <= b < FB - 1:
                            hid_act(b - 1)
                        if b < FB - 1:
                            for c in range(4, 7):
                                split_hi(C_FFN + 4 * b + c)
                    split_hi(C_DOWN)
                    split_hi(C_DOWN + 1)
                    hid_act(FB - 2)
                    split_hi(C_DOWN + 2)
                    hid_act(FB - 1)
                    for c in range(C_DOWN + 3, C_HG + AHEAD + 1):
                        split_hi(c)

                @block.vector
                def _(dve):
                    norm_dve(1)
                    transpose_dve(4, nT_hi_ready, nT_lo_ready)

                    def hid_dve(b):
                        for t in range(TT):
                            dve.wait_ge(silu_ready, TT * b + t + 1)
                            dve.wait_ge(chunk_used, C_FFN + 4 * b + 4)
                            if b:
                                dve.wait_ge(hidT_done, TT * (b - 1) + t + 1)
                            nc.vector.tensor_tensor(hid[:, t, :], silu[:, t, :], bank[2 + t][:, :],
                                                    ALU.mult).then_inc(hid_ready, 1)

                    def hidT_dve(b):
                        for t in range(TT):
                            dve.wait_ge(hidT_hi_ready, TT * b + t + 1)
                            part = slice(4 * b, 4 * b + 4), slice(t * P, (t + 1) * P)
                            nc.vector.tensor_tensor(hidT_lo[:, part[0], part[1]], bank4(4 + t),
                                                    hidT_hi[:, part[0], part[1]].bitcast(F32),
                                                    ALU.subtract).then_inc(hidT_lo_ready, 1)

                    for b in range(FB - 1):
                        split_lo(C_FFN + 4 * b + 3)
                        if b:
                            hidT_dve(b - 1)
                        split_lo(C_FFN + 4 * b + 4)
                        split_lo(C_FFN + 4 * b + 5)
                        hid_dve(b)
                        split_lo(C_FFN + 4 * b + 6)
                    for c in range(C_DOWN - 1, C_DOWN + 2):
                        split_lo(c)
                    hidT_dve(FB - 2)
                    hid_dve(FB - 1)
                    split_lo(C_DOWN + 2)
                    hidT_dve(FB - 1)
                    for c in range(C_DOWN + 3, C_HG):
                        split_lo(c)
                    residual_dve(C_HG - 1, 0)
                    for c in range(C_HG, C_HG + AHEAD + 1):
                        split_lo(c)

                @block.tensor
                def _(pe):
                    transpose_pe(hn, hn_ready, lambda t: TT + t + 1, nT_done)
                    pe.wait_ge(nT_lo_ready, 8)

                    def stream(c0, b0):
                        for q in range(2):
                            chunk_here(c0 + q)
                            for k in range(4):
                                for t in range(TT):
                                    kt = 4 * q + k
                                    last = mm3(bank[b0 + t][:, :], tok(hnT, kt, t),
                                               weights(c0 + q, k, 0, HALF, HALF), kt == 0, kt == KD - 1)
                            last.then_inc(chunk_used, 1)

                    def transposes(b):
                        for t in range(TT):
                            pe.wait_ge(hid_ready, TT * b + t + 1)
                            if b:
                                pe.wait_ge(hidT_lo_ready, TT * (b - 1) + t + 1)
                            for j in range(4):
                                last = nc.tensor.transpose(bank[4 + t][:, j * P:(j + 1) * P],
                                                           hid[:, t, j * P:(j + 1) * P], ident[:])
                            last.then_inc(hidT_done, 1)

                    for b in range(FB):
                        if b:
                            pe.wait_ge(silu_ready, TT * b)
                        stream(C_FFN + 4 * b, 0)
                        if 1 <= b < FB - 1:
                            transposes(b - 1)
                        if b:
                            pe.wait_ge(hid_ready, TT * b)
                        stream(C_FFN + 4 * b + 2, 2)
                    transposes(FB - 2)
                    pe.wait_ge(hid_ready, TT * FB)
                    hidT = (hidT_hi, hidT_lo)
                    pe.wait_ge(hidT_lo_ready, TT * (FB - 2))
                    out_proj_pe(C_DOWN, 2 * FB, hidT, 0, {1: lambda: transposes(FB - 1)},
                                lambda q: pe.wait_ge(hidT_lo_ready, TT * (q // 2 + 1)) if q >= 2 * FB - 4 else None)

        ph = ExitStack()
        with ph:
            qd = sb("qd", [P, HG, SEQ], where=ph)
            kf = sb("kf", [P, HG, SEQ], where=ph)
            g1 = sb("g1", [P, HG, SEQ], where=ph)
            g2 = sb("g2", [P, HG, SEQ], where=ph)
            g3 = sb("g3", [P, HG, SEQ], where=ph)
            v = sb("v", [P, TT, D], where=ph)
            sg = sb("sg", [P, TT, D], where=ph)
            att = sb("att", [P, 2, SEQ], where=ph)
            state = sb("state", [P, 2, 3, DK], where=ph)
            amask = sb("amask", [P, SEQ], where=ph)
            half_lo = sb("half_lo", [P, 1], where=ph)
            half_hi = sb("half_hi", [P, 1], where=ph)
            smask = sb("smask", [P, SEQ], where=ph)
            ogain = sb("ogain", [P, DK], where=ph)
            lbs = sb("lbs", [P, 2, HG], where=ph)
            lbt = sb("lbt", [P, 2, HG], where=ph)
            lbm = sb("lbm", [P, HG], where=ph)
            lb = sb("lb", [P, HG], where=ph)
            oml = sb("oml", [P, HG], where=ph)
            dec = sb("dec", [P, HG * SEQ // CH], where=ph)
            oss = sb("oss", [P, TT, HG], where=ph)
            kd_even = kf[:, :, :].rearrange("p a s -> p (a s)").rearrange("p (t n) -> p t n", t=TT)
            kd_odd = g2[:, :, :].rearrange("p a s -> p (a s)").rearrange("p (t n) -> p t n", t=TT)
            o_sb = hn
            NC_ = SEQ // CH

            hg_loaded = sem("hg_loaded")
            hg_const = sem("hg_const")
            hg_step = sem("hg_step")
            lbd_ready = sem("lbd_ready")
            lbe_ready = sem("lbe_ready")
            fq_copied = sem("fq_copied")
            vg_copied = sem("vg_copied")
            f_ready = sem("f_ready")
            logf_ready = sem("logf_ready")
            b_ready = sem("b_ready")
            eb_ready = sem("eb_ready")
            qd_ready = sem("qd_ready")
            enb_ready = sem("enb_ready")
            bl_ready = sem("bl_ready")
            ebl_ready = sem("ebl_ready")
            kd_ready = sem("kd_ready")
            kdec_ready = sem("kdec_ready")
            kdT_done = sem("kdT_done")
            kdT_copied = sem("kdT_copied")
            a_done = sem("a_done")
            a_ready = sem("a_ready")
            kv_done = sem("kv_done")
            state_ready = sem("state_ready")
            o_done = sem("o_done")
            o_copied = sem("o_copied")
            oms_ready = sem("oms_ready")
            orms_ready = sem("orms_ready")
            on_ready = sem("on_ready")

            with nc.Block() as block:
                @block.sync
                def _(sp):
                    for c in range(C_HG + RAW + AHEAD + 1, C_MOE):
                        load_chunk(c)
                    for k in range(RAW + AHEAD + 1):
                        load_chunk(C_MOE + k, item_dram(k, 0))

                @block.gpsimd
                def _(pool):
                    for tile, value in ((smask, 1.0), (half_lo, 0.0), (half_hi, 0.0), (att, 0.0), (amask, 1.0)):
                        pool_link(nc.gpsimd.memset(tile[:], value))
                    pool_link(nc.gpsimd.memset(smask[:, :].rearrange("p (a b) -> p a b", a=NC_)[:, :, 0:1], 0.0))
                    pool_link(nc.gpsimd.memset(half_lo[0:CH, :], 1.0))
                    pool_link(nc.gpsimd.memset(half_hi[CH:P, :], 1.0))
                    for t in range(TT):
                        part = amask[:, t * P:(t + 1) * P]
                        pool_link(nc.gpsimd.affine_select(out=part, in_=part, compare_op=ALU.is_ge, fill=0.0,
                                                          base=0, pattern=[[1, P]], channel_multiplier=-1))
                        pool_link(nc.gpsimd.memset(amask[0:CH, t * P + CH:(t + 1) * P], 0.0))
                    nc.gpsimd.memset(half_lo[0:CH, :], 1.0).then_inc(hg_const, 1)

                @block.scalar
                def _(act):
                    load_gain(3, "ffn_norm", 1)
                    nc.scalar.dma_start(ogain[:], w["hgrn_out_norm"].broadcast_to([P, DK])).then_inc(hg_loaded, 16)
                    for l in range(2):
                        nc.scalar.dma_start(lbs[:, l, :], w["hgrn_lower_bounds"][l:l + 1, :].rearrange(
                            "l (a p) -> p (l a)", p=P), allow_slow_non_contiguous=True).then_inc(hg_loaded, 16)
                    act.wait_ge(h_added, 8)
                    norm_act(2)
                    transpose_act(nT_done, 8, nT_hi_ready)
                    act.wait_ge(lbd_ready, 1)
                    nc.scalar.activation(lbs[:], lbt[:], ACT.Exp).then_inc(lbe_ready, 1)

                    def evacuate(B):
                        act.wait_ge(chunk_used, C_HG + 2 * B + 2)
                        if B < 4:
                            for a in range(4):
                                dst = (kf if B < 2 else qd)[:, 4 * (B % 2) + a, :]
                                src = bank[4 * (B % 2) + a][:, 0:SEQ]
                                if B < 2:
                                    nc.scalar.activation(dst, src, ACT.Sigmoid).then_inc(fq_copied, 1)
                                else:
                                    nc.scalar.activation(dst, src, ACT.Copy, scale=float(np.float32(DK ** -0.5))
                                                         ).then_inc(fq_copied, 1)
                        else:
                            n = B % 2
                            for t in range(TT):
                                dst = (v if B < 6 else sg)[:, t, n * HALF:(n + 1) * HALF]
                                src = bank[(0 if B < 6 else 4) + 2 * n + t][:, :]
                                nc.scalar.activation(dst, src, ACT.Copy if B < 6 else ACT.Silu
                                                     ).then_inc(vg_copied, 1)

                    for B in range(8):
                        split_hi(C_HG + 2 * B + 3)
                        if B == 2:
                            act.wait_ge(f_ready, 1)
                            nc.scalar.activation(g1[:], kf[:], ACT.Ln).then_inc(logf_ready, 1)
                        if B == 3:
                            act.wait_ge(b_ready, 1)
                            nc.scalar.activation(g1[:], g2[:], ACT.Exp).then_inc(eb_ready, 1)
                        if B == 5:
                            act.wait_ge(qd_ready, 1)
                            nc.scalar.activation(g1[:], g2[:], ACT.Exp, scale=-1.0).then_inc(enb_ready, 1)
                        if B == 6:
                            act.wait_ge(bl_ready, 1)
                            last_b = g2[:, :, :].rearrange("p a s -> p (a s)").rearrange(
                                "p (n c) -> p n c", c=CH)[:, :, CH - 1]
                            nc.scalar.activation(dec[:], last_b, ACT.Exp)
                            nc.scalar.activation(g3[:], g3[:], ACT.Exp).then_inc(ebl_ready, 1)
                        evacuate(B)
                        split_hi(C_HG + 2 * B + 4)
                    for t in range(TT):
                        for g in range(2):
                            act.wait_ge(kdT_done, 2 * t + g + 1)
                            nc.scalar.activation(kd_even[:, t, g * HALF:(g + 1) * HALF], bank[2 * t + g][:, :],
                                                 ACT.Copy, scale=half_lo[:]).then_inc(kdT_copied, 1)
                            if t == 0:
                                nc.scalar.activation(kd_odd[:, t, g * HALF:(g + 1) * HALF], bank[2 * t + g][:, :],
                                                     ACT.Copy, scale=half_hi[:]).then_inc(kdT_copied, 1)
                    for i in range(HG):
                        act.wait_ge(o_done, i + 1)
                        nc.scalar.activation(o_sb[:, :, i * DK:(i + 1) * DK],
                                             bank[4 + i % 2][:, 0:SEQ].rearrange("p (t n) -> p t n", t=TT),
                                             ACT.Copy).then_inc(o_copied, 1)
                    act.wait_ge(oms_ready, 1)
                    nc.scalar.activation(oss[:], oss[:], ACT.Sqrt).then_inc(orms_ready, 1)
                    transpose_act(nT_done, 12, nT_hi_ready)
                    for c in range(C_HGO + 3, C_MOE + AHEAD + 1):
                        split_hi(c)

                @block.vector
                def _(dve):
                    norm_dve(2)
                    transpose_dve(8, nT_hi_ready, nT_lo_ready)
                    dve.wait_ge(hg_loaded, 48)
                    dve_link(nc.vector.tensor_tensor(lbm[:], lbs[:, 0, :], lbs[:, 1, :], ALU.max))
                    nc.vector.tensor_tensor(lbt[:, 0, :], lbs[:, 0, :], lbm[:], ALU.subtract)
                    nc.vector.tensor_tensor(lbt[:, 1, :], lbs[:, 1, :], lbm[:], ALU.subtract).then_inc(lbd_ready, 1)
                    dve.wait_ge(lbe_ready, 1)
                    dve_link(nc.vector.tensor_tensor(lbm[:], lbs[:, 0, :], lbs[:, 1, :], ALU.add))
                    dve_link(nc.vector.reciprocal(lbm[:], lbm[:]))
                    nc.vector.tensor_tensor(lbt[:, 0, :], lbs[:, 0, :], lbm[:], ALU.mult)
                    dve_link(nc.vector.tensor_tensor(lbt[:, 1, :], lbs[:, 1, :], lbm[:], ALU.mult))
                    dve_link(nc.vector.tensor_tensor(lb[:], lbt[:, 0, :], lbt[:, 1, :], ALU.add))
                    dve_link(nc.vector.tensor_tensor(lb[:], lb[:], lbt[:, 0, :], ALU.subtract))
                    dve_link(nc.vector.tensor_scalar(oml[:], lb[:], -1.0, 1.0, ALU.mult, ALU.add))
                    dve.wait_ge(hg_const, 1)
                    for B in range(8):
                        split_lo(C_HG + 2 * B + 3)
                        if B == 1:
                            dve.wait_ge(fq_copied, 8)
                            for a in range(HG):
                                last = nc.vector.tensor_scalar(kf[:, a, :], kf[:, a, :], oml[:, a:a + 1],
                                                               lb[:, a:a + 1], ALU.mult, ALU.add)
                            last.then_inc(f_ready, 1)
                        if B == 2:
                            dve.wait_ge(logf_ready, 1)
                            for a in range(HG):
                                last = nc.vector.tensor_tensor_scan(g2[:, a, :], smask[:], g1[:, a, :], 0.0,
                                                                    ALU.mult, ALU.add)
                            last.then_inc(b_ready, 1)
                            nc.vector.tensor_scalar(kf[:], kf[:], -1.0, 1.0, ALU.mult, ALU.add
                                                    ).then_inc(hg_step, 1)
                        if B == 4:
                            dve.wait_ge(eb_ready, 1)
                            dve.wait_ge(fq_copied, 16)
                            nc.vector.tensor_tensor(qd[:], qd[:], g1[:], ALU.mult).then_inc(qd_ready, 1)
                            dve.wait_ge(b_ready, 1)
                            bv = g2[:, :, :].rearrange("p a s -> p (a s)").rearrange("p (n c) -> p n c", c=CH)
                            nc.vector.tensor_tensor(
                                g3[:, :, :].rearrange("p a s -> p (a s)").rearrange("p (n c) -> p n c", c=CH),
                                bv[:, :, CH - 1:CH].broadcast_to([P, HG * NC_, CH]), bv, ALU.subtract
                            ).then_inc(bl_ready, 1)
                        if B == 6:
                            dve.wait_ge(enb_ready, 1)
                            dve.wait_ge(hg_step, 1)
                            nc.vector.tensor_tensor(g1[:], kf[:], g1[:], ALU.mult).then_inc(kd_ready, 1)
                        if B == 7:
                            dve.wait_ge(ebl_ready, 1)
                            nc.vector.tensor_tensor(g3[:], kf[:], g3[:], ALU.mult).then_inc(kdec_ready, 1)
                        split_lo(C_HG + 2 * B + 4)
                    dve.wait_ge(vg_copied, 8)
                    sv = sg[:, :, :].rearrange("p t n -> p (t n)").rearrange("p (a n) -> p a n", n=DK)
                    nc.vector.tensor_tensor(sv, sv, ogain[:, :].unsqueeze(1).broadcast_to([P, TT * HG, DK]),
                                            ALU.mult).then_inc(hg_step, 1)

                    for i in range(HG):
                        dve.wait_ge(a_done, i + 1)
                        if i >= 2:
                            dve.wait_ge(o_done, i - 1)
                        nc.vector.copy_predicated(att[:, i % 2, :], amask[:].bitcast(U32),
                                                  bank[i % 2][:, 0:SEQ]).then_inc(a_ready, 1)
                        dve.wait_ge(kv_done, i + 1)
                        kv = bank[2 + i % 2]
                        dve_link(nc.vector.tensor_copy(state[:, i % 2, 0, :], kv[:, 0:DK]))
                        dve_link(nc.vector.scalar_tensor_tensor(
                            state[:, i % 2, 1, :], state[:, i % 2, 0, :], dec[:, NC_ * i + 1:NC_ * i + 2],
                            kv[:, DK:2 * DK], ALU.mult, ALU.add))
                        nc.vector.scalar_tensor_tensor(
                            state[:, i % 2, 2, :], state[:, i % 2, 1, :], dec[:, NC_ * i + 2:NC_ * i + 3],
                            kv[:, 2 * DK:3 * DK], ALU.mult, ALU.add).then_inc(state_ready, 1)
                    dve.wait_ge(o_copied, HG)
                    sq = g3[:, :, :].rearrange("p a s -> p (a s)").rearrange("p (t n) -> p t n", t=TT)
                    dve_link(nc.vector.tensor_tensor(sq, o_sb[:], o_sb[:], ALU.mult))
                    dve_link(nc.vector.tensor_reduce(
                        oss[:, :, :].rearrange("p t a -> p (t a)"),
                        sq.rearrange("p t n -> p (t n)").rearrange("p (a n) -> p a n", n=DK), AX.X, ALU.add))
                    nc.vector.tensor_scalar(oss[:], oss[:], 1.0 / DK, EPS, ALU.mult, ALU.add).then_inc(oms_ready, 1)
                    dve.wait_ge(orms_ready, 1)
                    dve_link(nc.vector.reciprocal(oss[:], oss[:]))
                    dve.wait_ge(hg_step, 2)
                    for t in range(TT):
                        ov = o_sb[:, t, :].rearrange("p (a n) -> p a n", n=DK)
                        dve_link(nc.vector.tensor_tensor(
                            ov, ov, oss[:, t, :].unsqueeze(2).broadcast_to([P, HG, DK]), ALU.mult))
                        nc.vector.tensor_tensor(o_sb[:, t, :], o_sb[:, t, :], sg[:, t, :], ALU.mult
                                                ).then_inc(on_ready, 1)
                    transpose_dve(12, nT_hi_ready, nT_lo_ready)
                    split_lo(C_HGO + 3)
                    residual_dve(C_MOE - 1)
                    for c in range(C_MOE, C_MOE + AHEAD + 1):
                        split_lo(c)

                @block.tensor
                def _(pe):
                    transpose_pe(hn, hn_ready, lambda t: 2 * TT + t + 1, nT_done)
                    pe.wait_ge(nT_lo_ready, 12)
                    for B in range(8):
                        c0 = C_HG + 2 * B
                        if 2 <= B < 4:
                            pe.wait_ge(fq_copied, 4 * (B - 1))
                        elif 4 <= B < 6:
                            pe.wait_ge(fq_copied, 12)
                        elif B >= 6:
                            pe.wait_ge(fq_copied, 16)
                        for q in range(2):
                            chunk_here(c0 + q)
                            for k in range(4):
                                kt = 4 * q + k
                                if B < 4:
                                    for a in range(4):
                                        last = mm3(bank[4 * (B % 2) + a][:, 0:SEQ],
                                                   weights(c0 + q, k, a * P, (a + 1) * P, HALF),
                                                   (hnT_hi[:, kt, :], hnT_lo[:, kt, :]), kt == 0, kt == KD - 1)
                                else:
                                    for t in range(TT):
                                        last = mm3(bank[(0 if B < 6 else 4) + 2 * (B % 2) + t][:, :],
                                                   tok(hnT, kt, t), weights(c0 + q, k, 0, HALF, HALF),
                                                   kt == 0, kt == KD - 1)
                            last.then_inc(chunk_used, 1)
                    pe.wait_ge(kdec_ready, 1)
                    pe.wait_ge(vg_copied, 4)
                    for t in range(TT):
                        for g in range(2):
                            for a in range(4):
                                last = nc.tensor.transpose(bank[2 * t + g][:, a * P:(a + 1) * P],
                                                           g3[:, 4 * g + a, t * P:(t + 1) * P], ident[:])
                            last.then_inc(kdT_done, 1)
                    pe.wait_ge(kdT_copied, 6)
                    pe.wait_ge(vg_copied, 8)
                    pe.wait_ge(kd_ready, 1)
                    pe.wait_ge(qd_ready, 1)

                    def head_scores(i):
                        if i >= 2:
                            pe.wait_ge(a_ready, i - 1)
                            pe.wait_ge(state_ready, i - 1)
                        for t in range(TT):
                            last = nc.tensor.matmul(bank[i % 2][:, t * P:(t + 1) * P], g1[:, i, t * P:(t + 1) * P],
                                                    qd[:, i, t * P:(t + 1) * P], start=True, stop=True)
                        last.then_inc(a_done, 1)
                        hd = slice(i * DK, (i + 1) * DK)
                        for n, (kd, t) in enumerate(((kd_even, 0), (kd_odd, 0), (kd_even, 1))):
                            last = nc.tensor.matmul(bank[2 + i % 2][:, n * DK:(n + 1) * DK], kd[:, t, hd], v[:, t, hd],
                                                    start=True, stop=True)
                        last.then_inc(kv_done, 1)

                    head_scores(0)
                    for i in range(HG):
                        if i + 1 < HG:
                            head_scores(i + 1)
                        pe.wait_ge(a_ready, i + 1)
                        pe.wait_ge(state_ready, i + 1)
                        if i >= 2:
                            pe.wait_ge(o_copied, i - 1)
                        hd = slice(i * DK, (i + 1) * DK)
                        for t in range(TT):
                            ob = bank[4 + i % 2][:, t * DK:(t + 1) * DK]
                            nc.tensor.matmul(ob, att[:, i % 2, t * P:(t + 1) * P], v[:, t, hd], start=True, stop=True)
                            for half in range(2):
                                n = 2 * t + half
                                if n == 0:
                                    continue
                                last = nc.tensor.matmul(ob[half * CH:(half + 1) * CH, :],
                                                        qd[:, i, n * CH:(n + 1) * CH], state[:, i % 2, n - 1, :],
                                                        start=False, stop=True, skip_group_check=True)
                        last.then_inc(o_done, 1)
                    transpose_pe(o_sb, on_ready, lambda t: t + 1, nT_done)
                    pe.wait_ge(nT_lo_ready, 16)
                    pe.wait_ge(o_copied, HG)
                    out_proj_pe(C_HGO, 4, hnT)

        ph = ExitStack()
        with ph:
            rt_raw = sb("rt_raw", [P, KD, E], where=ph)
            rt_hi = sb("rt_hi", [P, KD, E], F32R, where=ph)
            rt_lo = sb("rt_lo", [P, KD, E], F32R, where=ph)
            logit = sb("logit", [P, TT, E], where=ph)
            top = sb("top", [P, TT, 8], where=ph)
            topi = sb("topi", [P, TT, 8], U32, where=ph)
            topf = sb("topf", [P, TT, 8], where=ph)
            sel = sb("sel", [P, TT, 2, E], where=ph)
            wts = sb("wts", [P, TT, 4], where=ph)
            gates = sb("gates", [P, TT, E], where=ph)
            chosen = sb("chosen", [P, TT, E], where=ph)
            slot = sb("slot", [P, TT, E], where=ph)
            count = sb("count", [P, E], where=ph)
            over = sb("over", [P, E], where=ph)
            rank = sb("rank", [P, E], where=ph)
            scratch = sb("scratch", [P, E], where=ph)
            iota_e = sb("iota_e", [P, E], where=ph)
            ones_e = sb("ones_e", [P, E], where=ph)
            iota_s = sb("iota_s", [P, P], where=ph)
            before = sb("before", [P, P], where=ph)
            ones = sb("ones", [P, P], where=ph)
            shift = sb("shift", [P, 16], where=ph)
            plan_f = sb("plan_f", [P, 16], where=ph)
            plan = sb("plan", [1, 16], I32, where=ph)
            slot_i = sb("slot_i", [P, TT], where=ph)
            onehot = sb("onehot", [P, TT, P], where=ph)
            onehotT = sb("onehotT", [P, SEQ], F32R, where=ph)
            xT_hi = sb("xT_hi", [P, KD, P], F32R, where=ph)
            xT_lo = sb("xT_lo", [P, KD, P], F32R, where=ph)
            silu2 = sb("silu2", [P, 2, HALF], where=ph)
            hid2 = sb("hid2", [P, 2, HALF], where=ph)
            hT_hi = sb("hT_hi", [P, 2, 4, P], F32R, where=ph)
            hT_lo = sb("hT_lo", [P, 2, 4, P], F32R, where=ph)
            y_hi = sb("y_hi", [P, D], F32R, where=ph)
            y_lo = sb("y_lo", [P, D], F32R, where=ph)

            rt_loaded = sem("rt_loaded")
            moe_const = sem("moe_const")
            rt_hi_ready = sem("rt_hi_ready")
            rt_lo_ready = sem("rt_lo_ready")
            logits_done = sem("logits_done")
            diff_ready = sem("diff_ready")
            e2_ready = sem("e2_ready")
            chosen_ready = sem("chosen_ready")
            places_done = sem("places_done")
            plan_ready = sem("plan_ready")
            slot_ready = sem("slot_ready")
            onehot_ready = sem("onehot_ready")
            gathered = sem("gathered")
            xT_hi_ready = sem("xT_hi_ready")
            xT_lo_ready = sem("xT_lo_ready")
            onehotT_done = sem("onehotT_done")
            onehotT_ready = sem("onehotT_ready")
            silu2_ready = sem("silu2_ready")
            hid2_ready = sem("hid2_ready")
            hT_done = sem("hT_done")
            hT_hi_ready = sem("hT_hi_ready")
            hT_lo_ready = sem("hT_lo_ready")
            y_hi_ready = sem("y_hi_ready")
            y_lo_ready = sem("y_lo_ready")
            scattered = sem("scattered")
            combined = sem("combined")
            out_stored = sem("out_stored")
            G, U_, T_, Y, X = (0, 1), 2, 3, (4, 5), (6, 7)
            PRIMED = 1
            TURN = 16 * PER_ITEM // RAW

            def n_items_on(eng):
                eng.wait_ge(plan_ready, 1)
                return eng.value_load(plan[0:1, 12:13], min_val=E, max_val=MAX_ITEMS)

            def expert_on(eng, i):
                return eng.value_load(plan[0:1, bass.ds(i, 1)], min_val=0, max_val=E - 1)

            with nc.Block() as block:
                @block.sync
                def _(sp):
                    def load(k, i, e):
                        c = C_MOE + k
                        sp.wait_ge(lo_ready, PER_ITEM * i + (c - RAW + 1))
                        nc.sync.dma_start(w_raw[:, c % RAW, :].rearrange("p (k n) -> p k n",
                                                                         k=2 if item[k][0] == "down" else 4),
                                          item_dram(k, e)).then_inc(raw_loaded[c % RAW], 16)

                    first = RAW + AHEAD + 1
                    with sp.Fori(0, E - 1) as i:
                        for k in range(first, PER_ITEM):
                            load(k, i, i)
                        for k in range(first):
                            load(k, i + 1, i + 1)
                    for k in range(first, PER_ITEM):
                        load(k, E - 1, E - 1)
                    n = n_items_on(sp)
                    with sp.If(n > E):
                        with sp.Fori(E, n) as i:
                            e = expert_on(sp, i)
                            for k in range(PER_ITEM):
                                load(k, i, e)
                    for k in range(AHEAD + 1):
                        load(k, n, 0)
                    for t in range(TT):
                        sp.wait_ge(hn_ready, 4 * TT + t + 1)
                        nc.sync.dma_start(out[0, t * P:(t + 1) * P, :], hn[:, t, :]).then_inc(out_stored, 16)
                    sp.wait_ge(out_stored, 16 * TT)

                @block.gpsimd
                def _(pool):
                    for tile, value in ((before, 1.0), (ones, 1.0), (ones_e, 1.0), (shift, 0.0), (plan_f, 0.0)):
                        pool_link(nc.gpsimd.memset(tile[:], value))
                    pool_link(nc.gpsimd.memset(shift[:, E:16], float(-P)))
                    pool_link(nc.gpsimd.affine_select(out=before[:], in_=before[:], compare_op=ALU.is_gt, fill=0.0,
                                                      base=0, pattern=[[1, P]], channel_multiplier=-1))
                    pool_link(nc.gpsimd.iota(iota_s[:], pattern=[[1, P]], base=0, channel_multiplier=0,
                                             allow_small_or_imprecise_dtypes=True))
                    nc.gpsimd.iota(iota_e[:], pattern=[[1, E]], base=0, channel_multiplier=0,
                                   allow_small_or_imprecise_dtypes=True).then_inc(moe_const, 1)

                @block.scalar
                def _(act):
                    nc.scalar.dma_start(rt_raw[:], w["moe_router"][0].rearrange("(k p) e -> p k e", p=P)
                                        ).then_inc(rt_loaded, 16)
                    load_gain(4, "final_norm", None)
                    act.wait_ge(h_added, 12)
                    norm_act(3)
                    transpose_act(nT_done, 16, nT_hi_ready)
                    act.wait_ge(rt_loaded, 16)
                    nc.scalar.activation(rt_hi[:], rt_raw[:], ACT.Copy).then_inc(rt_hi_ready, 1)
                    act.wait_ge(diff_ready, 1)
                    nc.scalar.activation(wts[:, :, 0:1], wts[:, :, 0:1], ACT.Exp).then_inc(e2_ready, 1)

                    def xT_act(item_no):
                        for g in range(2):
                            act.wait_ge(gathered, 2 * item_no + (g + 1))
                            nc.scalar.activation(xT_hi[:, 4 * g:4 * g + 4, :], bank4(X[g]), ACT.Copy
                                                 ).then_inc(xT_hi_ready, 1)

                    act.sem_inc(silu2_ready, PRIMED)
                    xT_act(0)
                    n = n_items_on(act)
                    with act.Fori(0, n) as i:
                        base, turn = PER_ITEM * i, TURN * i

                        def silu_of(b):
                            act.wait_ge(chunk_used, base + (C_MOE + (2 if b == 0 else 6 * b)))
                            act.wait_ge(hid2_ready, FB * i + at_most(b - 1) + PRIMED)
                            nc.scalar.activation(silu2[:, b % 2, :], bank[G[b % 2]][:, :], ACT.Silu
                                                 ).then_inc(silu2_ready, 1)

                        def hT_of(b):
                            act.wait_ge(hT_done, FB * i + (b + 1) + PRIMED)
                            if b >= 2:
                                act.wait_ge(chunk_used, base + (C_MOE + 6 * (b - 1) + 4))
                            else:
                                act.wait_ge(chunk_used, base + C_MOE)
                            nc.scalar.activation(hT_hi[:, b % 2, :, :], bank4(T_), ACT.Copy).then_inc(hT_hi_ready, 1)

                        for k in range(AHEAD + 1, PER_ITEM + AHEAD + 1):
                            split_hi(C_MOE + k, base, turn)
                            if k % 6 == 1 and k > 1 and k < PER_ITEM - 1:
                                silu_of(k // 6)
                                hT_of(k // 6 - 1)
                            elif k == 3:
                                silu_of(0)
                            elif k == 9:
                                act.wait_ge(onehotT_done, i + 1)
                                act.wait_ge(scattered, 4 * i + PRIMED)
                                nc.scalar.activation(onehotT[:], bank[T_][:, 0:SEQ], ACT.Copy
                                                     ).then_inc(onehotT_ready, 1)
                            elif k == PER_ITEM - 2:
                                hT_of(FB - 1)
                            elif k == PER_ITEM - 1:
                                xT_act(i + 1)
                            elif k == PER_ITEM + 1:
                                for g in range(2):
                                    act.wait_ge(chunk_used, base + (C_MOE + PER_ITEM))
                                    nc.scalar.activation(y_hi[:, g * HALF:(g + 1) * HALF], bank[Y[g]][:, :], ACT.Copy
                                                         ).then_inc(y_hi_ready, 1)
                    act.wait_ge(combined, 4 * n + PRIMED)
                    norm_act(4)

                @block.vector
                def _(dve):
                    norm_dve(3)
                    transpose_dve(16, nT_hi_ready, nT_lo_ready)
                    dve.wait_ge(rt_hi_ready, 1)
                    nc.vector.tensor_tensor(rt_lo[:], rt_raw[:], rt_hi[:].bitcast(F32), ALU.subtract
                                            ).then_inc(rt_lo_ready, 1)
                    dve.wait_ge(moe_const, 1)
                    dve.wait_ge(logits_done, 1)
                    dve_link(nc.vector.tensor_copy(logit[:], bank[4][:, 0:TT * E].rearrange(
                        "p (t e) -> p t e", t=TT)))
                    for t in range(TT):
                        dve_link(nc.vector.max(top[:, t, :], logit[:, t, :]))
                        dve_link(nc.vector.max_index(topi[:, t, :], top[:, t, :], logit[:, t, :]))
                    nc.vector.tensor_tensor(wts[:, :, 0:1], top[:, :, 1:2], top[:, :, 0:1], ALU.subtract
                                            ).then_inc(diff_ready, 1)
                    dve_link(nc.vector.tensor_copy(topf[:], topi[:]))
                    for t in range(TT):
                        for a in range(2):
                            last = nc.vector.tensor_scalar(sel[:, t, a, :], iota_e[:], topf[:, t, a:a + 1], None,
                                                           ALU.is_equal)
                    dve_link(last)
                    nc.vector.tensor_tensor(chosen[:], sel[:, :, 0, :], sel[:, :, 1, :], ALU.add
                                            ).then_inc(chosen_ready, 1)
                    dve.wait_ge(e2_ready, 1)
                    dve_link(nc.vector.tensor_scalar(wts[:, :, 1:2], wts[:, :, 0:1], 1.0, None, ALU.add))
                    dve_link(nc.vector.reciprocal(wts[:, :, 2:3], wts[:, :, 1:2]))
                    dve_link(nc.vector.tensor_tensor(wts[:, :, 3:4], wts[:, :, 2:3], wts[:, :, 0:1], ALU.mult))
                    for t in range(TT):
                        dve_link(nc.vector.tensor_scalar(gates[:, t, :], sel[:, t, 0, :], wts[:, t, 2:3], None,
                                                         ALU.mult))
                        dve_link(nc.vector.scalar_tensor_tensor(gates[:, t, :], sel[:, t, 1, :], wts[:, t, 3:4],
                                                                gates[:, t, :], ALU.mult, ALU.add))
                    dve.wait_ge(places_done, 1)
                    dve_link(nc.vector.tensor_scalar(slot[:], bank[5][:, 0:TT * E].rearrange(
                        "p (t e) -> p t e", t=TT), 1.0, None, ALU.add))
                    dve_link(nc.vector.tensor_tensor(slot[:], slot[:], chosen[:], ALU.mult))
                    dve_link(nc.vector.tensor_scalar(slot[:], slot[:], -1.0, None, ALU.add))
                    dve_link(nc.vector.tensor_scalar(over[:], bank[5][:, TT * E:(TT + 1) * E], float(P), None,
                                                     ALU.is_gt))
                    dve_link(nc.vector.tensor_tensor_scan(rank[:], ones_e[:], over[:], 0.0, ALU.mult, ALU.add))
                    dve_link(nc.vector.tensor_scalar(plan_f[:, 12:13], rank[:, E - 1:E], float(E), None, ALU.add))
                    dve_link(nc.vector.tensor_tensor(rank[:], rank[:], over[:], ALU.mult))
                    dve_link(nc.vector.tensor_copy(plan_f[:, 0:E], iota_e[:]))
                    for r in range(MAX_EXTRA):
                        dve_link(nc.vector.tensor_scalar(scratch[:], rank[:], float(r + 1), None, ALU.is_equal))
                        dve_link(nc.vector.tensor_tensor(scratch[:], scratch[:], iota_e[:], ALU.mult))
                        dve_link(nc.vector.tensor_reduce(plan_f[:, E + r:E + r + 1], scratch[:], AX.X, ALU.add))
                    nc.vector.tensor_copy(plan[:], plan_f[0:1, :]).then_inc(plan_ready, 1)

                    def onehot_of(item_no, e):
                        nc.vector.tensor_scalar(slot_i[:], slot[:, :, bass.ds(e, 1)].rearrange("p t e -> p (t e)"),
                                                shift[:, bass.ds(item_no, 1)], None, ALU.add
                                                ).then_inc(slot_ready, 1)
                        dve.wait_ge(slot_ready, item_no + 1)
                        nc.vector.tensor_scalar(onehot[:, 0, :], iota_s[:], slot_i[:, 0:1], None, ALU.is_equal)
                        nc.vector.tensor_scalar(onehot[:, 1, :], iota_s[:], slot_i[:, 1:2], None, ALU.is_equal
                                                ).then_inc(onehot_ready, 1)

                    def xT_dve(item_no):
                        for g in range(2):
                            dve.wait_ge(xT_hi_ready, 2 * item_no + (g + 1))
                            nc.vector.tensor_tensor(xT_lo[:, 4 * g:4 * g + 4, :], bank4(X[g]),
                                                    xT_hi[:, 4 * g:4 * g + 4, :].bitcast(F32), ALU.subtract
                                                    ).then_inc(xT_lo_ready, 1)

                    n = n_items_on(dve)
                    for primed in (hid2_ready, hT_lo_ready, y_lo_ready, combined):
                        dve.sem_inc(primed, PRIMED)
                    onehot_of(0, 0)
                    xT_dve(0)
                    with dve.Fori(0, n) as i:
                        base = PER_ITEM * i

                        def hid_of(b):
                            dve.wait_ge(silu2_ready, FB * i + (b + 1) + PRIMED)
                            dve.wait_ge(chunk_used, base + (C_MOE + (4 if b == 0 else 6 * b + 2)))
                            dve.wait_ge(hT_done, FB * i + at_most(b - 1) + PRIMED)
                            nc.vector.tensor_tensor(hid2[:, b % 2, :], silu2[:, b % 2, :], bank[U_][:, :], ALU.mult
                                                    ).then_inc(hid2_ready, 1)

                        def hT_of(b):
                            dve.wait_ge(hT_hi_ready, FB * i + (b + 1))
                            nc.vector.tensor_tensor(hT_lo[:, b % 2, :, :], bank4(T_),
                                                    hT_hi[:, b % 2, :, :].bitcast(F32), ALU.subtract
                                                    ).then_inc(hT_lo_ready, 1)

                        for k in range(AHEAD + 1, PER_ITEM + AHEAD + 1):
                            split_lo(C_MOE + k, base)
                            if k % 6 == 3 and k > 3 and k < PER_ITEM - 1:
                                hid_of(k // 6)
                            elif k == 5:
                                hid_of(0)
                            elif k % 6 == 1 and k > 1 and k < PER_ITEM - 1:
                                hT_of(k // 6 - 1)
                            elif k == 26:
                                dve.wait_ge(onehotT_done, i + 1)
                                dve.wait_ge(gathered, 2 * i + 2)
                                onehot_of(i + 1, expert_on(dve, i + 1))
                            elif k == PER_ITEM - 2:
                                hT_of(FB - 1)
                            elif k == PER_ITEM - 1:
                                xT_dve(i + 1)
                            elif k == PER_ITEM + 1:
                                for g in range(2):
                                    dve.wait_ge(y_hi_ready, 2 * i + (g + 1))
                                    part = slice(g * HALF, (g + 1) * HALF)
                                    nc.vector.tensor_tensor(y_lo[:, part], bank[Y[g]][:, :], y_hi[:, part].bitcast(F32),
                                                            ALU.subtract).then_inc(y_lo_ready, 1)
                                e = expert_on(dve, i)
                                dve.wait_ge(combined, 4 * i + PRIMED)
                                for g in range(2):
                                    for t in range(TT):
                                        dve.wait_ge(scattered, 4 * i + (2 * g + t + 1) + PRIMED)
                                        part = h[:, t, g * HALF:(g + 1) * HALF]
                                        nc.vector.scalar_tensor_tensor(
                                            part, bank[X[t]][:, :], gates[:, t, bass.ds(e, 1)], part,
                                            ALU.mult, ALU.add).then_inc(combined, 1)
                    norm_dve(4)

                @block.tensor
                def _(pe):
                    transpose_pe(hn, hn_ready, lambda t: 3 * TT + t + 1, nT_done)
                    pe.wait_ge(nT_lo_ready, 20)
                    pe.wait_ge(rt_lo_ready, 1)
                    for t in range(TT):
                        for k in range(KD):
                            last = mm3(bank[4][:, t * E:(t + 1) * E], tok(hnT, k, t),
                                       (rt_hi[:, k, :], rt_lo[:, k, :]), k == 0, k == KD - 1)
                    last.then_inc(logits_done, 1)
                    pe.wait_ge(chosen_ready, 1)
                    nc.tensor.matmul(bank[5][:, 0:E], before[:], chosen[:, 0, :], start=True, stop=True)
                    nc.tensor.matmul(bank[5][:, E:2 * E], ones[:], chosen[:, 0, :], start=True, stop=False)
                    nc.tensor.matmul(bank[5][:, E:2 * E], before[:], chosen[:, 1, :], start=False, stop=True)
                    for t in range(TT):
                        last = nc.tensor.matmul(bank[5][:, 2 * E:3 * E], ones[:], chosen[:, t, :],
                                                start=t == 0, stop=t == TT - 1)
                    last.then_inc(places_done, 1)
                    n = n_items_on(pe)

                    def gather(item_no):
                        pe.wait_ge(onehot_ready, item_no + 1)
                        for g in range(2):
                            for j in range(4):
                                for t in range(TT):
                                    col = (4 * g + j) * P
                                    last = nc.tensor.matmul(bank[X[g]][:, j * P:(j + 1) * P], hn[:, t, col:col + P],
                                                            onehot[:, t, :], start=t == 0, stop=t == TT - 1)
                            last.then_inc(gathered, 1)

                    for primed in (hT_done, scattered):
                        pe.sem_inc(primed, PRIMED)
                    gather(0)
                    with pe.Fori(0, n) as i:
                        base = PER_ITEM * i

                        def project(k, b0):
                            for q in range(2):
                                c = C_MOE + k + q
                                chunk_here(c, base)
                                if k == 0:
                                    pe.wait_ge(xT_lo_ready, 2 * i + (q + 1))
                                for j in range(4):
                                    kt = 4 * q + j
                                    last = mm3(bank[b0][:, :], (xT_hi[:, kt, :], xT_lo[:, kt, :]),
                                               weights(c, j, 0, HALF, HALF), kt == 0, kt == KD - 1)
                                last.then_inc(chunk_used, 1)

                        def transposes(b):
                            pe.wait_ge(hid2_ready, FB * i + (b + 1) + PRIMED)
                            pe.wait_ge(hT_lo_ready, FB * i + b + PRIMED)
                            if b == 1:
                                pe.wait_ge(onehotT_ready, i + 1)
                            for j in range(4):
                                last = nc.tensor.transpose(bank[T_][:, j * P:(j + 1) * P],
                                                           hid2[:, b % 2, j * P:(j + 1) * P], ident[:])
                            last.then_inc(hT_done, 1)

                        def down(k, b, q):
                            c = C_MOE + k
                            chunk_here(c, base)
                            pe.wait_ge(hT_lo_ready, FB * i + (b + 1) + PRIMED)
                            for j in range(2):
                                kt = 2 * q + j
                                a = (hT_hi[:, b % 2, kt, :], hT_lo[:, b % 2, kt, :])
                                for g in range(2):
                                    last = mm3(bank[Y[g]][:, :], a, weights(c, j, g * HALF, (g + 1) * HALF, D),
                                               b == 0 and kt == 0, b == FB - 1 and kt == 3)
                            last.then_inc(chunk_used, 1)

                        for b in range(FB):
                            k0 = 0 if b == 0 else 6 * b - 2
                            pe.wait_ge(silu2_ready, FB * i + at_most(b - 1) + PRIMED)
                            project(k0, G[b % 2])
                            if b:
                                transposes(b - 1)
                            pe.wait_ge(hid2_ready, FB * i + b + PRIMED)
                            project(k0 + 2, U_)
                            if b == 1:
                                pe.wait_ge(hT_lo_ready, FB * i + 1 + PRIMED)
                                for t in range(TT):
                                    last = nc.tensor.transpose(bank[T_][:, t * P:(t + 1) * P], onehot[:, t, :], ident[:])
                                last.then_inc(onehotT_done, 1)
                                pe.wait_ge(y_lo_ready, 2 * i + PRIMED)
                            if b:
                                down(k0 + 4, b - 1, 0)
                                if b == FB - 1:
                                    transposes(b)
                                down(k0 + 5, b - 1, 1)
                        pe.wait_ge(combined, 4 * i + PRIMED)
                        gather(i + 1)
                        down(PER_ITEM - 2, FB - 1, 0)
                        down(PER_ITEM - 1, FB - 1, 1)
                        for g in range(2):
                            pe.wait_ge(y_lo_ready, 2 * i + (g + 1) + PRIMED)
                            for t in range(TT):
                                if g == 0:
                                    pe.wait_ge(xT_lo_ready, 2 * i + 4)
                                else:
                                    pe.wait_ge(combined, 4 * i + (t + 1) + PRIMED)
                                part = slice(g * HALF, (g + 1) * HALF)
                                a = onehotT[:, t * P:(t + 1) * P]
                                nc.tensor.matmul(bank[X[t]][:, :], a, y_hi[:, part], start=True, stop=False)
                                nc.tensor.matmul(bank[X[t]][:, :], a, y_lo[:, part], start=False, stop=True
                                                 ).then_inc(scattered, 1)



_INS = ["x", "positions", "mix_norm", "ffn_norm", "final_norm", "mla_w_in", "mla_q_norm", "mla_w_q_up",
        "mla_kv_norm", "mla_w_kv_up", "mla_w_o", "hgrn_w_in", "hgrn_lower_bounds", "hgrn_out_norm",
        "hgrn_w_o", "ffn_w_gate", "ffn_w_up", "ffn_w_down", "moe_router", "moe_w_gate", "moe_w_up",
        "moe_w_down"]


def kernel(**inputs):
    import concourse.bacc as bacc
    from concourse.bass_utils import run_bass_kernel_spmd

    nc = bacc.Bacc("TRN2", target_bir_lowering=False, num_devices=1)
    arrays, w = {}, {}
    for name in _INS:
        a = np.ascontiguousarray(inputs[name])
        arrays[f"in_{name}"] = a
        w[name] = nc.dram_tensor(f"in_{name}", a.shape, mybir.dt.from_np(a.dtype), kind="ExternalInput").ap()
    out = nc.dram_tensor("out", (1, SEQ, D), F32, kind="ExternalOutput").ap()
    trunk(nc, w, out)
    r = run_bass_kernel_spmd(nc, [arrays], core_ids=[0])
    return r.results[0]["out"]
```

```python
from contextlib import ExitStack

import numpy as np
import concourse.bass as bass
from concourse import mybir

F32 = mybir.dt.float32
F32R = mybir.dt.float32r
I32 = mybir.dt.int32
U32 = mybir.dt.uint32
ALU = mybir.AluOpType
ACT = mybir.ActivationFunctionType
AX = mybir.AxisListType

P = 128
D = 1024
SEQ = 256
TT = SEQ // P
KD = D // P
HALF = 512
EPS = 1e-6
HEADS, NOPE, ROPE, VD = 16, 64, 32, 64
QL, KVL = 384, 256
MLA_IN = QL + KVL + ROPE
QD = NOPE + ROPE
ROPE_THETA = 10000.0
HG, DK, CH = 8, 128, 64
NCH = SEQ // CH
FF = 3584
FB = FF // HALF
E = 8
RAW, SPLIT, CW = 6, 3, 2048
AHEAD = 2
NEG = -1e30

N_IN, N_QUP, N_KVUP, N_O = 3, 3, 2, 4
IN_ROWS = ((0, 2), (2, 5), (5, 8))
C_IN = 0
C_QUP = C_IN + N_IN
C_KVUP = C_QUP + N_QUP
C_O = C_KVUP + N_KVUP
C_FFN = C_O + N_O
C_DOWN = C_FFN + 4 * FB
C_HG = C_DOWN + 2 * FB
C_HGO = C_HG + 16
C_MOE = C_HGO + 4
PER_ITEM = 6 * FB
MAX_EXTRA = 3
MAX_ITEMS = E + MAX_EXTRA


def dense_chunks(w):
    def rows(m, k0, k1, n0=0, n1=None):
        v = m[k0 * P:k1 * P, :].rearrange("(k p) n -> p k n", p=P)
        return v[:, :, n0:(n1 if n1 is not None else m.shape[1])]
    out = [rows(w["mla_w_in"][0], k0, k1) for k0, k1 in IN_ROWS]
    out += [rows(w["mla_w_q_up"][0], k, k + 1) for k in range(3)]
    out += [rows(w["mla_w_kv_up"][0], k, k + 1) for k in range(2)]
    out += [rows(w["mla_w_o"][0], 2 * k, 2 * k + 2) for k in range(4)]
    for b in range(FB):
        for m in ("ffn_w_gate", "ffn_w_up"):
            out += [rows(w[m][0], 4 * q, 4 * q + 4, b * HALF, (b + 1) * HALF) for q in range(2)]
    out += [rows(w["ffn_w_down"][0], 2 * k, 2 * k + 2) for k in range(2 * FB)]
    for b in (2, 3, 0, 1, 4, 5, 6, 7):
        out += [rows(w["hgrn_w_in"][0], 4 * q, 4 * q + 4, b * HALF, (b + 1) * HALF) for q in range(2)]
    out += [rows(w["hgrn_w_o"][0], 2 * k, 2 * k + 2) for k in range(4)]
    assert len(out) == C_MOE
    return out


def item_chunks():
    out = []
    for b in range(FB):
        out += [("gate", b, 0), ("gate", b, 1), ("up", b, 0), ("up", b, 1)]
        if b:
            out += [("down", b - 1, 0), ("down", b - 1, 1)]
    out += [("down", FB - 1, 0), ("down", FB - 1, 1)]
    assert len(out) == PER_ITEM
    return out


def at_most(x, low=0):
    return x if x > low else low


def trunk(nc, w, out):
    ctx = ExitStack()

    def sb(name, shape, dt=F32, where=None):
        return (where or ctx).enter_context(nc.sbuf_tensor(name, shape, dt))

    def sem(name):
        return ctx.enter_context(nc.semaphore(name))

    with ctx:
        w_raw = sb("w_raw", [P, RAW, CW])
        w_hi = sb("w_hi", [P, SPLIT, CW], F32R)
        w_lo = sb("w_lo", [P, SPLIT, CW], F32R)
        h = sb("h", [P, TT, D])
        hn = sb("hn", [P, TT, D])
        hnT_hi = sb("hnT_hi", [P, KD, SEQ], F32R)
        hnT_lo = sb("hnT_lo", [P, KD, SEQ], F32R)
        gain = sb("gain", [P, 2, D])
        ident = sb("ident", [P, P])
        ss = sb("ss", [P, 2 * TT])
        rms = sb("rms", [P, 2 * TT])
        warm = sb("warm", [P, 2])
        rt_raw = sb("rt_raw", [P, KD, E])
        rt_hi = sb("rt_hi", [P, KD, E], F32R)
        rt_lo = sb("rt_lo", [P, KD, E], F32R)
        rstd = sb("rstd", [P, 2 * TT])
        bank = [ctx.enter_context(nc.psum_tensor(f"bank{i}", [P, HALF], F32)) for i in range(8)]

        raw_loaded = [sem(f"raw_loaded{i}") for i in range(RAW)]
        hi_ready, lo_ready, chunk_used = sem("hi_ready"), sem("lo_ready"), sem("chunk_used")
        hi_quarter = sem("hi_quarter")
        x_loaded = [sem("x_loaded0"), sem("x_loaded1")]
        rt_loaded, rt_hi_ready, rt_lo_ready = sem("rt_loaded"), sem("rt_hi_ready"), sem("rt_lo_ready")
        gain_loaded = [sem("gain_loaded0"), sem("gain_loaded1")]
        sq_done = sem("sq_done")
        ms_ready = sem("ms_ready")
        rms_ready = sem("rms_ready")
        hn_ready = sem("hn_ready")
        nT_done = sem("nT_done")
        nT_hi_ready = sem("nT_hi_ready")
        nT_lo_ready = sem("nT_lo_ready")
        h_added = sem("h_added")
        const_ready = sem("const_ready")
        out_done = sem("out_done")
        dve_step = sem("dve_step")
        act_step = sem("act_step")
        pool_step = sem("pool_step")
        steps = {"dve": 0, "act": 0, "pool": 0}

        def dve_link(ins):
            steps["dve"] += 1
            ins.then_inc(dve_step, 1)
            nc.vector.wait_ge(dve_step, steps["dve"])

        def act_link(ins):
            steps["act"] += 1
            ins.then_inc(act_step, 1)
            nc.scalar.wait_ge(act_step, steps["act"])

        def pool_link(ins):
            steps["pool"] += 1
            ins.then_inc(pool_step, 1)
            nc.gpsimd.wait_ge(pool_step, steps["pool"])

        block = ctx.enter_context(nc.Block())
        chunks = dense_chunks(w)
        item = item_chunks()
        C_END = C_MOE + AHEAD + 1

        def load_chunk(c, dram=None):
            src = chunks[c] if dram is None else dram
            if c >= RAW:
                nc.sync.wait_ge(lo_ready, c - RAW + 1)
            k, n = src.shape[1], src.shape[2]
            dst = w_raw[:, c % RAW, 0:k * n].rearrange("p (k n) -> p k n", k=k)
            nc.sync.dma_start(dst, src).then_inc(raw_loaded[c % RAW], 16)

        def width(c):
            return chunks[c].shape[1] * chunks[c].shape[2] if c < C_MOE else CW

        def split_hi(c, base=0, turn=0):
            n = width(c)
            nc.scalar.wait_ge(raw_loaded[c % RAW], turn + 16 * (c // RAW + 1))
            if c >= SPLIT:
                nc.scalar.wait_ge(chunk_used, base + (c - SPLIT + 1))
            nc.scalar.activation(w_hi[:, c % SPLIT, 0:n], w_raw[:, c % RAW, 0:n],
                                 ACT.Copy).then_inc(hi_ready, 1)

        def split_lo(c, base=0):
            n = width(c)
            nc.vector.wait_ge(hi_ready, base + (c + 1))
            nc.vector.tensor_tensor(w_lo[:, c % SPLIT, 0:n], w_raw[:, c % RAW, 0:n],
                                    w_hi[:, c % SPLIT, 0:n].bitcast(F32),
                                    ALU.subtract).then_inc(lo_ready, 1)

        def split_hi_quarter(c, j):
            nc.scalar.wait_ge(raw_loaded[c % RAW], 16 * (c // RAW + 1))
            nc.scalar.wait_ge(chunk_used, c - SPLIT + 1)
            n = width(c) // 4
            part = slice(j * n, (j + 1) * n)
            nc.scalar.activation(w_hi[:, c % SPLIT, part], w_raw[:, c % RAW, part], ACT.Copy
                                 ).then_inc(hi_ready if j == 3 else hi_quarter, 1)

        def split_lo_quarter(c, j, quarters):
            if j == 3:
                nc.vector.wait_ge(hi_ready, c + 1)
            else:
                nc.vector.wait_ge(hi_quarter, quarters)
            n = width(c) // 4
            part = slice(j * n, (j + 1) * n)
            last = nc.vector.tensor_tensor(w_lo[:, c % SPLIT, part], w_raw[:, c % RAW, part],
                                           w_hi[:, c % SPLIT, part].bitcast(F32), ALU.subtract)
            if j == 3:
                last.then_inc(lo_ready, 1)

        def chunk_here(c, base=0):
            nc.tensor.wait_ge(lo_ready, base + (c + 1))

        def weights(c, k, n0, n1, n):
            return w_hi[:, c % SPLIT, k * n + n0:k * n + n1], w_lo[:, c % SPLIT, k * n + n0:k * n + n1]

        def mm3(o, a, b, start, stop):
            nc.tensor.matmul(o, a[0], b[0], start=start, stop=False)
            nc.tensor.matmul(o, a[0], b[1], start=False, stop=False)
            return nc.tensor.matmul(o, a[1], b[0], start=False, stop=stop)

        def tok(a, k, t):
            return a[0][:, k, t * P:(t + 1) * P], a[1][:, k, t * P:(t + 1) * P]

        hnT = (hnT_hi, hnT_lo)

        def item_dram(k, e):
            kind, b, q = item[k]
            m = w["moe_w_" + kind]
            m = m[0, bass.ds(e, 1)].rearrange("e a n -> (e a) n")
            if kind == "down":
                r = (4 * b + 2 * q) * P
                return m[r:r + 2 * P, :].rearrange("(k p) n -> p k n", p=P)
            return m[4 * q * P:(4 * q + 4) * P, b * HALF:(b + 1) * HALF].rearrange("(k p) n -> p k n", p=P)

        def rng(lo, hi):
            return range(lo, hi)

        def warm_sqrt():
            nc.scalar.activation(warm[:, 1:2], warm[:, 0:1], ACT.Sqrt)

        def norm_act(k, t):
            if k == 0:
                nc.scalar.wait_ge(x_loaded[t], 16)
            elif k < 4:
                nc.scalar.wait_ge(h_added, 4 * (k - 1) + 2 * (t + 1))
            nc.scalar.activation(hn[:, t, :], h[:, t, :], ACT.Square,
                                 accum_out=ss[:, t:t + 1]).then_inc(sq_done, 1)
            nc.scalar.wait_ge(ms_ready, TT * k + t + 1)
            nc.scalar.activation(rms[:, t:t + 1], ss[:, t:t + 1], ACT.Sqrt).then_inc(rms_ready, 1)

        def norm_and_transpose_act(k, b0):
            for t in range(TT):
                norm_act(k, t)
                transpose_act(k, b0, t)

        def norm_dve(k, t):
            nc.vector.wait_ge(sq_done, TT * k + t + 1)
            nc.vector.tensor_scalar(ss[:, t:t + 1], ss[:, t:t + 1], 1.0 / D, EPS, ALU.mult,
                                    ALU.add).then_inc(ms_ready, 1)
            nc.vector.wait_ge(rms_ready, TT * k + t + 1)
            dve_link(nc.vector.reciprocal(rstd[:, t:t + 1], rms[:, t:t + 1]))
            nc.vector.wait_ge(gain_loaded[k % 2], 16 * (k // 2 + 1))
            nc.vector.scalar_tensor_tensor(hn[:, t, :], h[:, t, :], rstd[:, t:t + 1],
                                           gain[:, k % 2, :], ALU.mult, ALU.mult).then_inc(hn_ready, 1)

        def transpose_pe(k, b0, t):
            nc.tensor.wait_ge(hn_ready, TT * k + t + 1)
            for g in range(2):
                for j in range(4):
                    col = (4 * g + j) * P
                    last = nc.tensor.transpose(bank[b0 + 2 * t + g][:, j * P:(j + 1) * P],
                                               hn[:, t, col:col + P], ident[:])
                last.then_inc(nT_done, 1)

        def bank4(b):
            return bank[b][:, :].rearrange("p (j s) -> p j s", j=4)

        def transpose_act(k, b0, t):
            for g in range(2):
                nc.scalar.wait_ge(nT_done, 4 * k + 2 * t + g + 1)
                nc.scalar.activation(hnT_hi[:, 4 * g:4 * g + 4, t * P:(t + 1) * P],
                                     bank4(b0 + 2 * t + g), ACT.Copy).then_inc(nT_hi_ready, 1)

        def transpose_dve(k, b0, t):
            for g in range(2):
                nc.vector.wait_ge(nT_hi_ready, 4 * k + 2 * t + g + 1)
                nc.vector.tensor_tensor(hnT_lo[:, 4 * g:4 * g + 4, t * P:(t + 1) * P],
                                        bank4(b0 + 2 * t + g),
                                        hnT_hi[:, 4 * g:4 * g + 4, t * P:(t + 1) * P].bitcast(F32),
                                        ALU.subtract).then_inc(nT_lo_ready, 1)

        def transposed(k, t, g):
            nc.tensor.wait_ge(nT_lo_ready, 4 * k + 2 * t + g + 1)

        def out_proj_pe(c0, n_chunks, src, b0, before=None, between=None):
            def products(q, t):
                if before:
                    before(q, t)
                for k in range(2):
                    kt = 2 * q + k
                    for n in range(2):
                        last = mm3(bank[b0 + 2 * t + n][:, :], tok(src, kt, t),
                                   weights(c0 + q, k, n * HALF, (n + 1) * HALF, D),
                                   kt == 0, kt == 2 * n_chunks - 1)
                return last

            for q in range(n_chunks - 2):
                chunk_here(c0 + q)
                for t in range(TT):
                    last = products(q, t)
                last.then_inc(chunk_used, 1)
                if between:
                    between(q)
            for t in range(TT):
                for q in (n_chunks - 2, n_chunks - 1):
                    if t == 0:
                        chunk_here(c0 + q)
                    last = products(q, t)
                    if t == TT - 1:
                        last.then_inc(chunk_used, 1)
                if t == 0:
                    last.then_inc(out_done, 1)

        def residual_dve(stage, t, c_last, b0):
            if t == 0:
                nc.vector.wait_ge(out_done, stage + 1)
            else:
                nc.vector.wait_ge(chunk_used, c_last + 1)
            for n in range(2):
                part = h[:, t, n * HALF:(n + 1) * HALF]
                nc.vector.tensor_tensor(part, part, bank[b0 + 2 * t + n][:, :],
                                        ALU.add).then_inc(h_added, 1)

        def residual_and_norm_dve(stage, c_last, b0, bT):
            for t in range(TT):
                residual_dve(stage, t, c_last, b0)
                if t:
                    transpose_dve(stage + 1, bT, t - 1)
                norm_dve(stage + 1, t)
            transpose_dve(stage + 1, bT, TT - 1)

        def load_gain(k, name, row):
            src = w[name]
            src = src[row:row + 1, :] if row is not None else src.rearrange("(a n) -> a n", a=1)
            if k >= 2:
                nc.scalar.wait_ge(hn_ready, TT * (k - 1))
            nc.scalar.dma_start(gain[:, k % 2, :], src.broadcast_to([P, D])).then_inc(gain_loaded[k % 2], 16)

        ph = ExitStack()
        with ph:
            qg = sb("qg", [P, QL], where=ph)
            kvg = sb("kvg", [P, KVL], where=ph)
            pos_i = sb("pos_i", [P, TT], I32, where=ph)
            posf = sb("posf", [P, TT], where=ph)
            freq = sb("freq", [P, ROPE // 2], where=ph)
            ang = sb("ang", [P, TT, ROPE // 2], where=ph)
            turns = sb("turns", [P, TT, ROPE // 2], where=ph)
            absr = sb("absr", [P, TT, ROPE // 2], where=ph)
            cos = sb("cos", [P, TT, ROPE // 2], where=ph)
            sin = sb("sin", [P, TT, ROPE // 2], where=ph)
            halfpi = sb("halfpi", [P, 1], where=ph)
            mask = sb("mask", [P, 3 * P], where=ph)
            cqv = sb("cqv", [P, TT, MLA_IN], where=ph)
            krp = sb("krp", [P, TT, QD], where=ph)
            krT = sb("krT", [P, SEQ], where=ph)
            cT_hi = sb("cT_hi", [P, 5, SEQ], F32R, where=ph)
            cT_lo = sb("cT_lo", [P, 5, SEQ], F32R, where=ph)
            q_sb = sb("q_sb", [P, TT, HEADS * QD], where=ph)
            qT = sb("qT", [QD, HEADS, SEQ], where=ph)
            kT = sb("kT", [QD, HEADS, SEQ], where=ph)
            rt = sb("rt", [P, 4, HEADS * ROPE // 2], where=ph)
            nmax = sb("nmax", [P, 4, TT], where=ph)
            psum_ = sb("prob_sum", [P, 4, TT], where=ph)
            prcp = sb("prcp", [P, 4, TT], where=ph)
            v_sb = hn
            PB, PT = 4, 3
            SB = (0, 1, 6)
            SPLIT_AT = 2
            CT = ((0, 2, 0), (2, 1, 1), (3, 2, 6))
            prob3 = cqv[:, :, :].rearrange("p t n -> p (t n)")

            def prob(i, n0, n1):
                j = i % PB
                return prob3[:, j * 3 * P + n0:j * 3 * P + n1] if j < 3 else q_sb[:, 0, n0:n1]

            probT = q_sb[:, 1, 0:PT * 3 * P].rearrange("p (a n) -> p a n", a=PT)

            small_loaded = sem("small_loaded")
            rope_ready = sem("rope_ready")
            trig_ready = sem("trig_ready")
            red_ready = sem("red_ready")
            cq_squared = sem("cq_squared")
            krp_ready = sem("krp_ready")
            krT_done = sem("krT_done")
            cq_ms = sem("cq_ms")
            cq_rms = sem("cq_rms")
            rc_ready = sem("rc_ready")
            cq_done = sem("cq_done")
            q_done = sem("q_done")
            cn_ready = sem("cn_ready")
            cT_done = sem("cT_done")
            cT_hi_ready = sem("cT_hi_ready")
            cT_lo_ready = sem("cT_lo_ready")
            krT_ready = sem("krT_ready")
            kr_spread = sem("kr_spread")
            q_copied = sem("q_copied")
            q_roped = sem("q_roped")
            kn_done = sem("kn_done")
            kn_copied = sem("kn_copied")
            v_done = sem("v_done")
            v_copied = sem("v_copied")
            qT_done = sem("qT_done")
            qT_copied = sem("qT_copied")
            score_done = sem("score_done")
            masked = sem("masked")
            max_ready = sem("max_ready")
            exp_done = sem("exp_done")
            prob_ready = sem("prob_ready")
            probT_done = sem("probT_done")
            probT_copied = sem("probT_copied")
            pv_done = sem("pv_done")
            oT_hi_ready = sem("oT_hi_ready")
            oT_lo_ready = sem("oT_lo_ready")

            @block.sync
            def _(sp):
                for t in range(TT):
                    nc.sync.dma_start(h[:, t, :], w["x"][0, t * P:(t + 1) * P, :]).then_inc(x_loaded[t], 16)
                load_chunk(0)
                load_chunk(1)
                nc.sync.dma_start(pos_i[:], w["positions"].rearrange("b (t p) -> p (b t)", p=P),
                                  allow_slow_non_contiguous=True).then_inc(small_loaded, 16)
                nc.sync.dma_start(qg[:], w["mla_q_norm"].broadcast_to([P, QL])).then_inc(small_loaded, 16)
                nc.sync.dma_start(kvg[:], w["mla_kv_norm"].broadcast_to([P, KVL])).then_inc(small_loaded, 16)
                for c in range(2, RAW):
                    load_chunk(c)
                nc.sync.dma_start(rt_raw[:], w["moe_router"][0].rearrange("(k p) e -> p k e", p=P)
                                  ).then_inc(rt_loaded, 16)
                for c in range(RAW, C_FFN + RAW + AHEAD + 1):
                    load_chunk(c)

            @block.gpsimd
            def _(pool):
                nc.gpsimd.memset(warm[:], 1.0).then_inc(const_ready, 1)
                pool_link(nc.gpsimd.memset(ident[:], 0.0))
                nc.gpsimd.affine_select(out=ident[:], in_=ident[:], compare_op=ALU.not_equal, fill=1.0,
                                        base=0, pattern=[[-1, P]], channel_multiplier=1
                                        ).then_inc(const_ready, 1)
                inv = ROPE_THETA ** (-np.arange(0, ROPE, 2, dtype=np.float32) / np.float32(ROPE))
                for j in range(ROPE // 2):
                    nc.gpsimd.memset(freq[:, j:j + 1], float(np.float32(inv[j])))
                nc.gpsimd.memset(halfpi[:], float(np.pi / 2))
                nc.gpsimd.memset(krp[:], 0.0).then_inc(const_ready, 1)
                pool_link(nc.gpsimd.memset(mask[:], 0.0))
                for b in (0, 2):
                    nc.gpsimd.affine_select(out=mask[:, b * P:(b + 1) * P], in_=mask[:, b * P:(b + 1) * P],
                                            compare_op=ALU.is_ge, fill=NEG, base=0, pattern=[[-1, P]],
                                            channel_multiplier=1).then_inc(const_ready, 1)
                nc.gpsimd.wait_ge(const_ready, 5)
                nc.gpsimd.wait_ge(krT_ready, 1)
                nc.gpsimd.tensor_copy(kT[NOPE:QD, :, :],
                                      krT[NOPE:QD, :].unsqueeze(1).broadcast_to([ROPE, HEADS, SEQ])
                                      ).then_inc(kr_spread, 1)

            @block.scalar
            def _(act):
                load_gain(0, "mix_norm", 0)
                act.wait_ge(const_ready, 1)
                warm_sqrt()
                for t in range(TT):
                    norm_act(0, t)
                split_hi(0)
                for t in range(TT):
                    transpose_act(0, 0, t)
                for c in rng(1, 3):
                    split_hi(c)
                load_gain(1, "ffn_norm", 0)
                act.wait_ge(red_ready, 1)
                nc.scalar.activation(sin[:], turns[:], ACT.Sin).then_inc(trig_ready, 1)
                act_link(nc.scalar.activation(absr[:], turns[:], ACT.Abs))
                act.wait_ge(const_ready, 3)
                nc.scalar.activation(cos[:], absr[:], ACT.Sin, bias=halfpi[:], scale=-1.0
                                     ).then_inc(trig_ready, 1)
                warm_sqrt()
                for c in rng(3, 5):
                    split_hi(c)
                for t in range(TT):
                    act.wait_ge(cn_ready, t + 1)
                    nc.scalar.activation(q_sb[:, t, 0:QL], bank[4 + t][:, 0:QL], ACT.Square,
                                         accum_out=ss[:, 2 * t:2 * t + 1]).then_inc(cq_squared, 1)

                def cT_act(b):
                    act.wait_ge(cT_done, b + 1)
                    k0, n, bk = CT[b]
                    nc.scalar.activation(cT_hi[:, k0:k0 + n, :],
                                         bank[bk][:, 0:n * SEQ].rearrange("p (j s) -> p j s", j=n),
                                         ACT.Copy).then_inc(cT_hi_ready, 1)

                cT_act(0)
                cT_act(1)
                act.wait_ge(chunk_used, C_IN + N_IN)
                for t in range(TT):
                    nc.scalar.activation(q_sb[:, t, QL:QL + KVL], bank[6 + t][:, 0:KVL], ACT.Square,
                                         accum_out=ss[:, 2 * t + 1:2 * t + 2]).then_inc(cq_squared, 1)
                act.wait_ge(cq_ms, 1)
                nc.scalar.activation(rms[:], ss[:], ACT.Sqrt).then_inc(cq_rms, 1)
                split_hi(5)
                split_hi(6)
                cT_act(2)
                act.wait_ge(krT_done, 1)
                nc.scalar.activation(krT[NOPE:QD, :], bank[7][NOPE:QD, 0:SEQ], ACT.Copy
                                     ).then_inc(krT_ready, 1)
                split_hi(7)
                act.wait_ge(q_done, 1)
                act.wait_ge(rc_ready, 1)
                for n in range(3):
                    nc.scalar.activation(q_sb[:, 0, n * HALF:(n + 1) * HALF], bank[2 * n][:, :], ACT.Copy,
                                         scale=rstd[:, 0:1]).then_inc(q_copied, 1)
                for u in range(HEADS // 2):
                    act.wait_ge(kn_done, u + 1)
                    nc.scalar.activation(kT[0:NOPE, 2 * u:2 * u + 2, :],
                                         bank[6 + u % 2][0:NOPE, :].rearrange("p (a s) -> p a s", a=2),
                                         ACT.Copy).then_inc(kn_copied, 1)
                nc.scalar.activation(warm[:, 1:2], warm[:, 0:1], ACT.Exp)
                for g in range(4):
                    if g < 3:
                        act.wait_ge(v_done, g + 1)
                    else:
                        act.wait_ge(chunk_used, C_KVUP + N_KVUP)
                    nc.scalar.activation(v_sb[:, g // 2, (g % 2) * HALF:(g % 2 + 1) * HALF], bank[g][:, :],
                                         ACT.Copy).then_inc(v_copied, 1)

                def qT_act(u):
                    act.wait_ge(qT_done, u + 1)
                    nc.scalar.activation(qT[:, 2 * u:2 * u + 2, :],
                                         bank[4 + u % 2][0:QD, :].rearrange("p (a s) -> p a s", a=2),
                                         ACT.Copy).then_inc(qT_copied, 1)

                def exp_act(i):
                    act.wait_ge(max_ready, i + 1)
                    for t in range(TT):
                        s = prob(i, 0, P) if t == 0 else prob(i, P, 3 * P)
                        nc.scalar.activation(s, s, ACT.Exp, bias=nmax[:, i % PB, t:t + 1],
                                             accum_out=psum_[:, i % PB, t:t + 1]).then_inc(exp_done, 1)

                def probT_act(i):
                    act.wait_ge(probT_done, i + 1)
                    if i >= PT:
                        act.wait_ge(pv_done, i - PT + 1)
                    nc.scalar.activation(probT[:, i % PT, :], bank[2 + i % 2][:, 0:3 * P], ACT.Copy
                                         ).then_inc(probT_copied, 1)

                def o_act(u):
                    act.wait_ge(pv_done, 2 * u + 2)
                    nc.scalar.activation(hnT_hi[:, u, :], bank[4 + u % 2][:, 0:SEQ], ACT.Copy
                                         ).then_inc(oT_hi_ready, 1)

                for u in range(HEADS // 2 - 1):
                    qT_act(u)
                exp_act(0)
                qT_act(HEADS // 2 - 1)
                exp_act(1)
                exp_act(2)
                for i in range(HEADS):
                    probT_act(i)
                    if 0 <= i - SPLIT_AT < 12:
                        split_hi_quarter(C_O + (i - SPLIT_AT) // 4, (i - SPLIT_AT) % 4)
                    if i + 3 < HEADS:
                        exp_act(i + 3)
                    if i % 2 == 0 and i >= 2:
                        o_act(i // 2 - 1)
                o_act(HEADS // 2 - 1)
                split_hi(C_O + 3)
                warm_sqrt()
                split_hi(C_FFN)

            @block.vector
            def _(dve):
                for t in range(TT):
                    norm_dve(0, t)
                split_lo(0)
                for t in range(TT):
                    transpose_dve(0, 0, t)
                for c in rng(1, 3):
                    split_lo(c)
                dve.wait_ge(small_loaded, 48)
                dve_link(nc.vector.tensor_copy(posf[:], pos_i[:]))
                dve.wait_ge(const_ready, 3)
                for t in range(TT):
                    last = nc.vector.tensor_scalar(ang[:, t, :], freq[:], posf[:, t:t + 1], None, ALU.mult)
                dve_link(last)
                magic = 1.5 * 2.0 ** 23
                two_pi = 2 * np.pi
                p1 = 6.28125
                p2 = float(np.float32(np.round((two_pi - p1) * 2 ** 20) / 2 ** 20))
                p3 = float(np.float32(two_pi - p1 - p2))
                dve_link(nc.vector.tensor_scalar(absr[:], ang[:], float(1 / two_pi), magic, ALU.mult, ALU.add))
                dve_link(nc.vector.tensor_scalar(absr[:], absr[:], -magic, None, ALU.add))
                dve_link(nc.vector.scalar_tensor_tensor(turns[:], absr[:], -p1, ang[:], ALU.mult, ALU.add))
                dve_link(nc.vector.scalar_tensor_tensor(ang[:], absr[:], -p2, turns[:], ALU.mult, ALU.add))
                dve_link(nc.vector.scalar_tensor_tensor(turns[:], absr[:], -p3, ang[:], ALU.mult, ALU.add))
                nc.vector.tensor_scalar(turns[:], turns[:], float(np.float32(np.pi)), -float(np.float32(np.pi)),
                                        ALU.min, ALU.max).then_inc(red_ready, 1)
                for c in rng(3, 5):
                    split_lo(c)
                dve.wait_ge(cq_done, 1)
                for t in range(TT):
                    nc.vector.tensor_tensor(cqv[:, t, 0:QL], bank[4 + t][:, 0:QL], qg[:], ALU.mult
                                            ).then_inc(cn_ready, 1)

                def cT_dve(b):
                    dve.wait_ge(cT_hi_ready, b + 1)
                    k0, n, bk = CT[b]
                    nc.vector.tensor_tensor(cT_lo[:, k0:k0 + n, :],
                                            bank[bk][:, 0:n * SEQ].rearrange("p (j s) -> p j s", j=n),
                                            cT_hi[:, k0:k0 + n, :].bitcast(F32), ALU.subtract
                                            ).then_inc(cT_lo_ready, 1)

                cT_dve(0)
                cT_dve(1)
                dve.wait_ge(cq_squared, 2 * TT)
                sv = ss[:, :].rearrange("p (t a) -> p a t", a=2)
                nc.vector.tensor_scalar(sv[:, 0, :], sv[:, 0, :], 1.0 / QL, EPS, ALU.mult, ALU.add)
                nc.vector.tensor_scalar(sv[:, 1, :], sv[:, 1, :], 1.0 / KVL, EPS, ALU.mult, ALU.add
                                        ).then_inc(cq_ms, 1)
                dve.wait_ge(cq_rms, 1)
                nc.vector.reciprocal(rstd[:], rms[:]).then_inc(rc_ready, 1)
                dve.wait_ge(rc_ready, 1)
                for t in range(TT):
                    nc.vector.scalar_tensor_tensor(cqv[:, t, QL:QL + KVL], bank[6 + t][:, 0:KVL],
                                                   rstd[:, 2 * t + 1:2 * t + 2], kvg[:], ALU.mult, ALU.mult
                                                   ).then_inc(cn_ready, 1)
                dve.wait_ge(trig_ready, 2)

                def rotate(dst, src, t, n):
                    hf = ROPE // 2
                    c = cos[:, t, :].unsqueeze(1).broadcast_to([P, n, hf])
                    s = sin[:, t, :].unsqueeze(1).broadcast_to([P, n, hf])
                    x1, x2 = src[:, :, 0:hf], src[:, :, hf:ROPE]
                    tmp = [rt[:, j, 0:n * hf].rearrange("p (a b) -> p a b", a=n) for j in range(4)]
                    nc.vector.tensor_tensor(tmp[0], x1, c, ALU.mult)
                    nc.vector.tensor_tensor(tmp[1], x2, s, ALU.mult)
                    nc.vector.tensor_tensor(tmp[2], x2, c, ALU.mult)
                    dve_link(nc.vector.tensor_tensor(tmp[3], x1, s, ALU.mult))
                    nc.vector.tensor_tensor(dst[:, :, 0:hf], tmp[0], tmp[1], ALU.subtract)
                    return nc.vector.tensor_tensor(dst[:, :, hf:ROPE], tmp[2], tmp[3], ALU.add)

                for t in range(TT):
                    kr = bank[6 + t][:, KVL:KVL + ROPE].rearrange("p (a b) -> p a b", a=1)
                    last = rotate(krp[:, t:t + 1, NOPE:QD], kr, t, 1)
                    if t + 1 < TT:
                        dve_link(last)
                last.then_inc(krp_ready, 1)
                split_lo(5)
                split_lo(6)
                cT_dve(2)
                split_lo(7)
                dve.wait_ge(chunk_used, C_QUP + N_QUP)
                for n in range(3):
                    nc.vector.tensor_scalar(q_sb[:, 1, n * HALF:(n + 1) * HALF], bank[2 * n + 1][:, :],
                                            rstd[:, 2:3], None, ALU.mult).then_inc(q_copied, 1)
                dve.wait_ge(q_copied, 6)
                for t in range(TT):
                    part = q_sb[:, t, :].rearrange("p (a b) -> p a b", a=HEADS)[:, :, NOPE:QD]
                    last = rotate(part, part, t, HEADS)
                    if t + 1 < TT:
                        dve_link(last)
                last.then_inc(q_roped, 1)

                def scores_dve(i):
                    dve.wait_ge(score_done, i + 1)
                    if i == 0:
                        dve.wait_ge(const_ready, 5)
                    if i == 3:
                        dve.wait_ge(qT_done, HEADS // 2)
                    if i >= PB:
                        dve.wait_ge(probT_done, i - PB + 1)
                    nc.vector.scalar_tensor_tensor(prob(i, 0, 3 * P), bank[SB[i % 3]][:, 0:3 * P],
                                                   float(np.float32(QD ** -0.5)), mask[:],
                                                   ALU.mult, ALU.add).then_inc(masked, 1)
                    dve.wait_ge(masked, i + 1)
                    nc.vector.tensor_reduce(nmax[:, i % PB, 0:1], prob(i, 0, P), AX.X, ALU.max, negate=True)
                    nc.vector.tensor_reduce(nmax[:, i % PB, 1:2], prob(i, P, 3 * P), AX.X, ALU.max,
                                            negate=True).then_inc(max_ready, 1)

                def probs_dve(i):
                    dve.wait_ge(exp_done, TT * (i + 1))
                    dve_link(nc.vector.reciprocal(prcp[:, i % PB, :], psum_[:, i % PB, :]))
                    for t in range(TT):
                        s = prob(i, 0, P) if t == 0 else prob(i, P, 3 * P)
                        last = nc.vector.tensor_scalar(s, s, prcp[:, i % PB, t:t + 1], None, ALU.mult)
                    last.then_inc(prob_ready, 1)

                def o_dve(u):
                    dve.wait_ge(oT_hi_ready, u + 1)
                    nc.vector.tensor_tensor(hnT_lo[:, u, :], bank[4 + u % 2][:, 0:SEQ],
                                            hnT_hi[:, u, :].bitcast(F32), ALU.subtract
                                            ).then_inc(oT_lo_ready, 1)

                for i in range(3):
                    scores_dve(i)
                probs_dve(0)
                for i in range(HEADS):
                    if i + 1 < HEADS:
                        probs_dve(i + 1)
                    if i + 3 < HEADS:
                        scores_dve(i + 3)
                    if 0 <= i - SPLIT_AT < 12:
                        c, j = divmod(i - SPLIT_AT, 4)
                        split_lo_quarter(C_O + c, j, 3 * c + j + 1)
                    if i % 2 and i >= 3:
                        o_dve(i // 2 - 1)
                o_dve(HEADS // 2 - 1)
                split_lo(C_O + 3)
                split_lo(C_FFN)
                residual_and_norm_dve(0, C_O + N_O - 1, 0, 4)

            @block.tensor
            def _(pe):
                pe.wait_ge(const_ready, 2)
                transpose_pe(0, 0, 0)
                transpose_pe(0, 0, 1)
                for c, (k0, k1) in enumerate(IN_ROWS):
                    chunk_here(C_IN + c)

                    def latents(t, part):
                        n0, n1 = ((0, QL), (QL, MLA_IN))[part]
                        transposed(0, t, (k1 - 1) // 4)
                        for kt in range(k0, k1):
                            last = mm3(bank[4 + 2 * part + t][:, 0:n1 - n0], tok(hnT, kt, t),
                                       weights(c, kt - k0, n0, n1, MLA_IN), kt == 0, kt == KD - 1)
                        return last

                    if c < N_IN - 1:
                        for t in range(TT):
                            for part in range(2):
                                last = latents(t, part)
                    else:
                        for part in range(2):
                            for t in range(TT):
                                last = latents(t, part)
                            if part == 0:
                                last.then_inc(cq_done, 1)
                    last.then_inc(chunk_used, 1)

                def c_transposes(b):
                    k0, n, bk = CT[b]
                    for j in range(n):
                        for t in range(TT):
                            last = nc.tensor.transpose(bank[bk][:, j * SEQ + t * P:j * SEQ + (t + 1) * P],
                                                       cqv[:, t, (k0 + j) * P:(k0 + j + 1) * P], ident[:])
                    last.then_inc(cT_done, 1)

                pe.wait_ge(cn_ready, TT)
                c_transposes(0)
                c_transposes(1)
                cT = (cT_hi, cT_lo)
                for c in range(N_QUP):
                    chunk_here(C_QUP + c)
                    if c == 0:
                        pe.wait_ge(cT_lo_ready, 2)
                        pe.wait_ge(cq_squared, TT)
                    if c == 2:
                        pe.wait_ge(cn_ready, 2 * TT)
                        pe.wait_ge(krp_ready, 1)
                        c_transposes(2)
                        for t in range(TT):
                            last = nc.tensor.transpose(bank[7][0:QD, t * P:(t + 1) * P], krp[:, t, :], ident[:])
                        last.then_inc(krT_done, 1)
                    for t in range(TT):
                        for n in range(3):
                            last = mm3(bank[2 * n + t][:, :], tok(cT, c, t),
                                       weights(C_QUP + c, 0, n * HALF, (n + 1) * HALF, HEADS * QD),
                                       c == 0, c == N_QUP - 1)
                        if (c, t) == (2, 0):
                            last.then_inc(q_done, 1)
                    last.then_inc(chunk_used, 1)
                chunk_here(C_KVUP + 1)
                pe.wait_ge(cT_lo_ready, 3)
                for u in range(HEADS // 2):
                    if u == 1:
                        pe.wait_ge(krT_ready, 1)
                    if u >= 2:
                        pe.wait_ge(kn_copied, u - 1)
                    for a in range(2):
                        for k in range(N_KVUP):
                            wk = weights(C_KVUP + k, 0, (2 * u + a) * P, (2 * u + a + 1) * P, 0)
                            last = mm3(bank[6 + u % 2][:, a * SEQ:(a + 1) * SEQ], wk,
                                       (cT_hi[:, 3 + k, :], cT_lo[:, 3 + k, :]), k == 0, k == N_KVUP - 1)
                    last.then_inc(kn_done, 1)
                pe.wait_ge(q_copied, 6)
                for t in range(TT):
                    for n in range(2):
                        for k in range(N_KVUP):
                            wv = [x[:, (C_KVUP + k) % SPLIT, n * 1024:(n + 1) * 1024].rearrange(
                                "p (a b) -> p a b", a=8)[:, :, NOPE:NOPE + VD] for x in (w_hi, w_lo)]
                            last = mm3(bank[2 * t + n][:, :].rearrange("p (a b) -> p a b", a=8),
                                       tok(cT, 3 + k, t), wv, k == 0, k == N_KVUP - 1)
                        if (t, n) != (1, 1):
                            last.then_inc(v_done, 1)
                last.then_inc(chunk_used, 2)
                def scores(i):
                    if i >= 3:
                        pe.wait_ge(masked, i - 2)
                    sbank = bank[SB[i % 3]]
                    nc.tensor.matmul(sbank[:, 0:P], qT[:, i, 0:P], kT[:, i, 0:P], start=True, stop=True)
                    nc.tensor.matmul(sbank[:, P:3 * P], qT[:, i, P:SEQ], kT[:, i, :],
                                     start=True, stop=True).then_inc(score_done, 1)

                def prob_transposes(i):
                    pe.wait_ge(prob_ready, i + 1)
                    if i >= 2:
                        pe.wait_ge(probT_copied, i - 1)
                    for j in range(3):
                        last = nc.tensor.transpose(bank[2 + i % 2][:, j * P:(j + 1) * P],
                                                   prob(i, j * P, (j + 1) * P), ident[:])
                    last.then_inc(probT_done, 1)

                def values(i):
                    pe.wait_ge(probT_copied, i + 1)
                    u, r = i // 2, (i % 2) * VD
                    if i % 2 == 0 and u >= 2:
                        pe.wait_ge(oT_lo_ready, u - 1)
                    ob = bank[4 + u % 2]
                    nc.tensor.matmul(ob[r:r + VD, 0:SEQ], v_sb[:, 0, i * VD:(i + 1) * VD],
                                     probT[:, i % PT, 0:SEQ], start=True, stop=False)
                    nc.tensor.matmul(ob[r:r + VD, P:SEQ], v_sb[:, 1, i * VD:(i + 1) * VD],
                                     probT[:, i % PT, SEQ:3 * P], start=False, stop=True).then_inc(pv_done, 1)

                pe.wait_ge(q_roped, 1)
                for u in range(HEADS // 2):
                    if u >= 2:
                        pe.wait_ge(qT_copied, u - 1)
                    for a in range(2):
                        for t in range(TT):
                            col = (2 * u + a) * QD
                            last = nc.tensor.transpose(
                                bank[4 + u % 2][0:QD, a * SEQ + t * P:a * SEQ + (t + 1) * P],
                                q_sb[:, t, col:col + QD], ident[:])
                    last.then_inc(qT_done, 1)
                    if u == HEADS // 2 - 3:
                        pe.wait_ge(kr_spread, 1)
                        pe.wait_ge(kn_copied, HEADS // 2)
                        pe.wait_ge(v_copied, 4)
                    if u >= HEADS // 2 - 3:
                        scores(u - (HEADS // 2 - 3))
                pe.wait_ge(qT_copied, HEADS // 2)
                for i in range(HEADS):
                    prob_transposes(i)
                    if i + 3 < HEADS:
                        scores(i + 3)
                    if i:
                        values(i - 1)
                def o_here(q, t):
                    if (q, t) == (0, 1):
                        values(HEADS - 1)
                    pe.wait_ge(oT_lo_ready, 2 * q + 2)

                pe.wait_ge(masked, HEADS)
                out_proj_pe(C_O, N_O, hnT, 0, o_here)

        ph = ExitStack()
        with ph:
            hidT_hi = sb("hidT_hi", [P, 4 * FB, SEQ], F32R, where=ph)
            hidT_lo = sb("hidT_lo", [P, 4 * FB, SEQ], F32R, where=ph)
            silu = sb("silu", [P, TT, HALF], where=ph)
            hid = sb("hid", [P, TT, HALF], where=ph)
            silu_ready = sem("silu_ready")
            hid_ready = sem("hid_ready")
            hidT_done = sem("hidT_done")
            hidT_hi_ready = sem("hidT_hi_ready")
            hidT_lo_ready = sem("hidT_lo_ready")

            @block.sync
            def _(sp):
                for c in range(C_FFN + RAW + AHEAD + 1, C_HG + RAW + AHEAD + 1):
                    load_chunk(c)

            @block.scalar
            def _(act):
                load_gain(2, "mix_norm", 1)
                norm_and_transpose_act(1, 4)
                act.wait_ge(rt_loaded, 16)
                nc.scalar.activation(rt_hi[:], rt_raw[:], ACT.Copy).then_inc(rt_hi_ready, 1)
                for c in rng(C_FFN + 1, C_FFN + 3):
                    split_hi(c)

                def silu_act(b):
                    act.wait_ge(chunk_used, C_FFN + 4 * b + 2)
                    if b:
                        act.wait_ge(hid_ready, TT * b)
                    for t in range(TT):
                        nc.scalar.activation(silu[:, t, :], bank[t][:, :], ACT.Silu).then_inc(silu_ready, 1)

                def hid_act(b):
                    for t in range(TT):
                        act.wait_ge(hidT_done, TT * b + t + 1)
                        nc.scalar.activation(hidT_hi[:, 4 * b:4 * b + 4, t * P:(t + 1) * P], bank4(4 + t),
                                             ACT.Copy).then_inc(hidT_hi_ready, 1)

                for b in range(FB):
                    split_hi(C_FFN + 4 * b + 3)
                    silu_act(b)
                    if b:
                        hid_act(b - 1)
                    for c in range(4, 7):
                        split_hi(C_FFN + 4 * b + c)
                hid_act(FB - 1)
                for c in range(C_DOWN + 3, C_HG):
                    split_hi(c)
                warm_sqrt()
                split_hi(C_HG)

            @block.vector
            def _(dve):
                for c in rng(C_FFN + 1, C_FFN + 3):
                    split_lo(c)
                dve.wait_ge(rt_hi_ready, 1)
                nc.vector.tensor_tensor(rt_lo[:], rt_raw[:], rt_hi[:].bitcast(F32), ALU.subtract
                                        ).then_inc(rt_lo_ready, 1)

                def hid_dve(b):
                    for t in range(TT):
                        dve.wait_ge(silu_ready, TT * b + t + 1)
                        dve.wait_ge(chunk_used, C_FFN + 4 * b + 4)
                        if b:
                            dve.wait_ge(hidT_done, TT * (b - 1) + t + 1)
                        nc.vector.tensor_tensor(hid[:, t, :], silu[:, t, :], bank[2 + t][:, :],
                                                ALU.mult).then_inc(hid_ready, 1)

                def hidT_dve(b):
                    for t in range(TT):
                        dve.wait_ge(hidT_hi_ready, TT * b + t + 1)
                        part = slice(4 * b, 4 * b + 4), slice(t * P, (t + 1) * P)
                        nc.vector.tensor_tensor(hidT_lo[:, part[0], part[1]], bank4(4 + t),
                                                hidT_hi[:, part[0], part[1]].bitcast(F32),
                                                ALU.subtract).then_inc(hidT_lo_ready, 1)

                for b in range(FB):
                    split_lo(C_FFN + 4 * b + 3)
                    if b:
                        hidT_dve(b - 1)
                    split_lo(C_FFN + 4 * b + 4)
                    split_lo(C_FFN + 4 * b + 5)
                    hid_dve(b)
                    split_lo(C_FFN + 4 * b + 6)
                hidT_dve(FB - 1)
                for c in range(C_DOWN + 3, C_HG + 1):
                    split_lo(c)
                residual_and_norm_dve(1, C_HG - 1, 0, 4)

            @block.tensor
            def _(pe):
                transpose_pe(1, 4, 0)

                def stream(c0, b0):
                    for q in range(2):
                        chunk_here(c0 + q)
                        for t in range(TT):
                            if (c0, q, t) == (C_FFN, 0, 1):
                                transpose_pe(1, 4, 1)
                            transposed(1, t, q)
                            for k in range(4):
                                kt = 4 * q + k
                                last = mm3(bank[b0 + t][:, :], tok(hnT, kt, t),
                                           weights(c0 + q, k, 0, HALF, HALF), kt == 0, kt == KD - 1)
                        last.then_inc(chunk_used, 1)

                def transposes(b):
                    for t in range(TT):
                        pe.wait_ge(hid_ready, TT * b + t + 1)
                        if b:
                            pe.wait_ge(hidT_lo_ready, TT * (b - 1) + t + 1)
                        for j in range(4):
                            last = nc.tensor.transpose(bank[4 + t][:, j * P:(j + 1) * P],
                                                       hid[:, t, j * P:(j + 1) * P], ident[:])
                        last.then_inc(hidT_done, 1)

                for b in range(FB):
                    if b:
                        pe.wait_ge(silu_ready, TT * b)
                    stream(C_FFN + 4 * b, 0)
                    if b:
                        transposes(b - 1)
                        pe.wait_ge(hid_ready, TT * b)
                    stream(C_FFN + 4 * b + 2, 2)

                def rows_here(q, t):
                    if q == 0:
                        if t == 0:
                            pe.wait_ge(silu_ready, TT * FB)
                        else:
                            pe.wait_ge(hid_ready, TT * FB)
                    if q % 2 == 0:
                        pe.wait_ge(hidT_lo_ready, TT * (q // 2 + 1))

                out_proj_pe(C_DOWN, 2 * FB, (hidT_hi, hidT_lo), 0, rows_here,
                            lambda q: transposes(FB - 1) if q == 0 else None)

        ph = ExitStack()
        with ph:
            AB = 3
            qd = sb("qd", [P, HG, SEQ], where=ph)
            kf = sb("kf", [P, HG, SEQ], where=ph)
            g1 = sb("g1", [P, HG, SEQ], where=ph)
            g2 = sb("g2", [P, HG, SEQ], where=ph)
            g3 = sb("g3", [P, HG, SEQ], where=ph)
            v = sb("v", [P, TT, D], where=ph)
            sg = sb("sg", [P, TT, D], where=ph)
            att = sb("att", [P, AB, SEQ], where=ph)
            state = sb("state", [P, AB, 3, DK], where=ph)
            amask = sb("amask", [P, SEQ], where=ph)
            half_lo = sb("half_lo", [P, 1], where=ph)
            half_hi = sb("half_hi", [P, 1], where=ph)
            smask = sb("smask", [P, SEQ], where=ph)
            ogain = sb("ogain", [P, DK], where=ph)
            lbs = sb("lbs", [P, 2, HG], where=ph)
            lbt = sb("lbt", [P, 2, HG], where=ph)
            lbm = sb("lbm", [P, HG], where=ph)
            lb = sb("lb", [P, HG], where=ph)
            oml = sb("oml", [P, HG], where=ph)
            dec = sb("dec", [P, HG * SEQ // CH], where=ph)
            oss = sb("oss", [P, HG, TT], where=ph)
            kd_even = kf[:, :, :].rearrange("p a s -> p (a s)").rearrange("p (t n) -> p t n", t=TT)
            kd_odd = g2[:, :, :].rearrange("p a s -> p (a s)").rearrange("p (t n) -> p t n", t=TT)
            o_sb = hn
            NC_ = SEQ // CH

            hg_loaded = sem("hg_loaded")
            hg_const = sem("hg_const")
            k_ready = sem("k_ready")
            sg_ready = sem("sg_ready")
            lbd_ready = sem("lbd_ready")
            lbe_ready = sem("lbe_ready")
            fq_copied = sem("fq_copied")
            vg_copied = sem("vg_copied")
            f_ready = sem("f_ready")
            logf_ready = sem("logf_ready")
            b_ready = sem("b_ready")
            eb_ready = sem("eb_ready")
            qd_ready = sem("qd_ready")
            enb_ready = sem("enb_ready")
            bl_ready = sem("bl_ready")
            ebl_ready = sem("ebl_ready")
            dec_ready = sem("dec_ready")
            kd_ready = sem("kd_ready")
            kdec_ready = sem("kdec_ready")
            kdT_done = sem("kdT_done")
            kdT_copied = sem("kdT_copied")
            a_done = sem("a_done")
            a_ready = sem("a_ready")
            kv_done = sem("kv_done")
            state_ready = sem("state_ready")
            o_done = sem("o_done")
            o_squared = sem("o_squared")
            oms_ready = sem("oms_ready")
            orms_ready = sem("orms_ready")
            on_ready = sem("on_ready")
            ohT_done = sem("ohT_done")
            ohT_hi_ready = sem("ohT_hi_ready")
            ohT_lo_ready = sem("ohT_lo_ready")

            @block.sync
            def _(sp):
                for c in range(C_HG + RAW + AHEAD + 1, C_MOE):
                    load_chunk(c)
                for k in range(RAW + AHEAD + 1):
                    load_chunk(C_MOE + k, item_dram(k, 0))

            @block.gpsimd
            def _(pool):
                pool.wait_ge(h_added, 8)
                for tile, value in ((smask, 1.0), (half_lo, 0.0), (half_hi, 0.0), (att, 0.0), (amask, 1.0)):
                    pool_link(nc.gpsimd.memset(tile[:], value))
                pool_link(nc.gpsimd.memset(smask[:, :].rearrange("p (a b) -> p a b", a=NC_)[:, :, 0:1], 0.0))
                pool_link(nc.gpsimd.memset(half_lo[0:CH, :], 1.0))
                pool_link(nc.gpsimd.memset(half_hi[CH:P, :], 1.0))
                for t in range(TT):
                    part = amask[:, t * P:(t + 1) * P]
                    pool_link(nc.gpsimd.affine_select(out=part, in_=part, compare_op=ALU.is_ge, fill=0.0,
                                                      base=0, pattern=[[1, P]], channel_multiplier=-1))
                    pool_link(nc.gpsimd.memset(amask[0:CH, t * P + CH:(t + 1) * P], 0.0))
                nc.gpsimd.memset(half_lo[0:CH, :], 1.0).then_inc(hg_const, 1)

            @block.scalar
            def _(act):
                load_gain(3, "ffn_norm", 1)
                norm_and_transpose_act(2, 4)
                nc.scalar.dma_start(ogain[:], w["hgrn_out_norm"].broadcast_to([P, DK])).then_inc(hg_loaded, 16)
                for l in range(2):
                    nc.scalar.dma_start(lbs[:, l, :], w["hgrn_lower_bounds"][l:l + 1, :].rearrange(
                        "l (a p) -> p (l a)", p=P), allow_slow_non_contiguous=True).then_inc(hg_loaded, 16)
                for c in rng(C_HG + 1, C_HG + 3):
                    split_hi(c)
                act.wait_ge(lbd_ready, 1)
                nc.scalar.activation(lbs[:], lbt[:], ACT.Exp).then_inc(lbe_ready, 1)

                def evacuate(B):
                    act.wait_ge(chunk_used, C_HG + 2 * B + 2)
                    if B < 4:
                        for a in range(4):
                            dst = (kf if B < 2 else qd)[:, 4 * (B % 2) + a, :]
                            src = bank[4 * (B % 2) + a][:, 0:SEQ]
                            if B < 2:
                                nc.scalar.activation(dst, src, ACT.Sigmoid).then_inc(fq_copied, 1)
                            else:
                                nc.scalar.activation(dst, src, ACT.Copy, scale=float(np.float32(DK ** -0.5))
                                                     ).then_inc(fq_copied, 1)
                    else:
                        n = B % 2
                        for t in range(TT):
                            dst = (v if B < 6 else sg)[:, t, n * HALF:(n + 1) * HALF]
                            src = bank[(0 if B < 6 else 4) + 2 * n + t][:, :]
                            nc.scalar.activation(dst, src, ACT.Copy if B < 6 else ACT.Silu
                                                 ).then_inc(vg_copied, 1)

                for B in range(8):
                    split_hi(C_HG + 2 * B + 3)
                    if B == 2:
                        act.wait_ge(f_ready, 1)
                        nc.scalar.activation(g1[:], kf[:], ACT.Ln).then_inc(logf_ready, 1)
                    if B == 3:
                        act.wait_ge(b_ready, 1)
                        nc.scalar.activation(g1[:], g2[:], ACT.Exp).then_inc(eb_ready, 1)
                    if B == 4:
                        act.wait_ge(bl_ready, 1)
                        nc.scalar.activation(g3[:], g3[:], ACT.Exp).then_inc(ebl_ready, 1)
                        last_b = g2[:, :, :].rearrange("p a s -> p (a s)").rearrange(
                            "p (n c) -> p n c", c=CH)[:, :, CH - 1]
                        nc.scalar.activation(dec[:], last_b, ACT.Exp).then_inc(dec_ready, 1)
                    if B == 5:
                        act.wait_ge(qd_ready, 1)
                        nc.scalar.activation(g1[:], g2[:], ACT.Exp, scale=-1.0).then_inc(enb_ready, 1)
                    if B == 7:
                        act.wait_ge(kd_ready, 1)
                        act.wait_ge(dec_ready, 1)
                        for t in range(TT):
                            for g in range(2):
                                act.wait_ge(kdT_done, 2 * t + g + 1)
                                nc.scalar.activation(kd_even[:, t, g * HALF:(g + 1) * HALF],
                                                     bank[2 * t + g][:, :], ACT.Copy, scale=half_lo[:]
                                                     ).then_inc(kdT_copied, 1)
                                if t == 0:
                                    nc.scalar.activation(kd_odd[:, t, g * HALF:(g + 1) * HALF],
                                                         bank[2 * t + g][:, :], ACT.Copy, scale=half_hi[:]
                                                         ).then_inc(kdT_copied, 1)
                    evacuate(B)
                    if B == 7:
                        warm_sqrt()
                    else:
                        split_hi(C_HG + 2 * B + 4)
                for i in range(HG + 2):
                    if i < HG:
                        act.wait_ge(o_done, i + 1)
                        for t in range(TT):
                            nc.scalar.activation(o_sb[:, t, i * DK:(i + 1) * DK], bank[4 + i % 2][:, t * DK:(t + 1) * DK], ACT.Square,
                                                 accum_out=oss[:, i, t:t + 1]).then_inc(o_squared, 1)
                        act.wait_ge(oms_ready, i + 1)
                        nc.scalar.activation(oss[:, i, :], oss[:, i, :], ACT.Sqrt).then_inc(orms_ready, 1)
                    if HG - 1 <= i < HG + 1:
                        split_hi(C_HGO + 2 + i - (HG - 1))
                    if i >= 2:
                        act.wait_ge(ohT_done, i - 1)
                        nc.scalar.activation(hnT_hi[:, i - 2, :], bank[6 + i % 2][:, 0:SEQ], ACT.Copy
                                             ).then_inc(ohT_hi_ready, 1)
                split_hi(C_MOE)

            @block.vector
            def _(dve):
                dve.wait_ge(hg_loaded, 48)
                dve_link(nc.vector.tensor_tensor(lbm[:], lbs[:, 0, :], lbs[:, 1, :], ALU.max))
                nc.vector.tensor_tensor(lbt[:, 0, :], lbs[:, 0, :], lbm[:], ALU.subtract)
                nc.vector.tensor_tensor(lbt[:, 1, :], lbs[:, 1, :], lbm[:], ALU.subtract).then_inc(lbd_ready, 1)
                dve.wait_ge(lbe_ready, 1)
                dve_link(nc.vector.tensor_tensor(lbm[:], lbs[:, 0, :], lbs[:, 1, :], ALU.add))
                dve_link(nc.vector.reciprocal(lbm[:], lbm[:]))
                nc.vector.tensor_tensor(lbt[:, 0, :], lbs[:, 0, :], lbm[:], ALU.mult)
                dve_link(nc.vector.tensor_tensor(lbt[:, 1, :], lbs[:, 1, :], lbm[:], ALU.mult))
                dve_link(nc.vector.tensor_tensor(lb[:], lbt[:, 0, :], lbt[:, 1, :], ALU.add))
                dve_link(nc.vector.tensor_tensor(lb[:], lb[:], lbt[:, 0, :], ALU.subtract))
                dve_link(nc.vector.tensor_scalar(oml[:], lb[:], -1.0, 1.0, ALU.mult, ALU.add))
                for c in rng(C_HG + 1, C_HG + 3):
                    split_lo(c)
                dve.wait_ge(hg_const, 1)

                def gate_gain(n):
                    for t in range(TT):
                        part = sg[:, t, n * HALF:(n + 1) * HALF].rearrange("p (a n) -> p a n", n=DK)
                        last = nc.vector.tensor_tensor(
                            part, part, ogain[:, :].unsqueeze(1).broadcast_to([P, HALF // DK, DK]), ALU.mult)
                    last.then_inc(sg_ready, 1)

                for B in range(8):
                    split_lo(C_HG + 2 * B + 3)
                    if B == 1:
                        dve.wait_ge(fq_copied, 8)
                        for a in range(HG):
                            last = nc.vector.tensor_scalar(kf[:, a, :], kf[:, a, :], oml[:, a:a + 1],
                                                           lb[:, a:a + 1], ALU.mult, ALU.add)
                        last.then_inc(f_ready, 1)
                    if B == 2:
                        dve.wait_ge(logf_ready, 1)
                        for a in range(HG):
                            last = nc.vector.tensor_tensor_scan(g2[:, a, :], smask[:], g1[:, a, :], 0.0,
                                                                ALU.mult, ALU.add)
                        last.then_inc(b_ready, 1)
                        nc.vector.tensor_scalar(kf[:], kf[:], -1.0, 1.0, ALU.mult, ALU.add
                                                ).then_inc(k_ready, 1)
                    if B == 3:
                        dve.wait_ge(b_ready, 1)
                        bv = g2[:, :, :].rearrange("p a s -> p (a s)").rearrange("p (n c) -> p n c", c=CH)
                        nc.vector.tensor_tensor(
                            g3[:, :, :].rearrange("p a s -> p (a s)").rearrange("p (n c) -> p n c", c=CH),
                            bv[:, :, CH - 1:CH].broadcast_to([P, HG * NC_, CH]), bv, ALU.subtract
                        ).then_inc(bl_ready, 1)
                    if B == 4:
                        dve.wait_ge(eb_ready, 1)
                        dve.wait_ge(fq_copied, 16)
                        nc.vector.tensor_tensor(qd[:], qd[:], g1[:], ALU.mult).then_inc(qd_ready, 1)
                    if B == 5:
                        dve.wait_ge(ebl_ready, 1)
                        dve.wait_ge(k_ready, 1)
                        nc.vector.tensor_tensor(g3[:], kf[:], g3[:], ALU.mult).then_inc(kdec_ready, 1)
                    if B == 6:
                        dve.wait_ge(enb_ready, 1)
                        nc.vector.tensor_tensor(g1[:], kf[:], g1[:], ALU.mult).then_inc(kd_ready, 1)
                    if B == 7:
                        dve.wait_ge(vg_copied, 6)
                        gate_gain(0)
                    else:
                        split_lo(C_HG + 2 * B + 4)

                def scores_dve(i):
                    dve.wait_ge(a_done, i + 1)
                    if i >= AB:
                        dve.wait_ge(o_done, i - AB + 1)
                    nc.vector.copy_predicated(att[:, i % AB, :], amask[:].bitcast(U32),
                                              bank[i % 2][:, 0:SEQ]).then_inc(a_ready, 1)
                    dve.wait_ge(kv_done, i + 1)
                    kv = bank[2 + i % 2]
                    dve_link(nc.vector.tensor_copy(state[:, i % AB, 0, :], kv[:, 0:DK]))
                    dve_link(nc.vector.scalar_tensor_tensor(
                        state[:, i % AB, 1, :], state[:, i % AB, 0, :], dec[:, NC_ * i + 1:NC_ * i + 2],
                        kv[:, DK:2 * DK], ALU.mult, ALU.add))
                    nc.vector.scalar_tensor_tensor(
                        state[:, i % AB, 2, :], state[:, i % AB, 1, :], dec[:, NC_ * i + 2:NC_ * i + 3],
                        kv[:, 2 * DK:3 * DK], ALU.mult, ALU.add).then_inc(state_ready, 1)

                dve.wait_ge(dec_ready, 1)
                scores_dve(0)
                scores_dve(1)
                for i in range(HG + 2):
                    if i < HG:
                        dve.wait_ge(o_squared, TT * (i + 1))
                        nc.vector.tensor_scalar(oss[:, i, :], oss[:, i, :], 1.0 / DK, EPS, ALU.mult, ALU.add
                                                ).then_inc(oms_ready, 1)
                    if i + 2 < HG:
                        scores_dve(i + 2)
                    if i == 2:
                        dve.wait_ge(vg_copied, 8)
                        gate_gain(1)
                    if i < HG:
                        dve.wait_ge(orms_ready, i + 1)
                        dve_link(nc.vector.reciprocal(oss[:, i, :], oss[:, i, :]))
                        dve.wait_ge(sg_ready, i // 4 + 1)
                        hd = slice(i * DK, (i + 1) * DK)
                        for t in range(TT):
                            last = nc.vector.scalar_tensor_tensor(
                                o_sb[:, t, hd], bank[4 + i % 2][:, t * DK:(t + 1) * DK], oss[:, i, t:t + 1],
                                sg[:, t, hd], ALU.mult, ALU.mult)
                        last.then_inc(on_ready, 1)
                    if HG - 1 <= i < HG + 1:
                        split_lo(C_HGO + 2 + i - (HG - 1))
                    if i >= 2:
                        dve.wait_ge(ohT_hi_ready, i - 1)
                        nc.vector.tensor_tensor(hnT_lo[:, i - 2, :], bank[6 + i % 2][:, 0:SEQ],
                                                hnT_hi[:, i - 2, :].bitcast(F32), ALU.subtract
                                                ).then_inc(ohT_lo_ready, 1)
                split_lo(C_MOE)
                residual_and_norm_dve(2, C_MOE - 1, 0, 4)

            @block.tensor
            def _(pe):
                for t in range(TT):
                    transpose_pe(2, 4, t)
                for B in range(8):
                    c0 = C_HG + 2 * B
                    if 2 <= B < 4:
                        pe.wait_ge(fq_copied, 4 * (B - 1))
                    elif 4 <= B < 6:
                        pe.wait_ge(fq_copied, 12)
                    elif B >= 6:
                        pe.wait_ge(fq_copied, 16)
                    if B == 7:
                        pe.wait_ge(kdec_ready, 1)
                        pe.wait_ge(vg_copied, 4)
                        for t in range(TT):
                            for g in range(2):
                                for a in range(4):
                                    last = nc.tensor.transpose(bank[2 * t + g][:, a * P:(a + 1) * P],
                                                               g3[:, 4 * g + a, t * P:(t + 1) * P], ident[:])
                                last.then_inc(kdT_done, 1)
                    for q in range(2):
                        chunk_here(c0 + q)
                        if B == 0:
                            transposed(2, 1, q)
                        for k in range(4):
                            kt = 4 * q + k
                            if B < 4:
                                for a in range(4):
                                    last = mm3(bank[4 * (B % 2) + a][:, 0:SEQ],
                                               weights(c0 + q, k, a * P, (a + 1) * P, HALF),
                                               (hnT_hi[:, kt, :], hnT_lo[:, kt, :]), kt == 0, kt == KD - 1)
                            else:
                                for t in range(TT):
                                    last = mm3(bank[(0 if B < 6 else 4) + 2 * (B % 2) + t][:, :],
                                               tok(hnT, kt, t), weights(c0 + q, k, 0, HALF, HALF),
                                               kt == 0, kt == KD - 1)
                        last.then_inc(chunk_used, 1)
                pe.wait_ge(kdT_copied, 6)
                pe.wait_ge(vg_copied, 8)
                pe.wait_ge(kd_ready, 1)
                pe.wait_ge(qd_ready, 1)

                def head_scores(i):
                    if i >= 2:
                        pe.wait_ge(a_ready, i - 1)
                        pe.wait_ge(state_ready, i - 1)
                    for t in range(TT):
                        last = nc.tensor.matmul(bank[i % 2][:, t * P:(t + 1) * P], g1[:, i, t * P:(t + 1) * P],
                                                qd[:, i, t * P:(t + 1) * P], start=True, stop=True)
                    last.then_inc(a_done, 1)
                    hd = slice(i * DK, (i + 1) * DK)
                    for n, (kd, t) in enumerate(((kd_even, 0), (kd_odd, 0), (kd_even, 1))):
                        last = nc.tensor.matmul(bank[2 + i % 2][:, n * DK:(n + 1) * DK], kd[:, t, hd], v[:, t, hd],
                                                start=True, stop=True)
                    last.then_inc(kv_done, 1)

                def head_output(i):
                    pe.wait_ge(a_ready, i + 1)
                    pe.wait_ge(state_ready, i + 1)
                    if i >= 2:
                        pe.wait_ge(on_ready, i - 1)
                    hd = slice(i * DK, (i + 1) * DK)
                    for t in range(TT):
                        ob = bank[4 + i % 2][:, t * DK:(t + 1) * DK]
                        nc.tensor.matmul(ob, att[:, i % AB, t * P:(t + 1) * P], v[:, t, hd], start=True, stop=True)
                        for half in range(2):
                            n = 2 * t + half
                            if n == 0:
                                continue
                            last = nc.tensor.matmul(ob[half * CH:(half + 1) * CH, :],
                                                    qd[:, i, n * CH:(n + 1) * CH], state[:, i % AB, n - 1, :],
                                                    start=False, stop=True, skip_group_check=True)
                    last.then_inc(o_done, 1)

                def head_transposes(i):
                    pe.wait_ge(on_ready, i + 1)
                    if i >= 2:
                        pe.wait_ge(ohT_lo_ready, i - 1)
                    for t in range(TT):
                        last = nc.tensor.transpose(bank[6 + i % 2][:, t * P:(t + 1) * P],
                                                   o_sb[:, t, i * DK:(i + 1) * DK], ident[:])
                    last.then_inc(ohT_done, 1)

                head_scores(0)
                head_scores(1)
                for i in range(HG):
                    head_output(i)
                    if i + 2 < HG:
                        head_scores(i + 2)
                    if i >= 2:
                        head_transposes(i - 2)
                out_proj_pe(C_HGO, 4, hnT, 0, lambda q, t: pe.wait_ge(ohT_lo_ready, 2 * q + 2),
                            lambda q: head_transposes(HG - 2 + q))

        ph = ExitStack()
        with ph:
            logit = sb("logit", [P, TT, E], where=ph)
            top = sb("top", [P, TT, 8], where=ph)
            topi = sb("topi", [P, TT, 8], U32, where=ph)
            topf = sb("topf", [P, TT, 8], where=ph)
            sel = sb("sel", [P, TT, 2, E], where=ph)
            wts = sb("wts", [P, TT, 4], where=ph)
            gates = sb("gates", [P, TT, E], where=ph)
            chosen = sb("chosen", [P, TT, E], where=ph)
            slot = sb("slot", [P, TT, E], where=ph)
            count = sb("count", [P, E], where=ph)
            over = sb("over", [P, E], where=ph)
            rank = sb("rank", [P, E], where=ph)
            scratch = sb("scratch", [P, E], where=ph)
            iota_e = sb("iota_e", [P, E], where=ph)
            ones_e = sb("ones_e", [P, E], where=ph)
            iota_s = sb("iota_s", [P, P], where=ph)
            before = sb("before", [P, P], where=ph)
            ones = sb("ones", [P, P], where=ph)
            shift = sb("shift", [P, 16], where=ph)
            plan_f = sb("plan_f", [P, 16], where=ph)
            plan = sb("plan", [1, 16], I32, where=ph)
            slot_i = sb("slot_i", [P, TT], where=ph)
            onehot = sb("onehot", [P, TT, P], where=ph)
            onehotT = sb("onehotT", [P, SEQ], F32R, where=ph)
            xT_hi = sb("xT_hi", [P, KD, P], F32R, where=ph)
            xT_lo = sb("xT_lo", [P, KD, P], F32R, where=ph)
            silu2 = sb("silu2", [P, 2, HALF], where=ph)
            hid2 = sb("hid2", [P, 2, HALF], where=ph)
            hT_hi = sb("hT_hi", [P, 2, 4, P], F32R, where=ph)
            hT_lo = sb("hT_lo", [P, 2, 4, P], F32R, where=ph)
            y_hi = sb("y_hi", [P, D], F32R, where=ph)
            y_lo = sb("y_lo", [P, D], F32R, where=ph)

            moe_const = sem("moe_const")
            logits_done = sem("logits_done")
            diff_ready = sem("diff_ready")
            e2_ready = sem("e2_ready")
            chosen_ready = sem("chosen_ready")
            places_done = sem("places_done")
            plan_ready = sem("plan_ready")
            slot_ready = sem("slot_ready")
            onehot_ready = sem("onehot_ready")
            gathered = sem("gathered")
            xT_hi_ready = sem("xT_hi_ready")
            xT_lo_ready = sem("xT_lo_ready")
            onehotT_done = sem("onehotT_done")
            onehotT_ready = sem("onehotT_ready")
            silu2_ready = sem("silu2_ready")
            hid2_ready = sem("hid2_ready")
            hT_done = sem("hT_done")
            hT_hi_ready = sem("hT_hi_ready")
            hT_lo_ready = sem("hT_lo_ready")
            y_hi_ready = sem("y_hi_ready")
            y_lo_ready = sem("y_lo_ready")
            scattered = sem("scattered")
            combined = sem("combined")
            out_stored = sem("out_stored")
            G, U_, T_, Y, X = (0, 1), 2, 3, (4, 5), (6, 7)
            PRIMED = 1
            TURN = 16 * PER_ITEM // RAW

            def n_items_on(eng):
                eng.wait_ge(plan_ready, 1)
                return eng.value_load(plan[0:1, 12:13], min_val=E, max_val=MAX_ITEMS)

            def last_item_on(eng):
                eng.wait_ge(plan_ready, 1)
                return eng.value_load(plan[0:1, 13:14], min_val=E - 1, max_val=MAX_ITEMS - 1)

            def expert_on(eng, i):
                return eng.value_load(plan[0:1, bass.ds(i, 1)], min_val=0, max_val=E - 1)

            @block.sync
            def _(sp):
                def load(k, i, e):
                    c = C_MOE + k
                    sp.wait_ge(lo_ready, PER_ITEM * i + (c - RAW + 1))
                    nc.sync.dma_start(w_raw[:, c % RAW, :].rearrange("p (k n) -> p k n",
                                                                     k=2 if item[k][0] == "down" else 4),
                                      item_dram(k, e)).then_inc(raw_loaded[c % RAW], 16)

                first = RAW + AHEAD + 1
                with sp.Fori(0, E - 1) as i:
                    for k in range(first, PER_ITEM):
                        load(k, i, i)
                    for k in range(first):
                        load(k, i + 1, i + 1)
                for k in range(first, PER_ITEM):
                    load(k, E - 1, E - 1)
                n = n_items_on(sp)
                with sp.If(n > E):
                    with sp.Fori(E, n) as i:
                        e = expert_on(sp, i)
                        for k in range(PER_ITEM):
                            load(k, i, e)
                for t in range(TT):
                    sp.wait_ge(hn_ready, 4 * TT + t + 1)
                    nc.sync.dma_start(out[0, t * P:(t + 1) * P, :], hn[:, t, :]).then_inc(out_stored, 16)
                sp.wait_ge(out_stored, 16 * TT)

            @block.gpsimd
            def _(pool):
                pool.wait_ge(h_added, 12)
                for tile, value in ((before, 1.0), (ones, 1.0), (ones_e, 1.0), (shift, -1.0), (plan_f, 0.0)):
                    pool_link(nc.gpsimd.memset(tile[:], value))
                pool_link(nc.gpsimd.memset(shift[:, E:16], float(-1 - P)))
                pool_link(nc.gpsimd.affine_select(out=before[:], in_=before[:], compare_op=ALU.is_gt, fill=0.0,
                                                  base=0, pattern=[[1, P]], channel_multiplier=-1))
                pool_link(nc.gpsimd.iota(iota_s[:], pattern=[[1, P]], base=0, channel_multiplier=0,
                                         allow_small_or_imprecise_dtypes=True))
                nc.gpsimd.iota(iota_e[:], pattern=[[1, E]], base=0, channel_multiplier=0,
                               allow_small_or_imprecise_dtypes=True).then_inc(moe_const, 1)

            @block.scalar
            def _(act):
                load_gain(4, "final_norm", None)
                norm_and_transpose_act(3, 4)
                split_hi(C_MOE + 1)
                split_hi(C_MOE + 2)
                act.wait_ge(diff_ready, 1)
                nc.scalar.activation(wts[:, :, 0:1], wts[:, :, 0:1], ACT.Exp).then_inc(e2_ready, 1)

                def xT_act(item_no):
                    for g in range(2):
                        act.wait_ge(gathered, 2 * item_no + (g + 1))
                        nc.scalar.activation(xT_hi[:, 4 * g:4 * g + 4, :], bank4(X[g]), ACT.Copy
                                             ).then_inc(xT_hi_ready, 1)

                act.sem_inc(silu2_ready, PRIMED)
                xT_act(0)
                last_item = last_item_on(act)

                def item_act(i, last):
                    base, turn = PER_ITEM * i, TURN * i

                    def silu_of(b):
                        act.wait_ge(chunk_used, base + (C_MOE + (2 if b == 0 else 6 * b)))
                        act.wait_ge(hid2_ready, FB * i + at_most(b - 1) + PRIMED)
                        nc.scalar.activation(silu2[:, b % 2, :], bank[G[b % 2]][:, :], ACT.Silu
                                             ).then_inc(silu2_ready, 1)

                    def hT_of(b):
                        act.wait_ge(hT_done, FB * i + (b + 1) + PRIMED)
                        if b >= 2:
                            act.wait_ge(chunk_used, base + (C_MOE + 6 * (b - 1) + 4))
                        else:
                            act.wait_ge(chunk_used, base + C_MOE)
                        nc.scalar.activation(hT_hi[:, b % 2, :, :], bank4(T_), ACT.Copy).then_inc(hT_hi_ready, 1)

                    for k in range(AHEAD + 1, PER_ITEM + AHEAD + 1):
                        if not (last and k >= PER_ITEM):
                            split_hi(C_MOE + k, base, turn)
                        if k % 6 == 1 and k > 1 and k < PER_ITEM - 1:
                            silu_of(k // 6)
                            hT_of(k // 6 - 1)
                        elif k == 3:
                            silu_of(0)
                        elif k == 9:
                            act.wait_ge(onehotT_done, i + 1)
                            act.wait_ge(scattered, 4 * i + PRIMED)
                            nc.scalar.activation(onehotT[:], bank[T_][:, 0:SEQ], ACT.Copy
                                                 ).then_inc(onehotT_ready, 1)
                        elif k == PER_ITEM - 2:
                            hT_of(FB - 1)
                        elif k == PER_ITEM - 1 and not last:
                            xT_act(i + 1)
                        elif k == PER_ITEM + 1:
                            for g in range(2):
                                act.wait_ge(chunk_used, base + (C_MOE + PER_ITEM))
                                nc.scalar.activation(y_hi[:, g * HALF:(g + 1) * HALF], bank[Y[g]][:, :], ACT.Copy
                                                     ).then_inc(y_hi_ready, 1)

                with act.Fori(0, last_item) as i:
                    item_act(i, False)
                item_act(last_item, True)
                warm_sqrt()
                for t in range(TT):
                    act.wait_ge(combined, 4 * last_item + (3 + t) + PRIMED)
                    norm_act(4, t)

            @block.vector
            def _(dve):
                split_lo(C_MOE + 1)
                dve.wait_ge(moe_const, 1)
                dve.wait_ge(logits_done, 1)
                dve_link(nc.vector.tensor_copy(logit[:], bank[0][:, 0:TT * E].rearrange(
                    "p (t e) -> p t e", t=TT)))
                for t in range(TT):
                    last = nc.vector.max(top[:, t, :], logit[:, t, :])
                dve_link(last)
                nc.vector.tensor_tensor(wts[:, :, 0:1], top[:, :, 1:2], top[:, :, 0:1], ALU.subtract
                                        ).then_inc(diff_ready, 1)
                for t in range(TT):
                    last = nc.vector.max_index(topi[:, t, :], top[:, t, :], logit[:, t, :])
                dve_link(last)
                dve_link(nc.vector.tensor_copy(topf[:], topi[:]))
                for t in range(TT):
                    for a in range(2):
                        last = nc.vector.tensor_scalar(sel[:, t, a, :], iota_e[:], topf[:, t, a:a + 1], None,
                                                       ALU.is_equal)
                dve_link(last)
                nc.vector.tensor_tensor(chosen[:], sel[:, :, 0, :], sel[:, :, 1, :], ALU.add
                                        ).then_inc(chosen_ready, 1)
                dve.wait_ge(places_done, 1)
                dve_link(nc.vector.scalar_tensor_tensor(slot[:], bank[1][:, 0:TT * E].rearrange(
                    "p (t e) -> p t e", t=TT), 1.0, chosen[:], ALU.add, ALU.mult))

                def onehot_of(item_no, e):
                    nc.vector.tensor_scalar(slot_i[:], slot[:, :, bass.ds(e, 1)].rearrange("p t e -> p (t e)"),
                                            shift[:, bass.ds(item_no, 1)], None, ALU.add
                                            ).then_inc(slot_ready, 1)
                    dve.wait_ge(slot_ready, item_no + 1)
                    nc.vector.tensor_scalar(onehot[:, 0, :], iota_s[:], slot_i[:, 0:1], None, ALU.is_equal)
                    nc.vector.tensor_scalar(onehot[:, 1, :], iota_s[:], slot_i[:, 1:2], None, ALU.is_equal
                                            ).then_inc(onehot_ready, 1)

                def xT_dve(item_no):
                    for g in range(2):
                        dve.wait_ge(xT_hi_ready, 2 * item_no + (g + 1))
                        nc.vector.tensor_tensor(xT_lo[:, 4 * g:4 * g + 4, :], bank4(X[g]),
                                                xT_hi[:, 4 * g:4 * g + 4, :].bitcast(F32), ALU.subtract
                                                ).then_inc(xT_lo_ready, 1)

                onehot_of(0, 0)
                dve_link(nc.vector.tensor_scalar(over[:], bank[1][:, TT * E:(TT + 1) * E], float(P), None,
                                                 ALU.is_gt))
                dve_link(nc.vector.tensor_tensor_scan(rank[:], ones_e[:], over[:], 0.0, ALU.mult, ALU.add))
                nc.vector.tensor_scalar(plan_f[:, 12:13], rank[:, E - 1:E], float(E), None, ALU.add)
                dve_link(nc.vector.tensor_scalar(plan_f[:, 13:14], rank[:, E - 1:E], float(E - 1), None,
                                                 ALU.add))
                dve_link(nc.vector.tensor_tensor(rank[:], rank[:], over[:], ALU.mult))
                dve_link(nc.vector.tensor_copy(plan_f[:, 0:E], iota_e[:]))
                for r in range(MAX_EXTRA):
                    dve_link(nc.vector.tensor_scalar(scratch[:], rank[:], float(r + 1), None, ALU.is_equal))
                    dve_link(nc.vector.tensor_tensor(scratch[:], scratch[:], iota_e[:], ALU.mult))
                    dve_link(nc.vector.tensor_reduce(plan_f[:, E + r:E + r + 1], scratch[:], AX.X, ALU.add))
                nc.vector.tensor_copy(plan[:], plan_f[0:1, :]).then_inc(plan_ready, 1)
                split_lo(C_MOE + 2)
                dve.wait_ge(e2_ready, 1)
                dve_link(nc.vector.tensor_scalar(wts[:, :, 1:2], wts[:, :, 0:1], 1.0, None, ALU.add))
                dve_link(nc.vector.reciprocal(wts[:, :, 2:3], wts[:, :, 1:2]))
                dve_link(nc.vector.tensor_tensor(wts[:, :, 3:4], wts[:, :, 2:3], wts[:, :, 0:1], ALU.mult))
                for t in range(TT):
                    dve_link(nc.vector.tensor_scalar(gates[:, t, :], sel[:, t, 0, :], wts[:, t, 2:3], None,
                                                     ALU.mult))
                    dve_link(nc.vector.scalar_tensor_tensor(gates[:, t, :], sel[:, t, 1, :], wts[:, t, 3:4],
                                                            gates[:, t, :], ALU.mult, ALU.add))
                last_item = last_item_on(dve)
                for primed in (hid2_ready, hT_lo_ready, y_lo_ready, combined):
                    dve.sem_inc(primed, PRIMED)
                xT_dve(0)

                def item_dve(i, last):
                    base = PER_ITEM * i

                    def hid_of(b):
                        dve.wait_ge(silu2_ready, FB * i + (b + 1) + PRIMED)
                        dve.wait_ge(chunk_used, base + (C_MOE + (4 if b == 0 else 6 * b + 2)))
                        dve.wait_ge(hT_done, FB * i + at_most(b - 1) + PRIMED)
                        nc.vector.tensor_tensor(hid2[:, b % 2, :], silu2[:, b % 2, :], bank[U_][:, :], ALU.mult
                                                ).then_inc(hid2_ready, 1)

                    def hT_of(b):
                        dve.wait_ge(hT_hi_ready, FB * i + (b + 1))
                        nc.vector.tensor_tensor(hT_lo[:, b % 2, :, :], bank4(T_),
                                                hT_hi[:, b % 2, :, :].bitcast(F32), ALU.subtract
                                                ).then_inc(hT_lo_ready, 1)

                    for k in range(AHEAD + 1, PER_ITEM + AHEAD + 1):
                        if not (last and k >= PER_ITEM):
                            split_lo(C_MOE + k, base)
                        if k % 6 == 3 and k > 3 and k < PER_ITEM - 1:
                            hid_of(k // 6)
                        elif k == 5:
                            hid_of(0)
                        elif k % 6 == 1 and k > 1 and k < PER_ITEM - 1:
                            hT_of(k // 6 - 1)
                        elif k == 26 and not last:
                            dve.wait_ge(onehotT_done, i + 1)
                            dve.wait_ge(gathered, 2 * i + 2)
                            onehot_of(i + 1, expert_on(dve, i + 1))
                        elif k == PER_ITEM - 2:
                            hT_of(FB - 1)
                        elif k == PER_ITEM - 1 and not last:
                            xT_dve(i + 1)
                        elif k == PER_ITEM + 1:
                            for g in range(2):
                                dve.wait_ge(y_hi_ready, 2 * i + (g + 1))
                                part = slice(g * HALF, (g + 1) * HALF)
                                nc.vector.tensor_tensor(y_lo[:, part], bank[Y[g]][:, :], y_hi[:, part].bitcast(F32),
                                                        ALU.subtract).then_inc(y_lo_ready, 1)
                            e = expert_on(dve, i)
                            dve.wait_ge(combined, 4 * i + PRIMED)
                            for g in range(2):
                                for t in range(TT):
                                    dve.wait_ge(scattered, 4 * i + (2 * g + t + 1) + PRIMED)
                                    part = h[:, t, g * HALF:(g + 1) * HALF]
                                    nc.vector.scalar_tensor_tensor(
                                        part, bank[X[t]][:, :], gates[:, t, bass.ds(e, 1)], part,
                                        ALU.mult, ALU.add).then_inc(combined, 1)

                with dve.Fori(0, last_item) as i:
                    item_dve(i, False)
                item_dve(last_item, True)
                for t in range(TT):
                    norm_dve(4, t)

            @block.tensor
            def _(pe):
                pe.wait_ge(rt_lo_ready, 1)
                for t in range(TT):
                    transpose_pe(3, 4, t)
                    for k in range(KD):
                        if k % 4 == 0:
                            transposed(3, t, k // 4)
                        last = mm3(bank[0][:, t * E:(t + 1) * E], tok(hnT, k, t),
                                   (rt_hi[:, k, :], rt_lo[:, k, :]), k == 0, k == KD - 1)
                last.then_inc(logits_done, 1)
                pe.wait_ge(chosen_ready, 1)
                nc.tensor.matmul(bank[1][:, 0:E], before[:], chosen[:, 0, :], start=True, stop=True)
                nc.tensor.matmul(bank[1][:, E:2 * E], ones[:], chosen[:, 0, :], start=True, stop=False)
                nc.tensor.matmul(bank[1][:, E:2 * E], before[:], chosen[:, 1, :], start=False, stop=True)
                for t in range(TT):
                    last = nc.tensor.matmul(bank[1][:, 2 * E:3 * E], ones[:], chosen[:, t, :],
                                            start=t == 0, stop=t == TT - 1)
                last.then_inc(places_done, 1)

                def gather(item_no):
                    pe.wait_ge(onehot_ready, item_no + 1)
                    for g in range(2):
                        for j in range(4):
                            for t in range(TT):
                                col = (4 * g + j) * P
                                last = nc.tensor.matmul(bank[X[g]][:, j * P:(j + 1) * P], hn[:, t, col:col + P],
                                                        onehot[:, t, :], start=t == 0, stop=t == TT - 1)
                        last.then_inc(gathered, 1)

                for primed in (hT_done, scattered):
                    pe.sem_inc(primed, PRIMED)
                gather(0)

                def project(k, q, b0, first=0, items=0, base=0):
                    c = C_MOE + k + q
                    chunk_here(c, base)
                    if first:
                        pe.wait_ge(xT_lo_ready, items + (q + 1))
                    for j in range(4):
                        kt = 4 * q + j
                        last = mm3(bank[b0][:, :], (xT_hi[:, kt, :], xT_lo[:, kt, :]),
                                   weights(c, j, 0, HALF, HALF), kt == 0, kt == KD - 1)
                    last.then_inc(chunk_used, 1)

                project(0, 0, G[0], first=1)
                last_item = last_item_on(pe)

                def item_pe(i, final):
                    base = PER_ITEM * i

                    def transposes(b):
                        pe.wait_ge(hid2_ready, FB * i + (b + 1) + PRIMED)
                        pe.wait_ge(hT_lo_ready, FB * i + b + PRIMED)
                        if b == 1:
                            pe.wait_ge(onehotT_ready, i + 1)
                        for j in range(4):
                            last = nc.tensor.transpose(bank[T_][:, j * P:(j + 1) * P],
                                                       hid2[:, b % 2, j * P:(j + 1) * P], ident[:])
                        last.then_inc(hT_done, 1)

                    def down(k, b, q):
                        c = C_MOE + k
                        chunk_here(c, base)
                        pe.wait_ge(hT_lo_ready, FB * i + (b + 1) + PRIMED)
                        for j in range(2):
                            kt = 2 * q + j
                            a = (hT_hi[:, b % 2, kt, :], hT_lo[:, b % 2, kt, :])
                            for g in range(2):
                                last = mm3(bank[Y[g]][:, :], a, weights(c, j, g * HALF, (g + 1) * HALF, D),
                                           b == 0 and kt == 0, b == FB - 1 and kt == 3)
                        last.then_inc(chunk_used, 1)

                    for b in range(FB):
                        k0 = 0 if b == 0 else 6 * b - 2
                        if b == 0:
                            project(0, 1, G[0], first=1, items=2 * i, base=base)
                        else:
                            pe.wait_ge(silu2_ready, FB * i + at_most(b - 1) + PRIMED)
                            project(k0, 0, G[b % 2], base=base)
                            project(k0, 1, G[b % 2], base=base)
                        if b:
                            transposes(b - 1)
                        pe.wait_ge(hid2_ready, FB * i + b + PRIMED)
                        project(k0 + 2, 0, U_, base=base)
                        project(k0 + 2, 1, U_, base=base)
                        if b == 1:
                            pe.wait_ge(hT_lo_ready, FB * i + 1 + PRIMED)
                            for t in range(TT):
                                last = nc.tensor.transpose(bank[T_][:, t * P:(t + 1) * P], onehot[:, t, :], ident[:])
                            last.then_inc(onehotT_done, 1)
                            pe.wait_ge(y_lo_ready, 2 * i + PRIMED)
                        if b:
                            down(k0 + 4, b - 1, 0)
                            if b == FB - 1:
                                transposes(b)
                            down(k0 + 5, b - 1, 1)
                    pe.wait_ge(combined, 4 * i + PRIMED)
                    if not final:
                        gather(i + 1)
                    down(PER_ITEM - 2, FB - 1, 0)
                    down(PER_ITEM - 1, FB - 1, 1)
                    if not final:
                        pe.wait_ge(silu2_ready, FB * i + FB + PRIMED)
                        project(PER_ITEM, 0, G[0], first=1, items=2 * i + 2, base=base)
                    for g in range(2):
                        pe.wait_ge(y_lo_ready, 2 * i + (g + 1) + PRIMED)
                        for t in range(TT):
                            if g == 1:
                                pe.wait_ge(combined, 4 * i + (t + 1) + PRIMED)
                            elif not final:
                                pe.wait_ge(xT_lo_ready, 2 * i + 4)
                            part = slice(g * HALF, (g + 1) * HALF)
                            a = onehotT[:, t * P:(t + 1) * P]
                            nc.tensor.matmul(bank[X[t]][:, :], a, y_hi[:, part], start=True, stop=False)
                            nc.tensor.matmul(bank[X[t]][:, :], a, y_lo[:, part], start=False, stop=True
                                             ).then_inc(scattered, 1)

                with pe.Fori(0, last_item) as i:
                    item_pe(i, False)
                item_pe(last_item, True)


_INS = ["x", "positions", "mix_norm", "ffn_norm", "final_norm", "mla_w_in", "mla_q_norm", "mla_w_q_up",
        "mla_kv_norm", "mla_w_kv_up", "mla_w_o", "hgrn_w_in", "hgrn_lower_bounds", "hgrn_out_norm",
        "hgrn_w_o", "ffn_w_gate", "ffn_w_up", "ffn_w_down", "moe_router", "moe_w_gate", "moe_w_up",
        "moe_w_down"]


def kernel(**inputs):
    import concourse.bacc as bacc
    from concourse.bass_utils import run_bass_kernel_spmd

    nc = bacc.Bacc("TRN2", target_bir_lowering=False, num_devices=1)
    arrays, w = {}, {}
    for name in _INS:
        a = np.ascontiguousarray(inputs[name])
        arrays[f"in_{name}"] = a
        w[name] = nc.dram_tensor(f"in_{name}", a.shape, mybir.dt.from_np(a.dtype), kind="ExternalInput").ap()
    out = nc.dram_tensor("out", (1, SEQ, D), F32, kind="ExternalOutput").ap()
    trunk(nc, w, out)
    r = run_bass_kernel_spmd(nc, [arrays], core_ids=[0])
    return r.results[0]["out"]
```

```python
from contextlib import ExitStack

import numpy as np
import concourse.bass as bass
from concourse import mybir

F32 = mybir.dt.float32
F32R = mybir.dt.float32r
I32 = mybir.dt.int32
U32 = mybir.dt.uint32
ALU = mybir.AluOpType
ACT = mybir.ActivationFunctionType
AX = mybir.AxisListType

P = 128
D = 1024
SEQ = 256
TT = SEQ // P
KD = D // P
HALF = 512
EPS = 1e-6
HEADS, NOPE, ROPE, VD = 16, 64, 32, 64
QL, KVL = 384, 256
MLA_IN = QL + KVL + ROPE
QD = NOPE + ROPE
ROPE_THETA = 10000.0
HG, DK, CH = 8, 128, 64
NCH = SEQ // CH
FF = 3584
FB = FF // HALF
E = 8
RAW, SPLIT, CW = 6, 3, 2048
AHEAD = 2
NEG = -1e30

N_IN, N_QUP, N_KVUP, N_O = 3, 3, 2, 4
IN_ROWS = ((0, 2), (2, 5), (5, 8))
C_IN = 0
C_QUP = C_IN + N_IN
C_KVUP = C_QUP + N_QUP
C_O = C_KVUP + N_KVUP
C_FFN = C_O + N_O
C_DOWN = C_FFN + 4 * FB
C_HG = C_DOWN + 2 * FB
C_HGO = C_HG + 16
C_MOE = C_HGO + 4
PER_ITEM = 6 * FB
MAX_EXTRA = 3
MAX_ITEMS = E + MAX_EXTRA


def dense_chunks(w):
    def rows(m, k0, k1, n0=0, n1=None):
        v = m[k0 * P:k1 * P, :].rearrange("(k p) n -> p k n", p=P)
        return v[:, :, n0:(n1 if n1 is not None else m.shape[1])]
    out = [rows(w["mla_w_in"][0], k0, k1) for k0, k1 in IN_ROWS]
    out += [rows(w["mla_w_q_up"][0], k, k + 1) for k in range(3)]
    out += [rows(w["mla_w_kv_up"][0], k, k + 1) for k in range(2)]
    out += [rows(w["mla_w_o"][0], 2 * k, 2 * k + 2) for k in range(4)]
    for b in range(FB):
        for m in ("ffn_w_gate", "ffn_w_up"):
            out += [rows(w[m][0], 4 * q, 4 * q + 4, b * HALF, (b + 1) * HALF) for q in range(2)]
    out += [rows(w["ffn_w_down"][0], 2 * k, 2 * k + 2) for k in range(2 * FB)]
    for b in (4, 2, 3, 0, 1, 5, 6, 7):
        out += [rows(w["hgrn_w_in"][0], 4 * q, 4 * q + 4, b * HALF, (b + 1) * HALF) for q in range(2)]
    out += [rows(w["hgrn_w_o"][0], 2 * k, 2 * k + 2) for k in range(4)]
    assert len(out) == C_MOE
    return out


def item_chunks():
    out = []
    for b in range(FB):
        out += [("gate", b, 0), ("gate", b, 1), ("up", b, 0), ("up", b, 1)]
        if b:
            out += [("down", b - 1, 0), ("down", b - 1, 1)]
    out += [("down", FB - 1, 0), ("down", FB - 1, 1)]
    assert len(out) == PER_ITEM
    return out


def at_least(x, low=0):
    return x if x > low else low


def trunk(nc, w, out):
    ctx = ExitStack()

    def sb(name, shape, dt=F32, where=None):
        return (where or ctx).enter_context(nc.sbuf_tensor(name, shape, dt))

    def sem(name):
        return ctx.enter_context(nc.semaphore(name))

    with ctx:
        w_raw = sb("w_raw", [P, RAW, CW])
        w_hi = sb("w_hi", [P, SPLIT, CW], F32R)
        w_lo = sb("w_lo", [P, SPLIT, CW], F32R)
        h = sb("h", [P, TT, D])
        hn = sb("hn", [P, TT, D])
        hnT_hi = sb("hnT_hi", [P, KD, SEQ], F32R)
        hnT_lo = sb("hnT_lo", [P, KD, SEQ], F32R)
        gain = sb("gain", [P, 2, D])
        ident = sb("ident", [P, P])
        ss = sb("ss", [P, 2 * TT])
        rms = sb("rms", [P, 2 * TT])
        warm = sb("warm", [P, 2])
        eps = sb("eps", [P, 1])
        rt_raw = sb("rt_raw", [P, KD, E])
        rt = sb("rt", [P, KD, 2, E], F32R)
        rstd = sb("rstd", [P, 2 * TT])
        bank = [ctx.enter_context(nc.psum_tensor(f"bank{i}", [P, HALF], F32)) for i in range(8)]

        raw_loaded = [sem(f"raw_loaded{i}") for i in range(RAW)]
        hi_ready, lo_ready, chunk_used = sem("hi_ready"), sem("lo_ready"), sem("chunk_used")
        hi_quarter = sem("hi_quarter")
        x_loaded = [sem("x_loaded0"), sem("x_loaded1")]
        rt_loaded, rt_hi_ready, rt_lo_ready = sem("rt_loaded"), sem("rt_hi_ready"), sem("rt_lo_ready")
        gain_loaded = [sem("gain_loaded0"), sem("gain_loaded1")]
        sq_done = sem("sq_done")
        ms_ready = sem("ms_ready")
        rms_ready = sem("rms_ready")
        hn_ready = sem("hn_ready")
        nT_done = sem("nT_done")
        nT_hi_ready = sem("nT_hi_ready")
        nT_lo_ready = sem("nT_lo_ready")
        h_added = sem("h_added")
        const_ready = sem("const_ready")
        out_done = sem("out_done")
        dve_step = sem("dve_step")
        act_step = sem("act_step")
        pool_step = sem("pool_step")
        steps = {"dve": 0, "act": 0, "pool": 0}

        def dve_link(ins):
            steps["dve"] += 1
            ins.then_inc(dve_step, 1)
            nc.vector.wait_ge(dve_step, steps["dve"])

        def act_link(ins):
            steps["act"] += 1
            ins.then_inc(act_step, 1)
            nc.scalar.wait_ge(act_step, steps["act"])

        def pool_link(ins):
            steps["pool"] += 1
            ins.then_inc(pool_step, 1)
            nc.gpsimd.wait_ge(pool_step, steps["pool"])

        block = ctx.enter_context(nc.Block())
        chunks = dense_chunks(w)
        item = item_chunks()
        C_END = C_MOE + AHEAD + 1

        def load_chunk(c, dram=None):
            src = chunks[c] if dram is None else dram
            if c >= RAW:
                nc.sync.wait_ge(lo_ready, c - RAW + 1)
            k, n = src.shape[1], src.shape[2]
            dst = w_raw[:, c % RAW, 0:k * n].rearrange("p (k n) -> p k n", k=k)
            nc.sync.dma_start(dst, src).then_inc(raw_loaded[c % RAW], 16)

        def width(c):
            return chunks[c].shape[1] * chunks[c].shape[2] if c < C_MOE else CW

        def split_hi(c, base=0, turn=0):
            n = width(c)
            nc.scalar.wait_ge(raw_loaded[c % RAW], turn + 16 * (c // RAW + 1))
            if c >= SPLIT:
                nc.scalar.wait_ge(chunk_used, base + (c - SPLIT + 1))
            nc.scalar.activation(w_hi[:, c % SPLIT, 0:n], w_raw[:, c % RAW, 0:n],
                                 ACT.Copy).then_inc(hi_ready, 1)

        def split_lo(c, base=0):
            n = width(c)
            nc.vector.wait_ge(hi_ready, base + (c + 1))
            nc.vector.tensor_tensor(w_lo[:, c % SPLIT, 0:n], w_raw[:, c % RAW, 0:n],
                                    w_hi[:, c % SPLIT, 0:n].bitcast(F32),
                                    ALU.subtract).then_inc(lo_ready, 1)

        def split_hi_quarter(c, j):
            nc.scalar.wait_ge(raw_loaded[c % RAW], 16 * (c // RAW + 1))
            nc.scalar.wait_ge(chunk_used, c - SPLIT + 1)
            n = width(c) // 4
            part = slice(j * n, (j + 1) * n)
            nc.scalar.activation(w_hi[:, c % SPLIT, part], w_raw[:, c % RAW, part], ACT.Copy
                                 ).then_inc(hi_ready if j == 3 else hi_quarter, 1)

        def split_lo_quarter(c, j, quarters):
            if j == 3:
                nc.vector.wait_ge(hi_ready, c + 1)
            else:
                nc.vector.wait_ge(hi_quarter, quarters)
            n = width(c) // 4
            part = slice(j * n, (j + 1) * n)
            last = nc.vector.tensor_tensor(w_lo[:, c % SPLIT, part], w_raw[:, c % RAW, part],
                                           w_hi[:, c % SPLIT, part].bitcast(F32), ALU.subtract)
            if j == 3:
                last.then_inc(lo_ready, 1)

        def chunk_here(c, base=0):
            nc.tensor.wait_ge(lo_ready, base + (c + 1))

        def weights(c, k, n0, n1, n):
            return w_hi[:, c % SPLIT, k * n + n0:k * n + n1], w_lo[:, c % SPLIT, k * n + n0:k * n + n1]

        def mm3(o, a, b, start, stop):
            nc.tensor.matmul(o, a[0], b[0], start=start, stop=False)
            nc.tensor.matmul(o, a[0], b[1], start=False, stop=False)
            return nc.tensor.matmul(o, a[1], b[0], start=False, stop=stop)

        def tok(a, k, t):
            return a[0][:, k, t * P:(t + 1) * P], a[1][:, k, t * P:(t + 1) * P]

        hnT = (hnT_hi, hnT_lo)

        def item_dram(k, e):
            kind, b, q = item[k]
            m = w["moe_w_" + kind]
            m = m[0, bass.ds(e, 1)].rearrange("e a n -> (e a) n")
            if kind == "down":
                r = (4 * b + 2 * q) * P
                return m[r:r + 2 * P, :].rearrange("(k p) n -> p k n", p=P)
            return m[4 * q * P:(4 * q + 4) * P, b * HALF:(b + 1) * HALF].rearrange("(k p) n -> p k n", p=P)

        def warm_sqrt():
            nc.scalar.activation(warm[:, 1:2], warm[:, 0:1], ACT.Sqrt)

        def norm_act(k, t, here=None):
            for n in range(2):
                if here:
                    here(t, n)
                else:
                    nc.scalar.wait_ge(h_added, 4 * (k - 1) + 2 * t + n + 1)
                part = slice(n * HALF, (n + 1) * HALF)
                last = nc.scalar.activation(hn[:, t, part], h[:, t, part], ACT.Square,
                                            accum_out=ss[:, 2 * t + n:2 * t + n + 1])
            last.then_inc(sq_done, 1)
            nc.scalar.wait_ge(ms_ready, TT * k + t + 1)
            nc.scalar.activation(rms[:, t:t + 1], ss[:, 2 * t:2 * t + 1], ACT.Sqrt, bias=eps[:],
                                 scale=1.0 / D).then_inc(rms_ready, 1)

        def norm_and_transpose_act(k, c=None):
            for t in range(TT):
                norm_act(k, t)
                transpose_act(k, 4, t)
                if t == 0 and c is not None:
                    split_hi(c)

        def norm_dve(k, t):
            nc.vector.wait_ge(sq_done, TT * k + t + 1)
            nc.vector.tensor_tensor(ss[:, 2 * t:2 * t + 1], ss[:, 2 * t:2 * t + 1],
                                    ss[:, 2 * t + 1:2 * t + 2], ALU.add).then_inc(ms_ready, 1)
            nc.vector.wait_ge(rms_ready, TT * k + t + 1)
            dve_link(nc.vector.reciprocal(rstd[:, t:t + 1], rms[:, t:t + 1]))
            nc.vector.wait_ge(gain_loaded[k % 2], 16 * (k // 2 + 1))
            for n in range(2):
                part = slice(n * HALF, (n + 1) * HALF)
                nc.vector.scalar_tensor_tensor(hn[:, t, part], h[:, t, part], rstd[:, t:t + 1],
                                               gain[:, k % 2, part], ALU.mult, ALU.mult
                                               ).then_inc(hn_ready, 1)

        def transpose_pe(k, b0, t):
            for g in range(2):
                nc.tensor.wait_ge(hn_ready, 2 * (TT * k + t) + g + 1)
                for j in range(4):
                    col = (4 * g + j) * P
                    last = nc.tensor.transpose(bank[b0 + 2 * t + g][:, j * P:(j + 1) * P],
                                               hn[:, t, col:col + P], ident[:])
                last.then_inc(nT_done, 1)

        def bank4(b):
            return bank[b][:, :].rearrange("p (j s) -> p j s", j=4)

        def transpose_act(k, b0, t):
            for g in range(2):
                nc.scalar.wait_ge(nT_done, 4 * k + 2 * t + g + 1)
                nc.scalar.activation(hnT_hi[:, 4 * g:4 * g + 4, t * P:(t + 1) * P],
                                     bank4(b0 + 2 * t + g), ACT.Copy).then_inc(nT_hi_ready, 1)

        def transpose_dve(k, b0, t):
            for g in range(2):
                nc.vector.wait_ge(nT_hi_ready, 4 * k + 2 * t + g + 1)
                nc.vector.tensor_tensor(hnT_lo[:, 4 * g:4 * g + 4, t * P:(t + 1) * P],
                                        bank4(b0 + 2 * t + g),
                                        hnT_hi[:, 4 * g:4 * g + 4, t * P:(t + 1) * P].bitcast(F32),
                                        ALU.subtract).then_inc(nT_lo_ready, 1)

        def transposed(k, t, g):
            nc.tensor.wait_ge(nT_lo_ready, 4 * k + 2 * t + g + 1)

        def out_proj_pe(c0, n_chunks, src, norm, before=None, between=None):
            def products(q, t):
                if before:
                    before(q, t)
                for k in range(2):
                    kt = 2 * q + k
                    if (t, kt) == (TT - 1, 2 * n_chunks - 1):
                        transpose_pe(norm, 4, 0)
                    for n in range(2):
                        last = mm3(bank[2 * t + n][:, :], tok(src, kt, t),
                                   weights(c0 + q, k, n * HALF, (n + 1) * HALF, D),
                                   kt == 0, kt == 2 * n_chunks - 1)
                return last

            for q in range(n_chunks - 2):
                chunk_here(c0 + q)
                for t in range(TT):
                    last = products(q, t)
                last.then_inc(chunk_used, 1)
                if between:
                    between(q)
            for t in range(TT):
                for q in (n_chunks - 2, n_chunks - 1):
                    if t == 0:
                        chunk_here(c0 + q)
                    last = products(q, t)
                    if t == TT - 1:
                        last.then_inc(chunk_used, 1)
                if t == 0:
                    last.then_inc(out_done, 1)

        def first_block_pe(c0, norm):
            for t in range(TT):
                for q in range(2):
                    if t == 0:
                        chunk_here(c0 + q)
                    transposed(norm, t, q)
                    for k in range(4):
                        kt = 4 * q + k
                        if (t, kt) == (0, KD - 1):
                            transpose_pe(norm, 4, 1)
                        last = mm3(bank[t][:, :], tok(hnT, kt, t), weights(c0 + q, k, 0, HALF, HALF),
                                   kt == 0, kt == KD - 1)
                    if t == TT - 1:
                        last.then_inc(chunk_used, 1)

        def residual_dve(stage, t, c_last):
            if t == 0:
                nc.vector.wait_ge(out_done, stage + 1)
            else:
                nc.vector.wait_ge(chunk_used, c_last + 1)
            for n in range(2):
                part = h[:, t, n * HALF:(n + 1) * HALF]
                nc.vector.tensor_tensor(part, part, bank[2 * t + n][:, :],
                                        ALU.add).then_inc(h_added, 1)

        def residual_and_norm_dve(stage, c_last, c=None):
            for t in range(TT):
                residual_dve(stage, t, c_last)
                if t == 1 and c is not None:
                    split_lo(c)
                norm_dve(stage + 1, t)
                transpose_dve(stage + 1, 4, t)

        def load_gain(k, name, row):
            src = w[name]
            src = src[row:row + 1, :] if row is not None else src.rearrange("(a n) -> a n", a=1)
            if k >= 2:
                nc.scalar.wait_ge(hn_ready, 2 * TT * (k - 1))
            nc.scalar.dma_start(gain[:, k % 2, :], src.broadcast_to([P, D])).then_inc(gain_loaded[k % 2], 16)

        ph = ExitStack()
        with ph:
            qg = sb("qg", [P, QL], where=ph)
            kvg = sb("kvg", [P, KVL], where=ph)
            pos_i = sb("pos_i", [P, TT], I32, where=ph)
            posf = sb("posf", [P, TT], where=ph)
            freq = sb("freq", [P, ROPE // 2], where=ph)
            ang = sb("ang", [P, TT, ROPE // 2], where=ph)
            turns = sb("turns", [P, TT, ROPE // 2], where=ph)
            absr = sb("absr", [P, TT, ROPE // 2], where=ph)
            cos = sb("cos", [P, TT, ROPE // 2], where=ph)
            sin = sb("sin", [P, TT, ROPE // 2], where=ph)
            halfpi = sb("halfpi", [P, 1], where=ph)
            mask = sb("mask", [P, 3 * P], where=ph)
            cqv = sb("cqv", [P, TT, MLA_IN], where=ph)
            krp = sb("krp", [P, TT, QD], where=ph)
            krT = sb("krT", [P, SEQ], where=ph)
            cT_hi = sb("cT_hi", [P, 5, SEQ], F32R, where=ph)
            cT_lo = sb("cT_lo", [P, 5, SEQ], F32R, where=ph)
            q_sb = sb("q_sb", [P, TT, HEADS * QD], where=ph)
            qT = sb("qT", [QD, HEADS, SEQ], where=ph)
            kT = sb("kT", [QD, HEADS, SEQ], where=ph)
            rot = sb("rot", [P, 4, HEADS * ROPE // 2], where=ph)
            nmax = sb("nmax", [P, 4, TT], where=ph)
            psum_ = sb("prob_sum", [P, 4, TT], where=ph)
            prcp = sb("prcp", [P, 4, TT], where=ph)
            v_sb = hn
            PB, PT = 4, 3
            SB = (0, 1, 6)
            SPLIT_AT = 2
            CT = ((0, 2, 0), (2, 1, 1), (3, 2, 6))
            prob3 = cqv[:, :, :].rearrange("p t n -> p (t n)")

            def prob(i, n0, n1):
                j = i % PB
                return prob3[:, j * 3 * P + n0:j * 3 * P + n1] if j < 3 else q_sb[:, 0, n0:n1]

            probT = q_sb[:, 1, 0:PT * 3 * P].rearrange("p (a n) -> p a n", a=PT)

            small_loaded = sem("small_loaded")
            trig_ready = sem("trig_ready")
            red_ready = sem("red_ready")
            cq_squared = sem("cq_squared")
            krp_ready = sem("krp_ready")
            krT_done = sem("krT_done")
            cq_ms = sem("cq_ms")
            cq_rms = sem("cq_rms")
            rc_ready = sem("rc_ready")
            cq_done = sem("cq_done")
            q_done = sem("q_done")
            cn_ready = sem("cn_ready")
            cT_done = sem("cT_done")
            cT_hi_ready = sem("cT_hi_ready")
            cT_lo_ready = sem("cT_lo_ready")
            krT_ready = sem("krT_ready")
            kr_spread = sem("kr_spread")
            q_copied = sem("q_copied")
            q_roped = sem("q_roped")
            kn_done = sem("kn_done")
            kn_copied = sem("kn_copied")
            v_done = sem("v_done")
            v_copied = sem("v_copied")
            qT_done = sem("qT_done")
            qT_copied = sem("qT_copied")
            score_done = sem("score_done")
            masked = sem("masked")
            max_ready = sem("max_ready")
            exp_done = sem("exp_done")
            rcp_done = sem("rcp_done")
            prob_ready = sem("prob_ready")
            probT_done = sem("probT_done")
            probT_copied = sem("probT_copied")
            pv_done = sem("pv_done")
            oT_hi_ready = sem("oT_hi_ready")
            oT_lo_ready = sem("oT_lo_ready")

            @block.sync
            def _(sp):
                for t in range(TT):
                    nc.sync.dma_start(h[:, t, :], w["x"][0, t * P:(t + 1) * P, :]).then_inc(x_loaded[t], 16)
                load_chunk(0)
                load_chunk(1)
                nc.sync.dma_start(pos_i[:], w["positions"].rearrange("b (t p) -> p (b t)", p=P),
                                  allow_slow_non_contiguous=True).then_inc(small_loaded, 16)
                nc.sync.dma_start(qg[:], w["mla_q_norm"].broadcast_to([P, QL])).then_inc(small_loaded, 16)
                nc.sync.dma_start(kvg[:], w["mla_kv_norm"].broadcast_to([P, KVL])).then_inc(small_loaded, 16)
                for c in range(2, RAW):
                    load_chunk(c)
                nc.sync.dma_start(rt_raw[:], w["moe_router"][0].rearrange("(k p) e -> p k e", p=P)
                                  ).then_inc(rt_loaded, 16)
                for c in range(RAW, C_FFN + RAW + AHEAD + 1):
                    load_chunk(c)

            @block.gpsimd
            def _(pool):
                nc.gpsimd.memset(eps[:], EPS)
                nc.gpsimd.memset(warm[:], 1.0).then_inc(const_ready, 1)
                pool_link(nc.gpsimd.memset(ident[:], 0.0))
                nc.gpsimd.affine_select(out=ident[:], in_=ident[:], compare_op=ALU.not_equal, fill=1.0,
                                        base=0, pattern=[[-1, P]], channel_multiplier=1
                                        ).then_inc(const_ready, 1)
                inv = ROPE_THETA ** (-np.arange(0, ROPE, 2, dtype=np.float32) / np.float32(ROPE))
                for j in range(ROPE // 2):
                    nc.gpsimd.memset(freq[:, j:j + 1], float(np.float32(inv[j])))
                nc.gpsimd.memset(halfpi[:], float(np.pi / 2))
                nc.gpsimd.memset(krp[:], 0.0).then_inc(const_ready, 1)
                pool_link(nc.gpsimd.memset(mask[:], 0.0))
                for b in (0, 2):
                    nc.gpsimd.affine_select(out=mask[:, b * P:(b + 1) * P], in_=mask[:, b * P:(b + 1) * P],
                                            compare_op=ALU.is_ge, fill=NEG, base=0, pattern=[[-1, P]],
                                            channel_multiplier=1).then_inc(const_ready, 1)
                nc.gpsimd.wait_ge(const_ready, 5)
                nc.gpsimd.wait_ge(krT_ready, 1)
                nc.gpsimd.tensor_copy(kT[NOPE:QD, :, :],
                                      krT[NOPE:QD, :].unsqueeze(1).broadcast_to([ROPE, HEADS, SEQ])
                                      ).then_inc(kr_spread, 1)

            @block.scalar
            def _(act):
                load_gain(0, "mix_norm", 0)
                act.wait_ge(const_ready, 1)
                warm_sqrt()
                for t in range(TT):
                    norm_act(0, t, lambda t, n: act.wait_ge(x_loaded[t], 16))
                split_hi(0)
                for t in range(TT):
                    transpose_act(0, 0, t)
                for c in range(1, 3):
                    split_hi(c)
                load_gain(1, "ffn_norm", 0)
                split_hi(3)
                act.wait_ge(red_ready, 1)
                nc.scalar.activation(sin[:], turns[:], ACT.Sin).then_inc(trig_ready, 1)
                act_link(nc.scalar.activation(absr[:], turns[:], ACT.Abs))
                act.wait_ge(const_ready, 3)
                nc.scalar.activation(cos[:], absr[:], ACT.Sin, bias=halfpi[:], scale=-1.0
                                     ).then_inc(trig_ready, 1)
                warm_sqrt()
                split_hi(4)
                for t in range(TT):
                    act.wait_ge(cn_ready, t + 1)
                    nc.scalar.activation(q_sb[:, t, 0:QL], bank[4 + t][:, 0:QL], ACT.Square,
                                         accum_out=ss[:, 2 * t:2 * t + 1]).then_inc(cq_squared, 1)

                def cT_act(b):
                    act.wait_ge(cT_done, b + 1)
                    k0, n, bk = CT[b]
                    nc.scalar.activation(cT_hi[:, k0:k0 + n, :],
                                         bank[bk][:, 0:n * SEQ].rearrange("p (j s) -> p j s", j=n),
                                         ACT.Copy).then_inc(cT_hi_ready, 1)

                cT_act(0)
                cT_act(1)
                act.wait_ge(chunk_used, C_IN + N_IN)
                for t in range(TT):
                    nc.scalar.activation(q_sb[:, t, QL:QL + KVL], bank[6 + t][:, 0:KVL], ACT.Square,
                                         accum_out=ss[:, 2 * t + 1:2 * t + 2]).then_inc(cq_squared, 1)
                act.wait_ge(cq_ms, 1)
                nc.scalar.activation(rms[:], ss[:], ACT.Sqrt).then_inc(cq_rms, 1)
                split_hi(5)
                split_hi(6)
                cT_act(2)
                act.wait_ge(krT_done, 1)
                nc.scalar.activation(krT[NOPE:QD, :], bank[7][NOPE:QD, 0:SEQ], ACT.Copy
                                     ).then_inc(krT_ready, 1)
                split_hi(7)
                act.wait_ge(q_done, 1)
                act.wait_ge(rc_ready, 1)
                for n in range(3):
                    nc.scalar.activation(q_sb[:, 0, n * HALF:(n + 1) * HALF], bank[2 * n][:, :], ACT.Copy,
                                         scale=rstd[:, 0:1]).then_inc(q_copied, 1)
                for u in range(HEADS // 2):
                    act.wait_ge(kn_done, u + 1)
                    nc.scalar.activation(kT[0:NOPE, 2 * u:2 * u + 2, :],
                                         bank[6 + u % 2][0:NOPE, :].rearrange("p (a s) -> p a s", a=2),
                                         ACT.Copy).then_inc(kn_copied, 1)
                    if 2 <= u < 6:
                        split_hi_quarter(C_O, u - 2)
                nc.scalar.activation(warm[:, 1:2], warm[:, 0:1], ACT.Exp)
                for g in range(4):
                    if g < 3:
                        act.wait_ge(v_done, g + 1)
                    else:
                        act.wait_ge(chunk_used, C_KVUP + N_KVUP)
                    nc.scalar.activation(v_sb[:, g // 2, (g % 2) * HALF:(g % 2 + 1) * HALF], bank[g][:, :],
                                         ACT.Copy).then_inc(v_copied, 1)

                def qT_act(u):
                    act.wait_ge(qT_done, u + 1)
                    nc.scalar.activation(qT[:, 2 * u:2 * u + 2, :],
                                         bank[4 + u % 2][0:QD, :].rearrange("p (a s) -> p a s", a=2),
                                         ACT.Copy).then_inc(qT_copied, 1)

                def exp_act(i):
                    act.wait_ge(max_ready, i + 1)
                    for t in range(TT):
                        s = prob(i, 0, P) if t == 0 else prob(i, P, 3 * P)
                        nc.scalar.activation(s, s, ACT.Exp, bias=nmax[:, i % PB, t:t + 1],
                                             accum_out=psum_[:, i % PB, t:t + 1]).then_inc(exp_done, 1)

                def probT_act(i):
                    act.wait_ge(probT_done, i + 1)
                    if i >= PT:
                        act.wait_ge(pv_done, i - PT + 1)
                    nc.scalar.activation(probT[:, i % PT, :], bank[2 + i % 2][:, 0:3 * P], ACT.Copy
                                         ).then_inc(probT_copied, 1)

                def o_act(u):
                    act.wait_ge(pv_done, 2 * u + 2)
                    nc.scalar.activation(hnT_hi[:, u, :], bank[4 + u % 2][:, 0:SEQ], ACT.Copy
                                         ).then_inc(oT_hi_ready, 1)

                for u in range(HEADS // 2 - 1):
                    qT_act(u)
                exp_act(0)
                qT_act(HEADS // 2 - 1)
                exp_act(1)
                exp_act(2)
                for i in range(HEADS):
                    probT_act(i)
                    if 0 <= i - SPLIT_AT < 8:
                        split_hi_quarter(C_O + 1 + (i - SPLIT_AT) // 4, (i - SPLIT_AT) % 4)
                    if i + 3 < HEADS:
                        exp_act(i + 3)
                    if i % 2 == 0 and i >= 2:
                        o_act(i // 2 - 1)
                o_act(HEADS // 2 - 1)
                split_hi(C_O + 3)
                warm_sqrt()
                split_hi(C_FFN)

            @block.vector
            def _(dve):
                for t in range(TT):
                    norm_dve(0, t)
                split_lo(0)
                for t in range(TT):
                    transpose_dve(0, 0, t)
                for c in range(1, 3):
                    split_lo(c)
                split_lo(3)
                dve.wait_ge(small_loaded, 48)
                dve_link(nc.vector.tensor_copy(posf[:], pos_i[:]))
                dve.wait_ge(const_ready, 3)
                for t in range(TT):
                    last = nc.vector.tensor_scalar(ang[:, t, :], freq[:], posf[:, t:t + 1], None, ALU.mult)
                dve_link(last)
                magic = 1.5 * 2.0 ** 23
                two_pi = 2 * np.pi
                p1 = 6.28125
                p2 = float(np.float32(np.round((two_pi - p1) * 2 ** 20) / 2 ** 20))
                p3 = float(np.float32(two_pi - p1 - p2))
                dve_link(nc.vector.tensor_scalar(absr[:], ang[:], float(1 / two_pi), magic, ALU.mult, ALU.add))
                dve_link(nc.vector.tensor_scalar(absr[:], absr[:], -magic, None, ALU.add))
                dve_link(nc.vector.scalar_tensor_tensor(turns[:], absr[:], -p1, ang[:], ALU.mult, ALU.add))
                dve_link(nc.vector.scalar_tensor_tensor(ang[:], absr[:], -p2, turns[:], ALU.mult, ALU.add))
                dve_link(nc.vector.scalar_tensor_tensor(turns[:], absr[:], -p3, ang[:], ALU.mult, ALU.add))
                nc.vector.tensor_scalar(turns[:], turns[:], float(np.float32(np.pi)), -float(np.float32(np.pi)),
                                        ALU.min, ALU.max).then_inc(red_ready, 1)
                split_lo(4)
                dve.wait_ge(cq_done, 1)
                for t in range(TT):
                    nc.vector.tensor_tensor(cqv[:, t, 0:QL], bank[4 + t][:, 0:QL], qg[:], ALU.mult
                                            ).then_inc(cn_ready, 1)

                def cT_dve(b):
                    dve.wait_ge(cT_hi_ready, b + 1)
                    k0, n, bk = CT[b]
                    nc.vector.tensor_tensor(cT_lo[:, k0:k0 + n, :],
                                            bank[bk][:, 0:n * SEQ].rearrange("p (j s) -> p j s", j=n),
                                            cT_hi[:, k0:k0 + n, :].bitcast(F32), ALU.subtract
                                            ).then_inc(cT_lo_ready, 1)

                cT_dve(0)
                cT_dve(1)
                dve.wait_ge(cq_squared, 2 * TT)
                sv = ss[:, :].rearrange("p (t a) -> p a t", a=2)
                nc.vector.tensor_scalar(sv[:, 0, :], sv[:, 0, :], 1.0 / QL, EPS, ALU.mult, ALU.add)
                nc.vector.tensor_scalar(sv[:, 1, :], sv[:, 1, :], 1.0 / KVL, EPS, ALU.mult, ALU.add
                                        ).then_inc(cq_ms, 1)
                dve.wait_ge(cq_rms, 1)
                nc.vector.reciprocal(rstd[:], rms[:]).then_inc(rc_ready, 1)
                dve.wait_ge(rc_ready, 1)
                for t in range(TT):
                    nc.vector.scalar_tensor_tensor(cqv[:, t, QL:QL + KVL], bank[6 + t][:, 0:KVL],
                                                   rstd[:, 2 * t + 1:2 * t + 2], kvg[:], ALU.mult, ALU.mult
                                                   ).then_inc(cn_ready, 1)
                dve.wait_ge(trig_ready, 2)

                def rotate(dst, src, t, n):
                    hf = ROPE // 2
                    c = cos[:, t, :].unsqueeze(1).broadcast_to([P, n, hf])
                    s = sin[:, t, :].unsqueeze(1).broadcast_to([P, n, hf])
                    x1, x2 = src[:, :, 0:hf], src[:, :, hf:ROPE]
                    tmp = [rot[:, j, 0:n * hf].rearrange("p (a b) -> p a b", a=n) for j in range(4)]
                    nc.vector.tensor_tensor(tmp[0], x1, c, ALU.mult)
                    nc.vector.tensor_tensor(tmp[1], x2, s, ALU.mult)
                    nc.vector.tensor_tensor(tmp[2], x2, c, ALU.mult)
                    dve_link(nc.vector.tensor_tensor(tmp[3], x1, s, ALU.mult))
                    nc.vector.tensor_tensor(dst[:, :, 0:hf], tmp[0], tmp[1], ALU.subtract)
                    return nc.vector.tensor_tensor(dst[:, :, hf:ROPE], tmp[2], tmp[3], ALU.add)

                for t in range(TT):
                    kr = bank[6 + t][:, KVL:KVL + ROPE].rearrange("p (a b) -> p a b", a=1)
                    last = rotate(krp[:, t:t + 1, NOPE:QD], kr, t, 1)
                    if t + 1 < TT:
                        dve_link(last)
                last.then_inc(krp_ready, 1)
                split_lo(5)
                split_lo(6)
                cT_dve(2)
                split_lo(7)
                dve.wait_ge(chunk_used, C_QUP + N_QUP)
                for n in range(3):
                    nc.vector.tensor_scalar(q_sb[:, 1, n * HALF:(n + 1) * HALF], bank[2 * n + 1][:, :],
                                            rstd[:, 2:3], None, ALU.mult).then_inc(q_copied, 1)
                dve.wait_ge(q_copied, 6)
                for t in range(TT):
                    part = q_sb[:, t, :].rearrange("p (a b) -> p a b", a=HEADS)[:, :, NOPE:QD]
                    last = rotate(part, part, t, HEADS)
                    if t + 1 < TT:
                        dve_link(last)
                last.then_inc(q_roped, 1)
                for j in range(4):
                    split_lo_quarter(C_O, j, j + 1)

                def mask_dve(i):
                    dve.wait_ge(score_done, i + 1)
                    if i == 0:
                        dve.wait_ge(const_ready, 5)
                    if i == 3:
                        dve.wait_ge(qT_done, HEADS // 2)
                    if i >= PB:
                        dve.wait_ge(probT_done, i - PB + 1)
                    nc.vector.scalar_tensor_tensor(prob(i, 0, 3 * P), bank[SB[i % 3]][:, 0:3 * P],
                                                   float(np.float32(QD ** -0.5)), mask[:],
                                                   ALU.mult, ALU.add).then_inc(masked, 1)

                def max_dve(i):
                    dve.wait_ge(masked, i + 1)
                    nc.vector.tensor_reduce(nmax[:, i % PB, 0:1], prob(i, 0, P), AX.X, ALU.max, negate=True)
                    nc.vector.tensor_reduce(nmax[:, i % PB, 1:2], prob(i, P, 3 * P), AX.X, ALU.max,
                                            negate=True).then_inc(max_ready, 1)

                def rcp_dve(i):
                    dve.wait_ge(exp_done, TT * (i + 1))
                    nc.vector.reciprocal(prcp[:, i % PB, :], psum_[:, i % PB, :]).then_inc(rcp_done, 1)

                def probs_dve(i):
                    dve.wait_ge(rcp_done, i + 1)
                    for t in range(TT):
                        s = prob(i, 0, P) if t == 0 else prob(i, P, 3 * P)
                        last = nc.vector.tensor_scalar(s, s, prcp[:, i % PB, t:t + 1], None, ALU.mult)
                    last.then_inc(prob_ready, 1)

                def o_dve(u):
                    dve.wait_ge(oT_hi_ready, u + 1)
                    nc.vector.tensor_tensor(hnT_lo[:, u, :], bank[4 + u % 2][:, 0:SEQ],
                                            hnT_hi[:, u, :].bitcast(F32), ALU.subtract
                                            ).then_inc(oT_lo_ready, 1)

                for i in range(2):
                    mask_dve(i)
                    max_dve(i)
                for i in range(-1, HEADS):
                    if i + 1 < HEADS:
                        rcp_dve(i + 1)
                    if i + 3 < HEADS:
                        mask_dve(i + 3)
                    if i + 1 < HEADS:
                        probs_dve(i + 1)
                    if i + 3 < HEADS:
                        max_dve(i + 3)
                    if 0 <= i - SPLIT_AT < 8:
                        c, j = divmod(i - SPLIT_AT, 4)
                        split_lo_quarter(C_O + 1 + c, j, 3 * (1 + c) + j + 1)
                    if i % 2 and i >= 3:
                        o_dve(i // 2 - 1)
                o_dve(HEADS // 2 - 1)
                split_lo(C_O + 3)
                split_lo(C_FFN)
                residual_and_norm_dve(0, C_O + N_O - 1, C_FFN + 1)

            @block.tensor
            def _(pe):
                pe.wait_ge(const_ready, 2)
                transpose_pe(0, 0, 0)
                transpose_pe(0, 0, 1)
                for c, (k0, k1) in enumerate(IN_ROWS):
                    chunk_here(C_IN + c)

                    def latents(t, part):
                        n0, n1 = ((0, QL), (QL, MLA_IN))[part]
                        transposed(0, t, (k1 - 1) // 4)
                        for kt in range(k0, k1):
                            last = mm3(bank[4 + 2 * part + t][:, 0:n1 - n0], tok(hnT, kt, t),
                                       weights(c, kt - k0, n0, n1, MLA_IN), kt == 0, kt == KD - 1)
                        return last

                    if c < N_IN - 1:
                        for t in range(TT):
                            for part in range(2):
                                last = latents(t, part)
                    else:
                        for part in range(2):
                            for t in range(TT):
                                last = latents(t, part)
                            if part == 0:
                                last.then_inc(cq_done, 1)
                    last.then_inc(chunk_used, 1)

                def c_transposes(b):
                    k0, n, bk = CT[b]
                    for j in range(n):
                        for t in range(TT):
                            last = nc.tensor.transpose(bank[bk][:, j * SEQ + t * P:j * SEQ + (t + 1) * P],
                                                       cqv[:, t, (k0 + j) * P:(k0 + j + 1) * P], ident[:])
                    last.then_inc(cT_done, 1)

                pe.wait_ge(cn_ready, TT)
                c_transposes(0)
                c_transposes(1)
                cT = (cT_hi, cT_lo)
                for c in range(N_QUP):
                    chunk_here(C_QUP + c)
                    if c == 0:
                        pe.wait_ge(cT_lo_ready, 2)
                        pe.wait_ge(cq_squared, TT)
                    if c == 2:
                        pe.wait_ge(cn_ready, 2 * TT)
                        pe.wait_ge(krp_ready, 1)
                        c_transposes(2)
                        for t in range(TT):
                            last = nc.tensor.transpose(bank[7][0:QD, t * P:(t + 1) * P], krp[:, t, :], ident[:])
                        last.then_inc(krT_done, 1)
                    for t in range(TT):
                        for n in range(3):
                            last = mm3(bank[2 * n + t][:, :], tok(cT, c, t),
                                       weights(C_QUP + c, 0, n * HALF, (n + 1) * HALF, HEADS * QD),
                                       c == 0, c == N_QUP - 1)
                        if (c, t) == (2, 0):
                            last.then_inc(q_done, 1)
                    last.then_inc(chunk_used, 1)
                chunk_here(C_KVUP + 1)
                pe.wait_ge(cT_lo_ready, 3)
                for u in range(HEADS // 2):
                    if u == 1:
                        pe.wait_ge(krT_ready, 1)
                    if u >= 2:
                        pe.wait_ge(kn_copied, u - 1)
                    for a in range(2):
                        for k in range(N_KVUP):
                            wk = weights(C_KVUP + k, 0, (2 * u + a) * P, (2 * u + a + 1) * P, 0)
                            last = mm3(bank[6 + u % 2][:, a * SEQ:(a + 1) * SEQ], wk,
                                       (cT_hi[:, 3 + k, :], cT_lo[:, 3 + k, :]), k == 0, k == N_KVUP - 1)
                    last.then_inc(kn_done, 1)
                pe.wait_ge(q_copied, 6)
                for t in range(TT):
                    for n in range(2):
                        for k in range(N_KVUP):
                            wv = [x[:, (C_KVUP + k) % SPLIT, n * 1024:(n + 1) * 1024].rearrange(
                                "p (a b) -> p a b", a=8)[:, :, NOPE:NOPE + VD] for x in (w_hi, w_lo)]
                            last = mm3(bank[2 * t + n][:, :].rearrange("p (a b) -> p a b", a=8),
                                       tok(cT, 3 + k, t), wv, k == 0, k == N_KVUP - 1)
                        if (t, n) != (1, 1):
                            last.then_inc(v_done, 1)
                last.then_inc(chunk_used, 2)
                def scores(i):
                    if i >= 3:
                        pe.wait_ge(masked, i - 2)
                    sbank = bank[SB[i % 3]]
                    nc.tensor.matmul(sbank[:, 0:P], qT[:, i, 0:P], kT[:, i, 0:P], start=True, stop=True)
                    nc.tensor.matmul(sbank[:, P:3 * P], qT[:, i, P:SEQ], kT[:, i, :],
                                     start=True, stop=True).then_inc(score_done, 1)

                def prob_transposes(i):
                    pe.wait_ge(prob_ready, i + 1)
                    if i >= 2:
                        pe.wait_ge(probT_copied, i - 1)
                    for j in range(3):
                        last = nc.tensor.transpose(bank[2 + i % 2][:, j * P:(j + 1) * P],
                                                   prob(i, j * P, (j + 1) * P), ident[:])
                    last.then_inc(probT_done, 1)

                def values(i):
                    pe.wait_ge(probT_copied, i + 1)
                    u, r = i // 2, (i % 2) * VD
                    if i % 2 == 0 and u >= 2:
                        pe.wait_ge(oT_lo_ready, u - 1)
                    ob = bank[4 + u % 2]
                    nc.tensor.matmul(ob[r:r + VD, 0:SEQ], v_sb[:, 0, i * VD:(i + 1) * VD],
                                     probT[:, i % PT, 0:SEQ], start=True, stop=False)
                    nc.tensor.matmul(ob[r:r + VD, P:SEQ], v_sb[:, 1, i * VD:(i + 1) * VD],
                                     probT[:, i % PT, SEQ:3 * P], start=False, stop=True).then_inc(pv_done, 1)

                pe.wait_ge(q_roped, 1)
                for u in range(HEADS // 2):
                    if u >= 2:
                        pe.wait_ge(qT_copied, u - 1)
                    for a in range(2):
                        for t in range(TT):
                            col = (2 * u + a) * QD
                            last = nc.tensor.transpose(
                                bank[4 + u % 2][0:QD, a * SEQ + t * P:a * SEQ + (t + 1) * P],
                                q_sb[:, t, col:col + QD], ident[:])
                    last.then_inc(qT_done, 1)
                    if u == HEADS // 2 - 3:
                        pe.wait_ge(kr_spread, 1)
                        pe.wait_ge(kn_copied, HEADS // 2)
                        pe.wait_ge(v_copied, 4)
                    if u >= HEADS // 2 - 3:
                        scores(u - (HEADS // 2 - 3))
                pe.wait_ge(qT_copied, HEADS // 2)
                for i in range(HEADS):
                    prob_transposes(i)
                    if i + 3 < HEADS:
                        scores(i + 3)
                    if i:
                        values(i - 1)
                def o_here(q, t):
                    if (q, t) == (0, 1):
                        values(HEADS - 1)
                    pe.wait_ge(oT_lo_ready, 2 * q + 2)

                pe.wait_ge(masked, HEADS)
                out_proj_pe(C_O, N_O, hnT, 1, o_here)

        ph = ExitStack()
        with ph:
            hidT_hi = sb("hidT_hi", [P, 4 * FB, SEQ], F32R, where=ph)
            hidT_lo = sb("hidT_lo", [P, 4 * FB, SEQ], F32R, where=ph)
            silu = sb("silu", [P, TT, HALF], where=ph)
            hid = sb("hid", [P, TT, HALF], where=ph)
            silu_ready = sem("silu_ready")
            hid_ready = sem("hid_ready")
            hidT_done = sem("hidT_done")
            hidT_hi_ready = sem("hidT_hi_ready")
            hidT_lo_ready = sem("hidT_lo_ready")

            @block.sync
            def _(sp):
                for c in range(C_FFN + RAW + AHEAD + 1, C_HG + RAW + AHEAD + 1):
                    load_chunk(c)

            @block.scalar
            def _(act):
                load_gain(2, "mix_norm", 1)
                norm_and_transpose_act(1, C_FFN + 1)
                act.wait_ge(rt_loaded, 16)
                nc.scalar.activation(rt[:, :, 0, :], rt_raw[:], ACT.Copy).then_inc(rt_hi_ready, 1)
                split_hi(C_FFN + 2)

                def silu_act(b):
                    act.wait_ge(chunk_used, C_FFN + 4 * b + 2)
                    if b:
                        act.wait_ge(hid_ready, TT * b)
                    for t in range(TT):
                        nc.scalar.activation(silu[:, t, :], bank[t][:, :], ACT.Silu).then_inc(silu_ready, 1)

                def hid_act(b):
                    for t in range(TT):
                        act.wait_ge(hidT_done, TT * b + t + 1)
                        nc.scalar.activation(hidT_hi[:, 4 * b:4 * b + 4, t * P:(t + 1) * P], bank4(4 + t),
                                             ACT.Copy).then_inc(hidT_hi_ready, 1)

                for b in range(FB):
                    split_hi(C_FFN + 4 * b + 3)
                    silu_act(b)
                    if b:
                        hid_act(b - 1)
                    for c in range(4, 7):
                        split_hi(C_FFN + 4 * b + c)
                hid_act(FB - 1)
                for c in range(C_DOWN + 3, C_HG):
                    split_hi(c)
                warm_sqrt()
                split_hi(C_HG)

            @block.vector
            def _(dve):
                split_lo(C_FFN + 2)
                dve.wait_ge(rt_hi_ready, 1)
                nc.vector.tensor_tensor(rt[:, :, 1, :], rt_raw[:], rt[:, :, 0, :].bitcast(F32), ALU.subtract
                                        ).then_inc(rt_lo_ready, 1)

                def hid_dve(b):
                    for t in range(TT):
                        dve.wait_ge(silu_ready, TT * b + t + 1)
                        dve.wait_ge(chunk_used, C_FFN + 4 * b + 4)
                        if b:
                            dve.wait_ge(hidT_done, TT * (b - 1) + t + 1)
                        nc.vector.tensor_tensor(hid[:, t, :], silu[:, t, :], bank[2 + t][:, :],
                                                ALU.mult).then_inc(hid_ready, 1)

                def hidT_dve(b):
                    for t in range(TT):
                        dve.wait_ge(hidT_hi_ready, TT * b + t + 1)
                        part = slice(4 * b, 4 * b + 4), slice(t * P, (t + 1) * P)
                        nc.vector.tensor_tensor(hidT_lo[:, part[0], part[1]], bank4(4 + t),
                                                hidT_hi[:, part[0], part[1]].bitcast(F32),
                                                ALU.subtract).then_inc(hidT_lo_ready, 1)

                for b in range(FB):
                    split_lo(C_FFN + 4 * b + 3)
                    if b:
                        hidT_dve(b - 1)
                    split_lo(C_FFN + 4 * b + 4)
                    split_lo(C_FFN + 4 * b + 5)
                    hid_dve(b)
                    split_lo(C_FFN + 4 * b + 6)
                hidT_dve(FB - 1)
                for c in range(C_DOWN + 3, C_HG + 1):
                    split_lo(c)
                residual_and_norm_dve(1, C_HG - 1, C_HG + 1)

            @block.tensor
            def _(pe):
                def stream(c0, b0):
                    for q in range(2):
                        chunk_here(c0 + q)
                        for t in range(TT):
                            for k in range(4):
                                kt = 4 * q + k
                                last = mm3(bank[b0 + t][:, :], tok(hnT, kt, t),
                                           weights(c0 + q, k, 0, HALF, HALF), kt == 0, kt == KD - 1)
                        last.then_inc(chunk_used, 1)

                def transposes(b):
                    for t in range(TT):
                        pe.wait_ge(hid_ready, TT * b + t + 1)
                        if b:
                            pe.wait_ge(hidT_lo_ready, TT * (b - 1) + t + 1)
                        for j in range(4):
                            last = nc.tensor.transpose(bank[4 + t][:, j * P:(j + 1) * P],
                                                       hid[:, t, j * P:(j + 1) * P], ident[:])
                        last.then_inc(hidT_done, 1)

                for b in range(FB):
                    if b == 0:
                        first_block_pe(C_FFN, 1)
                    else:
                        pe.wait_ge(silu_ready, TT * b)
                        stream(C_FFN + 4 * b, 0)
                        transposes(b - 1)
                        pe.wait_ge(hid_ready, TT * b)
                    stream(C_FFN + 4 * b + 2, 2)

                def rows_here(q, t):
                    if q == 0:
                        if t == 0:
                            pe.wait_ge(silu_ready, TT * FB)
                        else:
                            pe.wait_ge(hid_ready, TT * FB)
                    if q % 2 == 0:
                        pe.wait_ge(hidT_lo_ready, TT * (q // 2 + 1))

                out_proj_pe(C_DOWN, 2 * FB, (hidT_hi, hidT_lo), 2, rows_here,
                            lambda q: transposes(FB - 1) if q == 0 else None)

        ph = ExitStack()
        with ph:
            AB = 3
            qd = sb("qd", [P, HG, SEQ], where=ph)
            kf = sb("kf", [P, HG, SEQ], where=ph)
            g1 = sb("g1", [P, HG, SEQ], where=ph)
            g2 = sb("g2", [P, HG, SEQ], where=ph)
            g3 = sb("g3", [P, HG, SEQ], where=ph)
            v = sb("v", [P, TT, D], where=ph)
            sg = sb("sg", [P, TT, D], where=ph)
            att = sb("att", [P, AB, SEQ], where=ph)
            state = sb("state", [P, AB, 3, DK], where=ph)
            amask = sb("amask", [P, SEQ], where=ph)
            half_lo = sb("half_lo", [P, 1], where=ph)
            half_hi = sb("half_hi", [P, 1], where=ph)
            smask = sb("smask", [P, SEQ], where=ph)
            ogain = sb("ogain", [P, DK], where=ph)
            lbs = sb("lbs", [P, 2, HG], where=ph)
            lbt = sb("lbt", [P, 2, HG], where=ph)
            lbm = sb("lbm", [P, HG], where=ph)
            lb = sb("lb", [P, HG], where=ph)
            oml = sb("oml", [P, HG], where=ph)
            dec = sb("dec", [P, HG * SEQ // CH], where=ph)
            oss = sb("oss", [P, HG, TT], where=ph)
            kd_even = kf[:, :, :].rearrange("p a s -> p (a s)").rearrange("p (t n) -> p t n", t=TT)
            kd_odd = g2[:, :, :].rearrange("p a s -> p (a s)").rearrange("p (t n) -> p t n", t=TT)
            o_sb = hn
            NC_ = SEQ // CH
            TOKEN_BANK = {0: 0, 5: 4, 6: 6, 7: 4}

            hg_loaded = sem("hg_loaded")
            hg_const = sem("hg_const")
            k_ready = sem("k_ready")
            sg_ready = sem("sg_ready")
            lbd_ready = sem("lbd_ready")
            lbe_ready = sem("lbe_ready")
            fq_copied = sem("fq_copied")
            vg_copied = sem("vg_copied")
            f_ready = sem("f_ready")
            logf_ready = sem("logf_ready")
            b_ready = sem("b_ready")
            eb_ready = sem("eb_ready")
            qd_ready = sem("qd_ready")
            enb_ready = sem("enb_ready")
            bl_ready = sem("bl_ready")
            ebl_ready = sem("ebl_ready")
            dec_ready = sem("dec_ready")
            kd_ready = sem("kd_ready")
            kdec_ready = sem("kdec_ready")
            kdT_done = sem("kdT_done")
            kdT_copied = sem("kdT_copied")
            a_done = sem("a_done")
            a_ready = sem("a_ready")
            kv_done = sem("kv_done")
            state0_ready = sem("state0_ready")
            state1_ready = sem("state1_ready")
            state_ready = sem("state_ready")
            orcp_done = sem("orcp_done")
            o_done = sem("o_done")
            o_squared = sem("o_squared")
            oms_ready = sem("oms_ready")
            orms_ready = sem("orms_ready")
            on_ready = sem("on_ready")
            ohT_done = sem("ohT_done")
            ohT_hi_ready = sem("ohT_hi_ready")
            ohT_lo_ready = sem("ohT_lo_ready")

            @block.sync
            def _(sp):
                for c in range(C_HG + RAW + AHEAD + 1, C_MOE):
                    load_chunk(c)
                for k in range(RAW + AHEAD + 1):
                    load_chunk(C_MOE + k, item_dram(k, 0))

            @block.gpsimd
            def _(pool):
                pool.wait_ge(h_added, 8)
                for tile, value in ((smask, 1.0), (half_lo, 0.0), (half_hi, 0.0), (att, 0.0), (amask, 1.0)):
                    pool_link(nc.gpsimd.memset(tile[:], value))
                pool_link(nc.gpsimd.memset(smask[:, :].rearrange("p (a b) -> p a b", a=NC_)[:, :, 0:1], 0.0))
                pool_link(nc.gpsimd.memset(half_lo[0:CH, :], 1.0))
                pool_link(nc.gpsimd.memset(half_hi[CH:P, :], 1.0))
                for t in range(TT):
                    part = amask[:, t * P:(t + 1) * P]
                    pool_link(nc.gpsimd.affine_select(out=part, in_=part, compare_op=ALU.is_ge, fill=0.0,
                                                      base=0, pattern=[[1, P]], channel_multiplier=-1))
                    pool_link(nc.gpsimd.memset(amask[0:CH, t * P + CH:(t + 1) * P], 0.0))
                nc.gpsimd.memset(half_lo[0:CH, :], 1.0).then_inc(hg_const, 1)

            @block.scalar
            def _(act):
                load_gain(3, "ffn_norm", 1)
                norm_and_transpose_act(2, C_HG + 1)
                nc.scalar.dma_start(ogain[:], w["hgrn_out_norm"].broadcast_to([P, DK])).then_inc(hg_loaded, 16)
                for l in range(2):
                    nc.scalar.dma_start(lbs[:, l, :], w["hgrn_lower_bounds"][l:l + 1, :].rearrange(
                        "l (a p) -> p (l a)", p=P), allow_slow_non_contiguous=True).then_inc(hg_loaded, 16)
                split_hi(C_HG + 2)
                act.wait_ge(lbd_ready, 1)
                nc.scalar.activation(lbs[:], lbt[:], ACT.Exp).then_inc(lbe_ready, 1)

                def evacuate(B):
                    act.wait_ge(chunk_used, C_HG + 2 * B + 2)
                    if 1 <= B <= 4:
                        for a in range(4):
                            dst = (kf if B < 3 else qd)[:, 4 * ((B - 1) % 2) + a, :]
                            src = bank[4 * (B % 2) + a][:, 0:SEQ]
                            if B < 3:
                                nc.scalar.activation(dst, src, ACT.Sigmoid).then_inc(fq_copied, 1)
                            else:
                                nc.scalar.activation(dst, src, ACT.Copy, scale=float(np.float32(DK ** -0.5))
                                                     ).then_inc(fq_copied, 1)
                    else:
                        n = B % 2
                        for t in range(TT):
                            dst = (v if B < 6 else sg)[:, t, n * HALF:(n + 1) * HALF]
                            nc.scalar.activation(dst, bank[TOKEN_BANK[B] + t][:, :],
                                                 ACT.Copy if B < 6 else ACT.Silu).then_inc(vg_copied, 1)

                for B in range(8):
                    if B < 7:
                        split_hi(C_HG + 2 * B + 3)
                    if B == 3:
                        act.wait_ge(f_ready, 1)
                        nc.scalar.activation(g1[:], kf[:], ACT.Ln).then_inc(logf_ready, 1)
                    if B == 4:
                        act.wait_ge(b_ready, 1)
                        nc.scalar.activation(g1[:], g2[:], ACT.Exp).then_inc(eb_ready, 1)
                    if B == 5:
                        act.wait_ge(bl_ready, 1)
                        nc.scalar.activation(g3[:], g3[:], ACT.Exp).then_inc(ebl_ready, 1)
                        last_b = g2[:, :, :].rearrange("p a s -> p (a s)").rearrange(
                            "p (n c) -> p n c", c=CH)[:, :, CH - 1]
                        nc.scalar.activation(dec[:], last_b, ACT.Exp).then_inc(dec_ready, 1)
                    if B == 6:
                        act.wait_ge(qd_ready, 1)
                        nc.scalar.activation(g1[:], g2[:], ACT.Exp, scale=-1.0).then_inc(enb_ready, 1)
                    if B == 7:
                        act.wait_ge(kd_ready, 1)
                        act.wait_ge(dec_ready, 1)
                        for t in range(TT):
                            for g in range(2):
                                act.wait_ge(kdT_done, 2 * t + g + 1)
                                nc.scalar.activation(kd_even[:, t, g * HALF:(g + 1) * HALF],
                                                     bank[2 * t + g][:, :], ACT.Copy, scale=half_lo[:]
                                                     ).then_inc(kdT_copied, 1)
                                if t == 0:
                                    nc.scalar.activation(kd_odd[:, t, g * HALF:(g + 1) * HALF],
                                                         bank[2 * t + g][:, :], ACT.Copy, scale=half_hi[:]
                                                         ).then_inc(kdT_copied, 1)
                        split_hi(C_HG + 2 * B + 3)
                    evacuate(B)
                    if B == 7:
                        warm_sqrt()
                    else:
                        split_hi(C_HG + 2 * B + 4)
                def state_act(i):
                    act.wait_ge(kv_done, i + 1)
                    if i >= AB:
                        act.wait_ge(o_done, i - AB + 1)
                    nc.scalar.activation(state[:, i % AB, 0, :], bank[2 + i % 2][:, 0:DK], ACT.Copy
                                         ).then_inc(state0_ready, 1)

                state_act(0)
                state_act(1)
                for i in range(HG + 2):
                    if i < HG:
                        act.wait_ge(o_done, i + 1)
                        for t in range(TT):
                            nc.scalar.activation(o_sb[:, t, i * DK:(i + 1) * DK], bank[4 + i % 2][:, t * DK:(t + 1) * DK], ACT.Square,
                                                 accum_out=oss[:, i, t:t + 1]).then_inc(o_squared, 1)
                        act.wait_ge(oms_ready, i + 1)
                        nc.scalar.activation(oss[:, i, :], oss[:, i, :], ACT.Sqrt).then_inc(orms_ready, 1)
                    if i + 2 < HG:
                        state_act(i + 2)
                    if HG - 1 <= i < HG + 1:
                        split_hi(C_HGO + 2 + i - (HG - 1))
                    if i >= 2:
                        act.wait_ge(ohT_done, i - 1)
                        nc.scalar.activation(hnT_hi[:, i - 2, :], bank[6 + i % 2][:, 0:SEQ], ACT.Copy
                                             ).then_inc(ohT_hi_ready, 1)
                split_hi(C_MOE)

            @block.vector
            def _(dve):
                split_lo(C_HG + 2)
                dve.wait_ge(hg_loaded, 48)
                dve_link(nc.vector.tensor_tensor(lbm[:], lbs[:, 0, :], lbs[:, 1, :], ALU.max))
                nc.vector.tensor_tensor(lbt[:, 0, :], lbs[:, 0, :], lbm[:], ALU.subtract)
                nc.vector.tensor_tensor(lbt[:, 1, :], lbs[:, 1, :], lbm[:], ALU.subtract).then_inc(lbd_ready, 1)
                dve.wait_ge(lbe_ready, 1)
                dve_link(nc.vector.tensor_tensor(lbm[:], lbs[:, 0, :], lbs[:, 1, :], ALU.add))
                dve_link(nc.vector.reciprocal(lbm[:], lbm[:]))
                nc.vector.tensor_tensor(lbt[:, 0, :], lbs[:, 0, :], lbm[:], ALU.mult)
                dve_link(nc.vector.tensor_tensor(lbt[:, 1, :], lbs[:, 1, :], lbm[:], ALU.mult))
                dve_link(nc.vector.tensor_tensor(lb[:], lbt[:, 0, :], lbt[:, 1, :], ALU.add))
                dve_link(nc.vector.tensor_tensor(lb[:], lb[:], lbt[:, 0, :], ALU.subtract))
                dve_link(nc.vector.tensor_scalar(oml[:], lb[:], -1.0, 1.0, ALU.mult, ALU.add))
                dve.wait_ge(hg_const, 1)

                def gate_gain(n, t):
                    part = sg[:, t, n * HALF:(n + 1) * HALF].rearrange("p (a n) -> p a n", n=DK)
                    nc.vector.tensor_tensor(
                        part, part, ogain[:, :].unsqueeze(1).broadcast_to([P, HALF // DK, DK]), ALU.mult
                    ).then_inc(sg_ready, 1)

                for B in range(8):
                    if B == 7:
                        dve.wait_ge(vg_copied, 6)
                        gate_gain(0, 0)
                        gate_gain(0, 1)
                    split_lo(C_HG + 2 * B + 3)
                    if B == 2:
                        dve.wait_ge(fq_copied, 8)
                        for a in range(HG):
                            last = nc.vector.tensor_scalar(kf[:, a, :], kf[:, a, :], oml[:, a:a + 1],
                                                           lb[:, a:a + 1], ALU.mult, ALU.add)
                        last.then_inc(f_ready, 1)
                    if B == 3:
                        dve.wait_ge(logf_ready, 1)
                        for a in range(HG):
                            last = nc.vector.tensor_tensor_scan(g2[:, a, :], smask[:], g1[:, a, :], 0.0,
                                                                ALU.mult, ALU.add)
                        last.then_inc(b_ready, 1)
                        nc.vector.tensor_scalar(kf[:], kf[:], -1.0, 1.0, ALU.mult, ALU.add
                                                ).then_inc(k_ready, 1)
                    if B == 4:
                        dve.wait_ge(b_ready, 1)
                        bv = g2[:, :, :].rearrange("p a s -> p (a s)").rearrange("p (n c) -> p n c", c=CH)
                        nc.vector.tensor_tensor(
                            g3[:, :, :].rearrange("p a s -> p (a s)").rearrange("p (n c) -> p n c", c=CH),
                            bv[:, :, CH - 1:CH].broadcast_to([P, HG * NC_, CH]), bv, ALU.subtract
                        ).then_inc(bl_ready, 1)
                    if B == 5:
                        dve.wait_ge(eb_ready, 1)
                        dve.wait_ge(fq_copied, 16)
                        nc.vector.tensor_tensor(qd[:], qd[:], g1[:], ALU.mult).then_inc(qd_ready, 1)
                        dve.wait_ge(ebl_ready, 1)
                        dve.wait_ge(k_ready, 1)
                        nc.vector.tensor_tensor(g3[:], kf[:], g3[:], ALU.mult).then_inc(kdec_ready, 1)
                    if B == 6:
                        dve.wait_ge(enb_ready, 1)
                        nc.vector.tensor_tensor(g1[:], kf[:], g1[:], ALU.mult).then_inc(kd_ready, 1)
                    if B < 7:
                        split_lo(C_HG + 2 * B + 4)

                def att_dve(i):
                    dve.wait_ge(a_done, i + 1)
                    if i >= AB:
                        dve.wait_ge(o_done, i - AB + 1)
                    nc.vector.copy_predicated(att[:, i % AB, :], amask[:].bitcast(U32),
                                              bank[i % 2][:, 0:SEQ]).then_inc(a_ready, 1)

                def state_dve(i, n):
                    dve.wait_ge(state0_ready if n == 1 else state1_ready, i + 1)
                    nc.vector.scalar_tensor_tensor(
                        state[:, i % AB, n, :], state[:, i % AB, n - 1, :], dec[:, NC_ * i + n:NC_ * i + n + 1],
                        bank[2 + i % 2][:, n * DK:(n + 1) * DK], ALU.mult, ALU.add
                    ).then_inc(state1_ready if n == 1 else state_ready, 1)

                dve.wait_ge(dec_ready, 1)
                for i in range(2):
                    att_dve(i)
                    state_dve(i, 1)
                    state_dve(i, 2)
                for i in range(HG + 2):
                    if i < HG:
                        dve.wait_ge(o_squared, TT * (i + 1))
                        nc.vector.tensor_scalar(oss[:, i, :], oss[:, i, :], 1.0 / DK, EPS, ALU.mult, ALU.add
                                                ).then_inc(oms_ready, 1)
                    if i + 2 < HG:
                        att_dve(i + 2)
                    if i in (1, 3):
                        dve.wait_ge(vg_copied, 8)
                        gate_gain(1, i // 2)
                    if i < HG:
                        dve.wait_ge(orms_ready, i + 1)
                        nc.vector.reciprocal(oss[:, i, :], oss[:, i, :]).then_inc(orcp_done, 1)
                    if i + 2 < HG:
                        state_dve(i + 2, 1)
                    if i < HG:
                        dve.wait_ge(orcp_done, i + 1)
                        dve.wait_ge(sg_ready, TT * (i // 4 + 1))
                        hd = slice(i * DK, (i + 1) * DK)
                        for t in range(TT):
                            last = nc.vector.scalar_tensor_tensor(
                                o_sb[:, t, hd], bank[4 + i % 2][:, t * DK:(t + 1) * DK], oss[:, i, t:t + 1],
                                sg[:, t, hd], ALU.mult, ALU.mult)
                        last.then_inc(on_ready, 1)
                    if i + 2 < HG:
                        state_dve(i + 2, 2)
                    if HG - 1 <= i < HG + 1:
                        split_lo(C_HGO + 2 + i - (HG - 1))
                    if i >= 2:
                        dve.wait_ge(ohT_hi_ready, i - 1)
                        nc.vector.tensor_tensor(hnT_lo[:, i - 2, :], bank[6 + i % 2][:, 0:SEQ],
                                                hnT_hi[:, i - 2, :].bitcast(F32), ALU.subtract
                                                ).then_inc(ohT_lo_ready, 1)
                split_lo(C_MOE)
                residual_and_norm_dve(2, C_MOE - 1)

            @block.tensor
            def _(pe):
                first_block_pe(C_HG, 2)
                for B in range(1, 8):
                    c0 = C_HG + 2 * B
                    if B == 2:
                        pe.wait_ge(vg_copied, 2)
                    elif B >= 3:
                        pe.wait_ge(fq_copied, 4 * (B - 2) if B < 5 else 12)
                    if B == 7:
                        pe.wait_ge(kdec_ready, 1)
                        pe.wait_ge(fq_copied, 16)
                        pe.wait_ge(vg_copied, 4)
                        for t in range(TT):
                            for g in range(2):
                                for a in range(4):
                                    last = nc.tensor.transpose(bank[2 * t + g][:, a * P:(a + 1) * P],
                                                               g3[:, 4 * g + a, t * P:(t + 1) * P], ident[:])
                                last.then_inc(kdT_done, 1)
                    for q in range(2):
                        chunk_here(c0 + q)
                        for k in range(4):
                            kt = 4 * q + k
                            if B < 5:
                                for a in range(4):
                                    last = mm3(bank[4 * (B % 2) + a][:, 0:SEQ],
                                               weights(c0 + q, k, a * P, (a + 1) * P, HALF),
                                               (hnT_hi[:, kt, :], hnT_lo[:, kt, :]), kt == 0, kt == KD - 1)
                            else:
                                for t in range(TT):
                                    last = mm3(bank[TOKEN_BANK[B] + t][:, :],
                                               tok(hnT, kt, t), weights(c0 + q, k, 0, HALF, HALF),
                                               kt == 0, kt == KD - 1)
                        last.then_inc(chunk_used, 1)
                pe.wait_ge(kdT_copied, 6)
                pe.wait_ge(kd_ready, 1)
                pe.wait_ge(qd_ready, 1)

                def head_scores(i):
                    if i >= 2:
                        pe.wait_ge(a_ready, i - 1)
                        pe.wait_ge(state_ready, i - 1)
                    for t in range(TT):
                        last = nc.tensor.matmul(bank[i % 2][:, t * P:(t + 1) * P], g1[:, i, t * P:(t + 1) * P],
                                                qd[:, i, t * P:(t + 1) * P], start=True, stop=True)
                    last.then_inc(a_done, 1)
                    hd = slice(i * DK, (i + 1) * DK)
                    for n, (kd, t) in enumerate(((kd_even, 0), (kd_odd, 0), (kd_even, 1))):
                        last = nc.tensor.matmul(bank[2 + i % 2][:, n * DK:(n + 1) * DK], kd[:, t, hd], v[:, t, hd],
                                                start=True, stop=True)
                    last.then_inc(kv_done, 1)

                def head_output(i):
                    pe.wait_ge(a_ready, i + 1)
                    pe.wait_ge(state_ready, i + 1)
                    if i == 0:
                        pe.wait_ge(vg_copied, 8)
                    if i >= 2:
                        pe.wait_ge(on_ready, i - 1)
                    hd = slice(i * DK, (i + 1) * DK)
                    for t in range(TT):
                        ob = bank[4 + i % 2][:, t * DK:(t + 1) * DK]
                        nc.tensor.matmul(ob, att[:, i % AB, t * P:(t + 1) * P], v[:, t, hd], start=True, stop=True)
                        for half in range(2):
                            n = 2 * t + half
                            if n == 0:
                                continue
                            last = nc.tensor.matmul(ob[half * CH:(half + 1) * CH, :],
                                                    qd[:, i, n * CH:(n + 1) * CH], state[:, i % AB, n - 1, :],
                                                    start=False, stop=True, skip_group_check=True)
                    last.then_inc(o_done, 1)

                def head_transposes(i):
                    pe.wait_ge(on_ready, i + 1)
                    if i >= 2:
                        pe.wait_ge(ohT_lo_ready, i - 1)
                    for t in range(TT):
                        last = nc.tensor.transpose(bank[6 + i % 2][:, t * P:(t + 1) * P],
                                                   o_sb[:, t, i * DK:(i + 1) * DK], ident[:])
                    last.then_inc(ohT_done, 1)

                head_scores(0)
                head_scores(1)
                for i in range(HG):
                    head_output(i)
                    if i + 2 < HG:
                        head_scores(i + 2)
                    if i >= 2:
                        head_transposes(i - 2)
                out_proj_pe(C_HGO, 4, hnT, 3, lambda q, t: pe.wait_ge(ohT_lo_ready, 2 * q + 2),
                            lambda q: head_transposes(HG - 2 + q))

        ph = ExitStack()
        with ph:
            logit = sb("logit", [P, TT, E], where=ph)
            top = sb("top", [P, TT, 8], where=ph)
            topi = sb("topi", [P, TT, 8], U32, where=ph)
            topf = sb("topf", [P, TT, 8], where=ph)
            sel = sb("sel", [P, TT, 2, E], where=ph)
            wts = sb("wts", [P, TT, 4], where=ph)
            gates = sb("gates", [P, TT, E], where=ph)
            chosen = sb("chosen", [P, TT, E], where=ph)
            slot = sb("slot", [P, TT, E], where=ph)
            count = sb("count", [P, E], where=ph)
            over = sb("over", [P, E], where=ph)
            rank = sb("rank", [P, E], where=ph)
            scratch = sb("scratch", [P, MAX_EXTRA, E], where=ph)
            iota_e = sb("iota_e", [P, E], where=ph)
            ones_e = sb("ones_e", [P, E], where=ph)
            iota_s = sb("iota_s", [P, P], where=ph)
            before = sb("before", [P, P], where=ph)
            ones = sb("ones", [P, P], where=ph)
            shift = sb("shift", [P, 16], where=ph)
            plan_f = sb("plan_f", [P, 16], where=ph)
            plan = sb("plan", [1, 16], I32, where=ph)
            slot_i = sb("slot_i", [P, TT], where=ph)
            onehot = sb("onehot", [P, TT, P], where=ph)
            onehotT = sb("onehotT", [P, SEQ], F32R, where=ph)
            xT_hi = sb("xT_hi", [P, KD, P], F32R, where=ph)
            xT_lo = sb("xT_lo", [P, KD, P], F32R, where=ph)
            silu2 = sb("silu2", [P, 2, HALF], where=ph)
            hid2 = sb("hid2", [P, 2, HALF], where=ph)
            hT_hi = sb("hT_hi", [P, 2, 4, P], F32R, where=ph)
            hT_lo = sb("hT_lo", [P, 2, 4, P], F32R, where=ph)
            y_hi = sb("y_hi", [P, D], F32R, where=ph)
            y_lo = sb("y_lo", [P, D], F32R, where=ph)

            moe_const = sem("moe_const")
            logits_done = sem("logits_done")
            diff_ready = sem("diff_ready")
            e2_ready = sem("e2_ready")
            chosen_ready = sem("chosen_ready")
            places_done = sem("places_done")
            counts_done = sem("counts_done")
            plan_ready = sem("plan_ready")
            slot_ready = sem("slot_ready")
            onehot_ready = sem("onehot_ready")
            gathered = sem("gathered")
            xT_hi_ready = sem("xT_hi_ready")
            xT_lo_ready = sem("xT_lo_ready")
            onehotT_done = sem("onehotT_done")
            onehotT_ready = sem("onehotT_ready")
            silu2_ready = sem("silu2_ready")
            hid2_ready = sem("hid2_ready")
            hT_done = sem("hT_done")
            hT_hi_ready = sem("hT_hi_ready")
            hT_lo_ready = sem("hT_lo_ready")
            y_done = sem("y_done")
            y_hi_ready = sem("y_hi_ready")
            y_lo_ready = sem("y_lo_ready")
            scattered = sem("scattered")
            combined = sem("combined")
            out_stored = sem("out_stored")
            G, U_, T_, Y, X = (0, 1), 2, 3, (4, 5), (6, 7)
            PRIMED = 1
            TURN = 16 * PER_ITEM // RAW

            def n_items_on(eng):
                eng.wait_ge(plan_ready, 1)
                return eng.value_load(plan[0:1, 12:13], min_val=E, max_val=MAX_ITEMS)

            def last_item_on(eng):
                eng.wait_ge(plan_ready, 1)
                return eng.value_load(plan[0:1, 13:14], min_val=E - 1, max_val=MAX_ITEMS - 1)

            def expert_on(eng, i):
                return eng.value_load(plan[0:1, bass.ds(i, 1)], min_val=0, max_val=E - 1)

            @block.sync
            def _(sp):
                def load(k, i, e):
                    c = C_MOE + k
                    sp.wait_ge(lo_ready, PER_ITEM * i + (c - RAW + 1))
                    nc.sync.dma_start(w_raw[:, c % RAW, :].rearrange("p (k n) -> p k n",
                                                                     k=2 if item[k][0] == "down" else 4),
                                      item_dram(k, e)).then_inc(raw_loaded[c % RAW], 16)

                first = RAW + AHEAD + 1
                with sp.Fori(0, E - 1) as i:
                    for k in range(first, PER_ITEM):
                        load(k, i, i)
                    for k in range(first):
                        load(k, i + 1, i + 1)
                for k in range(first, PER_ITEM):
                    load(k, E - 1, E - 1)
                n = n_items_on(sp)
                with sp.If(n > E):
                    with sp.Fori(E, n) as i:
                        e = expert_on(sp, i)
                        for k in range(PER_ITEM):
                            load(k, i, e)
                for t in range(TT):
                    for g in range(2):
                        sp.wait_ge(hn_ready, 2 * (4 * TT + t) + g + 1)
                        part = slice(g * HALF, (g + 1) * HALF)
                        nc.sync.dma_start(out[0, t * P:(t + 1) * P, part], hn[:, t, part]
                                          ).then_inc(out_stored, 16)
                sp.wait_ge(out_stored, 2 * 16 * TT)

            @block.gpsimd
            def _(pool):
                pool.wait_ge(h_added, 12)
                for tile, value in ((before, 1.0), (ones, 1.0), (ones_e, 1.0), (shift, -1.0), (plan_f, 0.0)):
                    pool_link(nc.gpsimd.memset(tile[:], value))
                pool_link(nc.gpsimd.memset(shift[:, E:16], float(-1 - P)))
                pool_link(nc.gpsimd.affine_select(out=before[:], in_=before[:], compare_op=ALU.is_gt, fill=0.0,
                                                  base=0, pattern=[[1, P]], channel_multiplier=-1))
                pool_link(nc.gpsimd.iota(iota_s[:], pattern=[[1, P]], base=0, channel_multiplier=0,
                                         allow_small_or_imprecise_dtypes=True))
                nc.gpsimd.iota(iota_e[:], pattern=[[1, E]], base=0, channel_multiplier=0,
                               allow_small_or_imprecise_dtypes=True).then_inc(moe_const, 1)

            @block.scalar
            def _(act):
                load_gain(4, "final_norm", None)
                norm_and_transpose_act(3)
                split_hi(C_MOE + 1)
                split_hi(C_MOE + 2)
                act.wait_ge(diff_ready, 1)
                nc.scalar.activation(wts[:, :, 0:1], wts[:, :, 0:1], ACT.Exp).then_inc(e2_ready, 1)

                def xT_act(item_no):
                    for g in range(2):
                        act.wait_ge(gathered, 2 * item_no + (g + 1))
                        nc.scalar.activation(xT_hi[:, 4 * g:4 * g + 4, :], bank4(X[g]), ACT.Copy
                                             ).then_inc(xT_hi_ready, 1)

                act.sem_inc(silu2_ready, PRIMED)
                xT_act(0)
                last_item = last_item_on(act)

                def item_act(i, last):
                    base, turn = PER_ITEM * i, TURN * i

                    def silu_of(b):
                        act.wait_ge(chunk_used, base + (C_MOE + (2 if b == 0 else 6 * b)))
                        act.wait_ge(hid2_ready, FB * i + at_least(b - 1) + PRIMED)
                        nc.scalar.activation(silu2[:, b % 2, :], bank[G[b % 2]][:, :], ACT.Silu
                                             ).then_inc(silu2_ready, 1)

                    def hT_of(b):
                        act.wait_ge(hT_done, FB * i + (b + 1) + PRIMED)
                        if b >= 2:
                            act.wait_ge(chunk_used, base + (C_MOE + 6 * (b - 1) + 4))
                        else:
                            act.wait_ge(chunk_used, base + C_MOE)
                        nc.scalar.activation(hT_hi[:, b % 2, :, :], bank4(T_), ACT.Copy).then_inc(hT_hi_ready, 1)

                    for k in range(AHEAD + 1, PER_ITEM + AHEAD + 1):
                        if not (last and k >= PER_ITEM):
                            split_hi(C_MOE + k, base, turn)
                        if k % 6 == 1 and k > 1 and k < PER_ITEM - 1:
                            silu_of(k // 6)
                            hT_of(k // 6 - 1)
                        elif k == 3:
                            silu_of(0)
                        elif k == 9:
                            act.wait_ge(onehotT_done, i + 1)
                            act.wait_ge(scattered, 4 * i + PRIMED)
                            nc.scalar.activation(onehotT[:], bank[T_][:, 0:SEQ], ACT.Copy
                                                 ).then_inc(onehotT_ready, 1)
                        elif k == PER_ITEM - 2:
                            hT_of(FB - 1)
                        elif k == PER_ITEM - 1 and not last:
                            xT_act(i + 1)
                        elif k == PER_ITEM + 1:
                            for g in range(2):
                                if g == 0:
                                    act.wait_ge(y_done, i + 1)
                                else:
                                    act.wait_ge(chunk_used, base + (C_MOE + PER_ITEM))
                                nc.scalar.activation(y_hi[:, g * HALF:(g + 1) * HALF], bank[Y[g]][:, :], ACT.Copy
                                                     ).then_inc(y_hi_ready, 1)

                with act.Fori(0, last_item) as i:
                    item_act(i, False)
                item_act(last_item, True)
                warm_sqrt()
                for t in range(TT):
                    norm_act(4, t, lambda t, g: act.wait_ge(combined, 4 * last_item + (2 * g + t + 1) + PRIMED))

            @block.vector
            def _(dve):
                dve.wait_ge(moe_const, 1)
                dve.wait_ge(logits_done, 1)
                dve_link(nc.vector.tensor_reduce(logit[:], bank[0][:, 0:2 * TT * E].rearrange(
                    "p (t a e) -> p t e a", t=TT, a=2), AX.X, ALU.add))
                for t in range(TT):
                    last = nc.vector.max(top[:, t, :], logit[:, t, :])
                dve_link(last)
                nc.vector.tensor_tensor(wts[:, :, 0:1], top[:, :, 1:2], top[:, :, 0:1], ALU.subtract
                                        ).then_inc(diff_ready, 1)
                for t in range(TT):
                    last = nc.vector.max_index(topi[:, t, :], top[:, t, :], logit[:, t, :])
                dve_link(last)
                dve_link(nc.vector.tensor_copy(topf[:], topi[:]))
                dve_link(nc.vector.tensor_tensor(
                    sel[:], iota_e[:, :].unsqueeze(1).unsqueeze(1).broadcast_to([P, TT, 2, E]),
                    topf[:, :, 0:2].unsqueeze(3).broadcast_to([P, TT, 2, E]), ALU.is_equal))
                nc.vector.tensor_tensor(chosen[:], sel[:, :, 0, :], sel[:, :, 1, :], ALU.add
                                        ).then_inc(chosen_ready, 1)
                dve.wait_ge(places_done, 1)
                dve_link(nc.vector.scalar_tensor_tensor(slot[:], bank[1][:, 0:TT * E].rearrange(
                    "p (t e) -> p t e", t=TT), 1.0, chosen[:], ALU.add, ALU.mult))

                def onehot_of(item_no, e):
                    nc.vector.tensor_scalar(slot_i[:], slot[:, :, bass.ds(e, 1)].rearrange("p t e -> p (t e)"),
                                            shift[:, bass.ds(item_no, 1)], None, ALU.add
                                            ).then_inc(slot_ready, 1)
                    dve.wait_ge(slot_ready, item_no + 1)
                    nc.vector.tensor_scalar(onehot[:, 0, :], iota_s[:], slot_i[:, 0:1], None, ALU.is_equal)
                    nc.vector.tensor_scalar(onehot[:, 1, :], iota_s[:], slot_i[:, 1:2], None, ALU.is_equal
                                            ).then_inc(onehot_ready, 1)

                def xT_dve(item_no, halves=(0, 1)):
                    for g in halves:
                        dve.wait_ge(xT_hi_ready, 2 * item_no + (g + 1))
                        nc.vector.tensor_tensor(xT_lo[:, 4 * g:4 * g + 4, :], bank4(X[g]),
                                                xT_hi[:, 4 * g:4 * g + 4, :].bitcast(F32), ALU.subtract
                                                ).then_inc(xT_lo_ready, 1)

                onehot_of(0, 0)
                split_lo(C_MOE + 1)
                dve.wait_ge(counts_done, 1)
                dve_link(nc.vector.tensor_scalar(over[:], bank[2][:, 0:E], float(P), None,
                                                 ALU.is_gt))
                dve_link(nc.vector.tensor_tensor_scan(rank[:], ones_e[:], over[:], 0.0, ALU.mult, ALU.add))
                nc.vector.tensor_scalar(plan_f[:, 12:13], rank[:, E - 1:E], float(E), None, ALU.add)
                dve_link(nc.vector.tensor_scalar(plan_f[:, 13:14], rank[:, E - 1:E], float(E - 1), None,
                                                 ALU.add))
                dve_link(nc.vector.tensor_tensor(rank[:], rank[:], over[:], ALU.mult))
                nc.vector.tensor_copy(plan_f[:, 0:E], iota_e[:])
                shape = [P, MAX_EXTRA, E]
                dve_link(nc.vector.tensor_tensor(
                    scratch[:], rank[:, :].unsqueeze(1).broadcast_to(shape),
                    iota_e[:, 1:1 + MAX_EXTRA].unsqueeze(2).broadcast_to(shape), ALU.is_equal))
                dve_link(nc.vector.tensor_tensor(scratch[:], scratch[:],
                                                 iota_e[:, :].unsqueeze(1).broadcast_to(shape), ALU.mult))
                dve_link(nc.vector.tensor_reduce(plan_f[:, E:E + MAX_EXTRA], scratch[:], AX.X, ALU.add))
                nc.vector.tensor_copy(plan[:], plan_f[0:1, :]).then_inc(plan_ready, 1)
                last_item = last_item_on(dve)
                for primed in (hid2_ready, hT_lo_ready, y_lo_ready, combined):
                    dve.sem_inc(primed, PRIMED)
                xT_dve(0, (0,))
                split_lo(C_MOE + 2)
                xT_dve(0, (1,))
                dve.wait_ge(e2_ready, 1)
                dve_link(nc.vector.tensor_scalar(wts[:, :, 1:2], wts[:, :, 0:1], 1.0, None, ALU.add))
                dve_link(nc.vector.reciprocal(wts[:, :, 2:3], wts[:, :, 1:2]))
                dve_link(nc.vector.tensor_tensor(wts[:, :, 3:4], wts[:, :, 2:3], wts[:, :, 0:1], ALU.mult))
                for t in range(TT):
                    dve_link(nc.vector.tensor_scalar(gates[:, t, :], sel[:, t, 0, :], wts[:, t, 2:3], None,
                                                     ALU.mult))
                    dve_link(nc.vector.scalar_tensor_tensor(gates[:, t, :], sel[:, t, 1, :], wts[:, t, 3:4],
                                                            gates[:, t, :], ALU.mult, ALU.add))

                def item_dve(i, last):
                    base = PER_ITEM * i

                    def hid_of(b):
                        dve.wait_ge(silu2_ready, FB * i + (b + 1) + PRIMED)
                        dve.wait_ge(chunk_used, base + (C_MOE + (4 if b == 0 else 6 * b + 2)))
                        dve.wait_ge(hT_done, FB * i + at_least(b - 1) + PRIMED)
                        nc.vector.tensor_tensor(hid2[:, b % 2, :], silu2[:, b % 2, :], bank[U_][:, :], ALU.mult
                                                ).then_inc(hid2_ready, 1)

                    def hT_of(b):
                        dve.wait_ge(hT_hi_ready, FB * i + (b + 1))
                        nc.vector.tensor_tensor(hT_lo[:, b % 2, :, :], bank4(T_),
                                                hT_hi[:, b % 2, :, :].bitcast(F32), ALU.subtract
                                                ).then_inc(hT_lo_ready, 1)

                    for k in range(AHEAD + 1, PER_ITEM + AHEAD + 1):
                        if not (last and k >= PER_ITEM):
                            split_lo(C_MOE + k, base)
                        if k % 6 == 3 and k > 3 and k < PER_ITEM - 1:
                            hid_of(k // 6)
                        elif k == 5:
                            hid_of(0)
                        elif k % 6 == 1 and k > 1 and k < PER_ITEM - 1:
                            hT_of(k // 6 - 1)
                        elif k == 26 and not last:
                            dve.wait_ge(onehotT_done, i + 1)
                            dve.wait_ge(gathered, 2 * i + 2)
                            onehot_of(i + 1, expert_on(dve, i + 1))
                        elif k == PER_ITEM - 2:
                            hT_of(FB - 1)
                        elif k == PER_ITEM - 1 and not last:
                            xT_dve(i + 1)
                        elif k == PER_ITEM + 1:
                            for g in range(2):
                                dve.wait_ge(y_hi_ready, 2 * i + (g + 1))
                                part = slice(g * HALF, (g + 1) * HALF)
                                nc.vector.tensor_tensor(y_lo[:, part], bank[Y[g]][:, :], y_hi[:, part].bitcast(F32),
                                                        ALU.subtract).then_inc(y_lo_ready, 1)
                            e = expert_on(dve, i)
                            dve.wait_ge(combined, 4 * i + PRIMED)
                            for g in range(2):
                                for t in range(TT):
                                    dve.wait_ge(scattered, 4 * i + (2 * g + t + 1) + PRIMED)
                                    part = h[:, t, g * HALF:(g + 1) * HALF]
                                    nc.vector.scalar_tensor_tensor(
                                        part, bank[X[t]][:, :], gates[:, t, bass.ds(e, 1)], part,
                                        ALU.mult, ALU.add).then_inc(combined, 1)

                with dve.Fori(0, last_item) as i:
                    item_dve(i, False)
                item_dve(last_item, True)
                for t in range(TT):
                    norm_dve(4, t)

            @block.tensor
            def _(pe):
                pe.wait_ge(rt_lo_ready, 1)

                def logits(t, g):
                    transposed(3, t, g)
                    for k in range(4 * g, 4 * g + 4):
                        for j, part in enumerate(tok(hnT, k, t)):
                            last = nc.tensor.matmul(bank[0][:, t * 2 * E:(t + 1) * 2 * E], part,
                                                    rt[:, k, :, :].rearrange("p a e -> p (a e)"),
                                                    start=(k, j) == (0, 0), stop=(k, j) == (KD - 1, 1))
                    return last

                logits(0, 0)
                logits(0, 1)
                transpose_pe(3, 4, 1)
                logits(1, 0)
                logits(1, 1).then_inc(logits_done, 1)
                pe.wait_ge(chosen_ready, 1)
                nc.tensor.matmul(bank[1][:, 0:2 * E], before[:], chosen[:].rearrange("p t e -> p (t e)"),
                                 start=True, stop=True)
                nc.tensor.matmul(bank[1][:, E:2 * E], ones[:], chosen[:, 0, :], start=False, stop=True,
                                 skip_group_check=True).then_inc(places_done, 1)
                for t in range(TT):
                    last = nc.tensor.matmul(bank[2][:, 0:E], ones[:], chosen[:, t, :],
                                            start=t == 0, stop=t == TT - 1)
                last.then_inc(counts_done, 1)

                def gather(item_no):
                    pe.wait_ge(onehot_ready, item_no + 1)
                    for g in range(2):
                        for j in range(4):
                            for t in range(TT):
                                col = (4 * g + j) * P
                                last = nc.tensor.matmul(bank[X[g]][:, j * P:(j + 1) * P], hn[:, t, col:col + P],
                                                        onehot[:, t, :], start=t == 0, stop=t == TT - 1)
                        last.then_inc(gathered, 1)

                for primed in (hT_done, scattered):
                    pe.sem_inc(primed, PRIMED)
                gather(0)

                def project(k, q, b0, first=0, items=0, base=0):
                    c = C_MOE + k + q
                    chunk_here(c, base)
                    if first:
                        pe.wait_ge(xT_lo_ready, items + (q + 1))
                    for j in range(4):
                        kt = 4 * q + j
                        last = mm3(bank[b0][:, :], (xT_hi[:, kt, :], xT_lo[:, kt, :]),
                                   weights(c, j, 0, HALF, HALF), kt == 0, kt == KD - 1)
                    last.then_inc(chunk_used, 1)

                project(0, 0, G[0], first=1)
                last_item = last_item_on(pe)

                def item_pe(i, final):
                    base = PER_ITEM * i

                    def transposes(b):
                        pe.wait_ge(hid2_ready, FB * i + (b + 1) + PRIMED)
                        pe.wait_ge(hT_lo_ready, FB * i + b + PRIMED)
                        if b == 1:
                            pe.wait_ge(onehotT_ready, i + 1)
                        for j in range(4):
                            last = nc.tensor.transpose(bank[T_][:, j * P:(j + 1) * P],
                                                       hid2[:, b % 2, j * P:(j + 1) * P], ident[:])
                        last.then_inc(hT_done, 1)

                    def down(k, b, q):
                        c = C_MOE + k
                        chunk_here(c, base)
                        pe.wait_ge(hT_lo_ready, FB * i + (b + 1) + PRIMED)
                        for g in range(2):
                            for j in range(2):
                                kt = 2 * q + j
                                a = (hT_hi[:, b % 2, kt, :], hT_lo[:, b % 2, kt, :])
                                last = mm3(bank[Y[g]][:, :], a, weights(c, j, g * HALF, (g + 1) * HALF, D),
                                           b == 0 and kt == 0, b == FB - 1 and kt == 3)
                            if (b, q, g) == (FB - 1, 1, 0):
                                last.then_inc(y_done, 1)
                        last.then_inc(chunk_used, 1)

                    for b in range(FB):
                        k0 = 0 if b == 0 else 6 * b - 2
                        if b == 0:
                            project(0, 1, G[0], first=1, items=2 * i, base=base)
                        else:
                            pe.wait_ge(silu2_ready, FB * i + at_least(b - 1) + PRIMED)
                            project(k0, 0, G[b % 2], base=base)
                            project(k0, 1, G[b % 2], base=base)
                        if b:
                            transposes(b - 1)
                        pe.wait_ge(hid2_ready, FB * i + b + PRIMED)
                        project(k0 + 2, 0, U_, base=base)
                        project(k0 + 2, 1, U_, base=base)
                        if b == 1:
                            pe.wait_ge(hT_lo_ready, FB * i + 1 + PRIMED)
                            for t in range(TT):
                                last = nc.tensor.transpose(bank[T_][:, t * P:(t + 1) * P], onehot[:, t, :], ident[:])
                            last.then_inc(onehotT_done, 1)
                            pe.wait_ge(y_lo_ready, 2 * i + PRIMED)
                        if b:
                            down(k0 + 4, b - 1, 0)
                            if b == FB - 1:
                                transposes(b)
                            down(k0 + 5, b - 1, 1)
                    pe.wait_ge(combined, 4 * i + PRIMED)
                    if not final:
                        gather(i + 1)
                    down(PER_ITEM - 2, FB - 1, 0)
                    down(PER_ITEM - 1, FB - 1, 1)
                    if not final:
                        pe.wait_ge(silu2_ready, FB * i + FB + PRIMED)
                        project(PER_ITEM, 0, G[0], first=1, items=2 * i + 2, base=base)
                    for g in range(2):
                        pe.wait_ge(y_lo_ready, 2 * i + (g + 1) + PRIMED)
                        for t in range(TT):
                            if g == 1:
                                pe.wait_ge(combined, 4 * i + (t + 1) + PRIMED)
                            elif not final:
                                pe.wait_ge(xT_lo_ready, 2 * i + 4)
                            part = slice(g * HALF, (g + 1) * HALF)
                            a = onehotT[:, t * P:(t + 1) * P]
                            nc.tensor.matmul(bank[X[t]][:, :], a, y_hi[:, part], start=True, stop=False)
                            nc.tensor.matmul(bank[X[t]][:, :], a, y_lo[:, part], start=False, stop=True
                                             ).then_inc(scattered, 1)

                with pe.Fori(0, last_item) as i:
                    item_pe(i, False)
                item_pe(last_item, True)


_INS = ["x", "positions", "mix_norm", "ffn_norm", "final_norm", "mla_w_in", "mla_q_norm", "mla_w_q_up",
        "mla_kv_norm", "mla_w_kv_up", "mla_w_o", "hgrn_w_in", "hgrn_lower_bounds", "hgrn_out_norm",
        "hgrn_w_o", "ffn_w_gate", "ffn_w_up", "ffn_w_down", "moe_router", "moe_w_gate", "moe_w_up",
        "moe_w_down"]


def kernel(**inputs):
    import concourse.bacc as bacc
    from concourse.bass_utils import run_bass_kernel_spmd

    nc = bacc.Bacc("TRN2", target_bir_lowering=False, num_devices=1)
    arrays, w = {}, {}
    for name in _INS:
        a = np.ascontiguousarray(inputs[name])
        arrays[f"in_{name}"] = a
        w[name] = nc.dram_tensor(f"in_{name}", a.shape, mybir.dt.from_np(a.dtype), kind="ExternalInput").ap()
    out = nc.dram_tensor("out", (1, SEQ, D), F32, kind="ExternalOutput").ap()
    trunk(nc, w, out)
    r = run_bass_kernel_spmd(nc, [arrays], core_ids=[0])
    return r.results[0]["out"]
```
